# Optimizing a Trainium2 kernel written in Bass

```python
import jax, jax.numpy as jnp
from jax import lax
import numpy as np

D_MODEL = 1024
BATCH = 1
SEQ = 512
DEPTH = 1

MIX_WIDTH = D_MODEL
CONV_WIDTH = MIX_WIDTH // 2
CONV_GROUPS = 8
CONV_K = 3
MLSTM_HEADS = 4
MLSTM_V_DIM = (MIX_WIDTH - CONV_WIDTH) // MLSTM_HEADS
MLSTM_QK_DIM = MLSTM_V_DIM // 2
CHUNK = 128
D_FF = 2816
FFN_RESIDUAL_SCALE = 0.5
EPS = 1e-6
NEG_INF = -1e30
IN_SIZES = (CONV_WIDTH, CONV_WIDTH, CONV_WIDTH,
            MLSTM_HEADS * MLSTM_QK_DIM, MLSTM_HEADS * MLSTM_QK_DIM,
            MLSTM_HEADS * MLSTM_V_DIM, MLSTM_HEADS * MLSTM_V_DIM,
            2 * MLSTM_HEADS, 2 * MLSTM_HEADS)
W_IN_COLS = sum(IN_SIZES)


def rmsnorm(x, g):
    x32 = x.astype(jnp.float32)
    y = x32 * lax.rsqrt(jnp.mean(x32 * x32, axis=-1, keepdims=True) + EPS)
    return (y * g.astype(jnp.float32)).astype(x.dtype)

def swiglu(x, w_in, w_out):
    gate, up = jnp.split(x @ w_in, 2, axis=-1)
    return (jax.nn.silu(gate) * up) @ w_out

def mlstm_chunkwise(q, k, v, li, lf):
    B, H, S, DK = q.shape
    DV = v.shape[-1]
    NC = S // CHUNK
    q = q.reshape(B, H, NC, CHUNK, DK)
    k = k.reshape(B, H, NC, CHUNK, DK)
    v = v.reshape(B, H, NC, CHUNK, DV)
    li = li.reshape(B, H, NC, CHUNK)
    lf = lf.reshape(B, H, NC, CHUNK)
    b = jnp.cumsum(lf, axis=-1)
    g = b[..., -1]
    causal = jnp.tril(jnp.ones((CHUNK, CHUNK), dtype=bool))
    D = jnp.where(causal, b[..., :, None] - b[..., None, :] + li[..., None, :], NEG_INF)
    m_intra = jnp.max(D, axis=-1)
    w = g[..., None] - b + li
    m_chunk = jnp.max(w, axis=-1)
    e = jnp.exp(w - m_chunk[..., None])
    C_chunk = jnp.einsum('bhcl,bhclk,bhclv->bhckv', e, k, v)
    n_chunk = jnp.einsum('bhcl,bhclk->bhck', e, k)

    def step(carry, inp):
        C, n, m = carry
        g_c, Cc, nc, mc = inp
        m_new = jnp.maximum(g_c + m, mc)
        a = jnp.exp(g_c + m - m_new)
        s = jnp.exp(mc - m_new)
        C_new = a[..., None, None] * C + s[..., None, None] * Cc
        n_new = a[..., None] * n + s[..., None] * nc
        return (C_new, n_new, m_new), (C, n, m)

    init = (jnp.zeros((B, H, DK, DV), jnp.float32),
            jnp.zeros((B, H, DK), jnp.float32),
            jnp.full((B, H), NEG_INF, jnp.float32))
    xs = (jnp.moveaxis(g, 2, 0), jnp.moveaxis(C_chunk, 2, 0),
          jnp.moveaxis(n_chunk, 2, 0), jnp.moveaxis(m_chunk, 2, 0))
    _, (C_prev, n_prev, m_prev) = lax.scan(step, init, xs)
    C_prev = jnp.moveaxis(C_prev, 0, 2)
    n_prev = jnp.moveaxis(n_prev, 0, 2)
    m_prev = jnp.moveaxis(m_prev, 0, 2)

    m_inter = b + m_prev[..., None]
    m_t = jnp.maximum(m_inter, m_intra)
    P = jnp.exp(D - m_t[..., None]) * jnp.einsum('bhctk,bhcsk->bhcts', q, k)
    inter = jnp.exp(m_inter - m_t)
    numer = inter[..., None] * jnp.einsum('bhctk,bhckv->bhctv', q, C_prev) \
        + jnp.einsum('bhcts,bhcsv->bhctv', P, v)
    denom = inter * jnp.einsum('bhctk,bhck->bhct', q, n_prev) + jnp.sum(P, axis=-1)
    h = numer / jnp.maximum(jnp.abs(denom), jnp.exp(-m_t))[..., None]
    return h.reshape(B, H, S, DV)

def mixer(xn, w_in, conv_w, conv_b, gate_i_bias, gate_f_bias, head_gain, w_out):
    Bsz, S, _ = xn.shape
    H, DK, DV = MLSTM_HEADS, MLSTM_QK_DIM, MLSTM_V_DIM
    split_points = [int(p) for p in np.cumsum(IN_SIZES)[:-1]]
    bg, cg, hc, q, k, v, o, ig, fg = jnp.split(xn @ w_in, split_points, axis=-1)

    u = cg * hc
    u = lax.conv_general_dilated(u, conv_w[:, None, :].astype(u.dtype), window_strides=(1,),
                                 padding=[(1, 1)], dimension_numbers=('NWC', 'WIO', 'NWC'),
                                 feature_group_count=CONV_WIDTH)
    y_conv = bg * (u + conv_b.astype(u.dtype))

    def heads(t, d):
        return t.reshape(Bsz, S, H, d).transpose(0, 2, 1, 3).astype(jnp.float32)
    qh = heads(q, DK) * (DK ** -0.5)
    kh = heads(k, DK)
    vh = heads(v, DV)
    li = (ig.astype(jnp.float32) + gate_i_bias.astype(jnp.float32)).reshape(Bsz, S, 2, H).transpose(2, 0, 3, 1)
    lf = jax.nn.log_sigmoid(fg.astype(jnp.float32) + gate_f_bias.astype(jnp.float32)).reshape(Bsz, S, 2, H).transpose(2, 0, 3, 1)
    h_fwd = mlstm_chunkwise(qh, kh, vh, li[0], lf[0])
    flip = lambda t: jnp.flip(t, axis=2)
    h_bwd = flip(mlstm_chunkwise(flip(qh), flip(kh), flip(vh), flip(li[1]), flip(lf[1])))
    h = h_fwd + h_bwd
    h = h * lax.rsqrt(jnp.mean(h * h, axis=-1, keepdims=True) + EPS) \
        * head_gain.astype(jnp.float32).reshape(H, 1, DV)
    h = h.transpose(0, 2, 1, 3).reshape(Bsz, S, H * DV).astype(xn.dtype)
    y_mlstm = jax.nn.sigmoid(o) * h

    return jnp.concatenate([y_conv, y_mlstm], axis=-1) @ w_out

def first_inputs(seed: int = 0) -> dict:
    key = jax.random.key(seed)
    ks = jax.random.split(key, 20)
    H = MLSTM_HEADS

    def nrm(k, shape, scale):
        return jax.random.normal(k, shape, jnp.float32) * scale

    def gain(k, n):
        return 1.0 + 0.05 * jax.random.normal(k, (DEPTH, n), jnp.float32)

    f_bias = jnp.tile(jnp.linspace(3.0, 6.0, H, dtype=jnp.float32), 2)[None, :] + nrm(ks[12], (DEPTH, 2 * H), 0.1)
    return {
        'x': jax.random.normal(ks[0], (BATCH, SEQ, D_MODEL), jnp.float32),
        'norm_ffn1_pre': gain(ks[1], D_MODEL),
        'norm_ffn1_post': gain(ks[2], D_MODEL),
        'w_ffn1_in': nrm(ks[3], (DEPTH, D_MODEL, 2 * D_FF), D_MODEL ** -0.5),
        'w_ffn1_out': nrm(ks[4], (DEPTH, D_FF, D_MODEL), D_FF ** -0.5),
        'norm_mix_pre': gain(ks[5], D_MODEL),
        'norm_mix_post': gain(ks[6], D_MODEL),
        'w_mix_in': nrm(ks[7], (DEPTH, D_MODEL, W_IN_COLS), D_MODEL ** -0.5),
        'conv_w': nrm(ks[8], (DEPTH, CONV_K, CONV_WIDTH), CONV_K ** -0.5),
        'conv_b': nrm(ks[9], (DEPTH, CONV_WIDTH), 0.02),
        'gate_i_bias': nrm(ks[10], (DEPTH, 2 * H), 0.1),
        'gate_f_bias': f_bias,
        'mlstm_norm': gain(ks[11], H * MLSTM_V_DIM),
        'w_mix_out': nrm(ks[13], (DEPTH, MIX_WIDTH, D_MODEL), MIX_WIDTH ** -0.5),
        'norm_ffn2_pre': gain(ks[14], D_MODEL),
        'norm_ffn2_post': gain(ks[15], D_MODEL),
        'w_ffn2_in': nrm(ks[16], (DEPTH, D_MODEL, 2 * D_FF), D_MODEL ** -0.5),
        'w_ffn2_out': nrm(ks[17], (DEPTH, D_FF, D_MODEL), D_FF ** -0.5),
    }

def first_block(x, norm_ffn1_pre, norm_ffn1_post, w_ffn1_in, w_ffn1_out,
              norm_mix_pre, norm_mix_post, w_mix_in, conv_w, conv_b,
              gate_i_bias, gate_f_bias, mlstm_norm, w_mix_out,
              norm_ffn2_pre, norm_ffn2_post, w_ffn2_in, w_ffn2_out):
    for l in range(DEPTH):
        h = swiglu(rmsnorm(x, norm_ffn1_pre[l]), w_ffn1_in[l], w_ffn1_out[l])
        x = x + FFN_RESIDUAL_SCALE * rmsnorm(h, norm_ffn1_post[l])
        h = mixer(rmsnorm(x, norm_mix_pre[l]), w_mix_in[l], conv_w[l], conv_b[l],
                  gate_i_bias[l], gate_f_bias[l], mlstm_norm[l], w_mix_out[l])
        x = x + rmsnorm(h, norm_mix_post[l])
        h = swiglu(rmsnorm(x, norm_ffn2_pre[l]), w_ffn2_in[l], w_ffn2_out[l])
        x = x + FFN_RESIDUAL_SCALE * rmsnorm(h, norm_ffn2_post[l])
    return x


N_HEADS = 16
HEAD_DIM = D_MODEL // N_HEADS
D_ATTN = N_HEADS * HEAD_DIM
BLOCK_Q = 128
SB_SCALE = HEAD_DIM ** -0.5
POOL_WINDOWS = (2, 4, 8, 16)
N_POOL_GROUPS = len(POOL_WINDOWS)
D_POOL = D_MODEL
POOL_GROUP_DIM = D_POOL // N_POOL_GROUPS
SPLITS = (D_ATTN, D_ATTN, D_ATTN, D_ATTN, D_POOL, D_POOL, D_MODEL, D_MODEL)
IN_COLS = sum(SPLITS)


def rms_norm(x, gain):
    xf = x.astype(jnp.float32)
    y = xf * lax.rsqrt(jnp.mean(xf * xf, axis=-1, keepdims=True) + EPS)
    return (y * gain.astype(jnp.float32)).astype(x.dtype)

def stick_breaking_attention(q, k, v):
    S = q.shape[2]
    outs = []
    for i in range(S // BLOCK_Q):
        q0, q1 = i * BLOCK_Q, (i + 1) * BLOCK_Q
        qb = q[:, :, q0:q1]
        kb = k[:, :, :q1]
        vb = v[:, :, :q1]
        z = jnp.einsum('bhqd,bhkd->bhqk', qb, kb).astype(jnp.float32) * SB_SCALE
        q_pos = jnp.arange(q0, q1)[:, None]
        k_pos = jnp.arange(q1)[None, :]
        mask = k_pos < q_pos
        log_1m_beta = jnp.where(mask, -jax.nn.softplus(z), 0.0)
        suffix = lax.cumsum(log_1m_beta, axis=3, reverse=True) - log_1m_beta
        w = jnp.where(mask, jnp.exp(jax.nn.log_sigmoid(z) + suffix), 0.0)
        outs.append(jnp.einsum('bhqk,bhkd->bhqd', w.astype(vb.dtype), vb))
    return jnp.concatenate(outs, axis=2)

def multiscale_causal_pool(u, pool_w, pool_scale):
    B, S, _ = u.shape
    uf = u.astype(jnp.float32)
    pos_count = jnp.arange(S) + 1
    diffs = []
    for g, win in enumerate(POOL_WINDOWS):
        ug = uf[:, :, g * POOL_GROUP_DIM:(g + 1) * POOL_GROUP_DIM]
        cs = jnp.cumsum(ug, axis=1)
        cs_shift = jnp.pad(cs, ((0, 0), (win, 0), (0, 0)))[:, :S]
        count = jnp.minimum(pos_count, win).astype(jnp.float32)[None, :, None]
        diffs.append((cs - cs_shift) / count - ug)
    d = jnp.stack(diffs, axis=2).astype(u.dtype)
    mixed = jnp.einsum('bsgc,gcd->bsgd', d, pool_w).reshape(B, S, D_POOL)
    return mixed * pool_scale

def hybrid_layer(x, c, norm_gain, w_ada, b_ada, w_in, pool_w, pool_scale,
                 w_branch_a, w_branch_b, w_out):
    B, S, D = x.shape
    mod = jax.nn.silu(c) @ w_ada + b_ada
    shift, scale, gate = jnp.split(mod, 3, axis=-1)
    h = rms_norm(x, norm_gain) * (1.0 + scale[:, None, :]) + shift[:, None, :]

    proj = h @ w_in
    offs = np.cumsum(SPLITS)[:-1].tolist()
    q, k, v, z_a, u, z_b, m_a, m_b = jnp.split(proj, offs, axis=-1)

    to_heads = lambda t: t.reshape(B, S, N_HEADS, HEAD_DIM).transpose(0, 2, 1, 3)
    attn = stick_breaking_attention(to_heads(q), to_heads(k), to_heads(v))
    attn = attn.transpose(0, 2, 1, 3).reshape(B, S, D_ATTN)
    p_a = (attn * jax.nn.silu(z_a)) @ w_branch_a

    pooled = multiscale_causal_pool(u, pool_w, pool_scale)
    p_b = (pooled * jax.nn.silu(z_b)) @ w_branch_b

    merged = jax.nn.sigmoid(m_a) * p_a + jax.nn.sigmoid(m_b) * p_b
    out = merged @ w_out
    return x + gate[:, None, :] * out

def second_inputs(seed: int = 0) -> dict:
    key = jax.random.key(seed)
    ks = jax.random.split(key, 13)
    f32 = jnp.float32
    nrm = lambda k, shape, s: jax.random.normal(k, shape, f32) * s
    return {
        "x": nrm(ks[0], (BATCH, SEQ, D_MODEL), 1.0),
        "c": nrm(ks[1], (BATCH, D_MODEL), 1.0),
        "norm_gain": 1.0 + nrm(ks[2], (DEPTH, D_MODEL), 0.05),
        "w_ada": nrm(ks[3], (DEPTH, D_MODEL, 3 * D_MODEL), 0.5 * D_MODEL ** -0.5),
        "b_ada": nrm(ks[4], (DEPTH, 3 * D_MODEL), 0.01),
        "w_in": nrm(ks[5], (DEPTH, D_MODEL, IN_COLS), D_MODEL ** -0.5),
        "pool_w": nrm(ks[6], (DEPTH, N_POOL_GROUPS, POOL_GROUP_DIM, POOL_GROUP_DIM), POOL_GROUP_DIM ** -0.5),
        "pool_scale": 1.0 + nrm(ks[7], (DEPTH, D_POOL), 0.1),
        "w_branch_a": nrm(ks[8], (DEPTH, D_ATTN, D_MODEL), D_ATTN ** -0.5),
        "w_branch_b": nrm(ks[9], (DEPTH, D_POOL, D_MODEL), D_POOL ** -0.5),
        "w_out": nrm(ks[10], (DEPTH, D_MODEL, D_MODEL), D_MODEL ** -0.5),
        "final_gain": 1.0 + nrm(ks[11], (D_MODEL,), 0.05),
    }

def second_block(x, c, norm_gain, w_ada, b_ada, w_in, pool_w, pool_scale,
              w_branch_a, w_branch_b, w_out, final_gain):
    for l in range(DEPTH):
        x = hybrid_layer(x, c, norm_gain[l], w_ada[l], b_ada[l], w_in[l], pool_w[l],
                         pool_scale[l], w_branch_a[l], w_branch_b[l], w_out[l])
    return rms_norm(x, final_gain)


def setup_inputs(seed=0):
    out = dict(first_inputs(seed))
    for name, value in second_inputs(seed + 1).items():
        if name != "x":
            out[name + "_2"] = value
    return out


def reference(
    x, norm_ffn1_pre, norm_ffn1_post, w_ffn1_in, w_ffn1_out, norm_mix_pre, norm_mix_post,
    w_mix_in, conv_w, conv_b, gate_i_bias, gate_f_bias, mlstm_norm, w_mix_out, norm_ffn2_pre,
    norm_ffn2_post, w_ffn2_in, w_ffn2_out, c_2, norm_gain_2, w_ada_2, b_ada_2, w_in_2, pool_w_2,
    pool_scale_2, w_branch_a_2, w_branch_b_2, w_out_2, final_gain_2,
):
    x = first_block(
        x, norm_ffn1_pre, norm_ffn1_post, w_ffn1_in, w_ffn1_out, norm_mix_pre, norm_mix_post,
        w_mix_in, conv_w, conv_b, gate_i_bias, gate_f_bias, mlstm_norm, w_mix_out,
        norm_ffn2_pre, norm_ffn2_post, w_ffn2_in, w_ffn2_out,
    )
    return second_block(
        x, c_2, norm_gain_2, w_ada_2, b_ada_2, w_in_2, pool_w_2, pool_scale_2, w_branch_a_2,
        w_branch_b_2, w_out_2, final_gain_2,
    )


_drawn_inputs = setup_inputs


def setup_inputs(seed=0):
    import zlib

    import numpy as np

    out = dict(_drawn_inputs(seed))
    spreads = {}
    factors = {'conv_b': 4.475,
     'gate_i_bias': 8.0,
     'mlstm_norm': 3.189,
     'norm_ffn2_post': 3.614,
     'norm_gain_2': 8.0,
     'b_ada_2': 8.0,
     'pool_scale_2': 8.0}
    for name, (base, spread) in spreads.items():
        noise = np.random.default_rng([zlib.crc32(name.encode()), seed]).standard_normal(out[name].shape)
        drawn = base * np.exp(spread * noise) if base else spread * noise
        out[name] = __import__('jax').numpy.asarray(drawn.astype(out[name].dtype))
    for name, factor in factors.items():
        out[name] = (out[name] * factor).astype(out[name].dtype)
    return out
```

```python
import concourse.bass as bass
from concourse import mybir
from contextlib import ExitStack

fp32 = mybir.dt.float32
f32r = mybir.dt.float32r
bf16 = mybir.dt.bfloat16
ALU = mybir.AluOpType
ACT = mybir.ActivationFunctionType

P = 128
T = 512
TB = T // P
D = 1024
KD = D // P
FF = 2816
KF = FF // P
SLOT = 2048
CB = SLOT // KD
EPS = 1e-6
NEG = -1e30

HEADS = 4
DK = 64
DV = 128
CONV = 512
QO, KO, VO, OO, GO = 3 * CONV, 3 * CONV + 256, 3 * CONV + 512, 3 * CONV + 1024, 3 * CONV + 1536
PAIRS = 8
WINDOWS = (2, 4, 8, 16)
ZSCALE = 0.125

NFI = 2 * FF // CB
NFO = KF // 2
S_F1I = 0
S_F1O = S_F1I + NFI
S_MIX = S_F1O + NFO
S_MO = S_MIX + 12
S_F2I = S_MO + 4
S_F2O = S_F2I + NFI
S_ATT = S_F2O + NFO
S_POOL = S_ATT + 2 * PAIRS
S_FIN = S_POOL + 9
S_OUT = S_FIN + 16
S_END = S_OUT + 4
POOL_ORDER = [("u", 0), ("u", 1), ("z", 0), ("u", 2), ("z", 1), ("u", 3), ("z", 2), ("z", 3)]

MIXER = [("gates",), ("slot", 0, "qk"), ("rows",), ("slot", 0, "v"), ("S", 0, 0), ("cols",), ("bc", 0),
         ("slot", 0, "o"), ("vt", 0), ("prep", 0, 0, 0), ("prep", 0, 0, 1), ("slot", 0, "cg"),
         ("mm", 0, 0, 0), ("mm", 0, 0, 1), ("S", 0, 1), ("slot", 0, "hc"), ("prep", 0, 1, 0), ("prep", 0, 1, 1),
         ("slot", 0, "bg"), ("mm", 0, 1, 0), ("mm", 0, 1, 1), ("hn", 0, 0),
         ("slot", 1, "qk"), ("hn", 0, 1), ("bc", 1), ("slot", 1, "v"), ("S", 1, 0),
         ("slot", 1, "o"), ("vt", 1), ("prep", 1, 0, 0), ("prep", 1, 0, 1), ("slot", 1, "cg"),
         ("mm", 1, 0, 0), ("mm", 1, 0, 1), ("S", 1, 1), ("slot", 1, "hc"), ("prep", 1, 1, 0), ("prep", 1, 1, 1),
         ("slot", 1, "bg"), ("mm", 1, 1, 0), ("mm", 1, 1, 1), ("hn", 1, 0), ("hn", 1, 1)]
MSLOTS = [s for s in MIXER if s[0] == "slot"]
DVE_EVAC = ("hc", "bg")

ATT_STEPS = {0: [("Q", 0, 0)], 1: [("Q", 0, 1), ("V",)], 2: [("Q", 0, 2)], 3: [("Q", 0, 3), ("T", 0, 0)],
             4: [("T", 0, 1), ("Q", 1, 0)], 5: [("T", 0, 2), ("Q", 1, 1)], 6: [("T", 0, 3), ("Q", 1, 2)],
             7: [("Q", 1, 3)], 8: [("PV", 0)], 9: [("T", 1, 0)], 10: [("T", 1, 1)], 11: [("T", 1, 2)],
             12: [("T", 1, 3)], 14: [("PV", 1)]}


class Chain:

    def __init__(self, engine, sem):
        self.engine, self.sem, self.base, self.n, self.i, self.per = engine, sem, 0, 0, None, 0

    def enter(self, i, per):
        self.base, self.n, self.i, self.per = self.base + self.n, 0, i, per

    def leave(self, times):
        assert self.n == self.per, self.n
        self.base, self.n, self.i = self.base + times * self.per, 0, None

    def link(self, instruction):
        self.n += 1
        at = self.base + self.n
        if self.i is not None:
            at = self.i * self.per + at
        instruction.then_inc(self.sem, 1)
        self.engine.wait_ge(self.sem, at)


def program(nc, a, out):
    with ExitStack() as ctx:
        keep = ctx

        def sb(name, shape, dt=fp32, where=None):
            return (where or keep).enter_context(nc.sbuf_tensor(name, shape, dt))

        def sem(name):
            return ctx.enter_context(nc.semaphore(name))

        xT = sb("xT", [P, KD, T])
        ah = sb("ah", [P, KD, T], f32r)
        al = sb("al", [P, KD, T], f32r)
        raw = [sb(f"raw{i}", [P, SLOT]) for i in range(2)]
        wh = [sb(f"wh{i}", [P, SLOT], f32r) for i in range(2)]
        wl = [sb(f"wl{i}", [P, SLOT], f32r) for i in range(2)]
        sq = sb("sq", [P, 2, T])
        rstd = sb("rstd", [P, T])
        tt = sb("tt", [P, 2, T])
        ident = sb("ident", [P, P])
        ones = sb("ones", [P, P])
        maskF = sb("maskF", [P, P])
        maskB = sb("maskB", [P, P])
        identb = sb("identb", [P, P], bf16)
        maskS = sb("maskS", [P, P], bf16)
        zero1 = sb("zero1", [P, 1])
        par_rows = sb("par_rows", [P, P])
        par = sb("par", [P, P])
        gbias = sb("gbias", [P, 1])
        gw = sb("gw", [P, KD, 16])
        sc = sb("sc", [P, KD])
        mod = sb("mod", [P, 24])
        gmod = sb("gmod", [P, KD])
        cT = sb("cT", [P, TB, 64])
        invc = sb("invc", [P, 4, 16])
        h7 = sb("h7", [P, T])

        with ExitStack() as phase:
            hid = sb("hid", [P, KF, T], where=phase)
            sg = sb("sg", [P, 2, T], where=phase)
            rh = sb("rh", [P, 2, 2, T], f32r, where=phase)
            rl = sb("rl", [P, 2, 2, T], f32r, where=phase)
            ada_raw = sb("ada_raw", [P, KD, P], where=phase)
            ada = sb("ada", [P, 3 * D], where=phase)
        with ExitStack() as phase:
            xtok = sb("xtok", [P, TB, D], where=phase)
        with ExitStack() as phase:
            outS = sb("outS", [P, TB, D], where=phase)
        with ExitStack() as phase:
            E = sb("E", [P, 2, TB, T], where=phase)
            Sx = sb("Sx", [P, TB, T], where=phase)
            Mb = sb("Mb", [P, 4, T], where=phase)
            Nm = sb("Nm", [P, 4, T], where=phase)
            mrow = sb("mrow", [64, T], where=phase)
            erow = sb("erow", [64, T], where=phase)
            vT = sb("vT", [P, 2, T], where=phase)
            vS = sb("vS", [P, 2, TB, P], where=phase)
            qS = sb("qS", [P, T], where=phase)
            kS = sb("kS", [P, T], where=phase)
            cgS = sb("cgS", [P, 2, T], where=phase)
            ux = sb("ux", [P, 2, T + 2], where=phase)
            ct = sb("ct", [P, 2, T], where=phase)
            sgo = sb("sgo", [P, 2, T], where=phase)
            hs = sb("hs", [P, 2, T], where=phase)
            dg = sb("dg", [P, TB, P], where=phase)
            with ExitStack() as inner:
                gh = sb("gh", [P, KD, P], f32r, where=inner)
                gl = sb("gl", [P, KD, P], f32r, where=inner)
            yT = sb("yT", [P, KD, T], where=phase)
        dt_ = h7
        zrow, lrow = E[:, 0, 0, :], E[:, 0, 1, :]
        frow, brow, crow = E[0:64, 0, 2, :], E[0:64, 0, 3, :], E[0:64, 1, 0, :]
        with ExitStack() as phase:
            gah = sb("gah", [P, KD, T], f32r, where=phase)
            gal = sb("gal", [P, KD, T], f32r, where=phase)
            with ExitStack() as inner:
                wTh = sb("wTh", [P, TB, T], f32r, where=inner)
                wTl = sb("wTl", [P, TB, T], f32r, where=inner)
                Gc = sb("Gc", [P, TB, T + 1], where=inner)
                Wt = sb("Wt", [P, 4, T], where=inner)
                vph = sb("vph", [P, 2, TB, P], f32r, where=inner)
                vpl = sb("vpl", [P, 2, TB, P], f32r, where=inner)
                zs = sb("zs", [P, T], where=inner)
                sz = sb("sz", [P, T], where=inner)
                ga = sb("ga", [P, T], where=inner)
                be = sb("be", [P, 2, T], where=inner)
                g1 = sb("g1", [P, 2, T], where=inner)
                q2 = sb("q2", [P, T], where=inner)
                k2 = sb("k2", [P, T], where=inner)
                v2 = sb("v2", [P, T], where=inner)
            dh = sb("dh", [P, KD, T], f32r, where=phase)
            dl = sb("dl", [P, KD, T], f32r, where=phase)
            with ExitStack() as inner:
                zb = sb("zb", [P, KD, T], where=inner)
                uS = sb("uS", [P, 2, T], where=inner)
                p1 = sb("p1", [P, 2, T], where=inner)
                p2 = sb("p2", [P, 2, T], where=inner)
            mg = sb("mg", [P, KD, T], where=phase)
            sm = sb("sm", [P, 2, T], where=phase)
            sn = sb("sn", [P, 2, T], where=phase)
            m1 = sb("m1", [P, 2, T], where=phase)
        sb2, m2 = tt, sq
        ps = ctx.enter_context(nc.psum_tensor("ps", [P, 8, T], fp32))

        raw_full = [sem(f"raw_full{i}") for i in range(2)]
        hi_done, lo_done = sem("hi_done"), sem("lo_done")
        slot_used = sem("slot_used")
        x_in, par_in = sem("x_in"), sem("par_in")
        const_done, par_cols, par_ready = sem("const_done"), sem("par_cols"), sem("par_ready")
        xt_mm, xt_free = sem("xt_mm"), sem("xt_free")
        x_ready = sem("x_ready")
        sq_done, sum_acc, var_done, rstd_done = sem("sq_done"), sem("sum_acc"), sem("var_done"), sem("rstd_done")
        t_done, ah_done, a_ready = sem("t_done"), sem("ah_done"), sem("a_ready")
        silu_done, hid_ready = sem("silu_done"), sem("hid_ready")
        rhi_done, rlo_done = sem("rhi_done"), sem("rlo_done")
        h7_done = sem("h7_done")
        sc_done, ada_in, ada_step, ada_mm, mod_done = sem("sc_done"), sem("ada_in"), sem("ada_step"), sem("ada_mm"), sem("mod_done")
        act_self, dve_self, pool_self = sem("act_self"), sem("dve_self"), sem("pool_self")
        gpad, gw_hi, gw_lo, gate_mm = sem("gpad"), sem("gw_hi"), sem("gw_lo"), sem("gate_mm")
        z_done, abs_done, ln_done, rows_done, erow_done = sem("z_done"), sem("abs_done"), sem("ln_done"), sem("rows_done"), sem("erow_done")
        wk_mm, wk_free = sem("wk_mm"), sem("wk_free")
        pf_act, pf_dve = sem("pf_act"), sem("pf_dve")
        dg_done, E_done, p_ready = sem("dg_done"), sem("E_done"), sem("p_ready")
        u_mm, h_done, hsq_done, hr_done, hsr_done = sem("u_mm"), sem("h_done"), sem("hsq_done"), sem("hr_done"), sem("hsr_done")
        y_done = sem("y_done")
        att_init = sem("att_init")
        q_mm, sig_done, w_done, t_mm, thi_done, tlo_done = sem("q_mm"), sem("sig_done"), sem("w_done"), sem("t_mm"), sem("thi_done"), sem("tlo_done")
        v_mm, vhi_done, vlo_done, pv_mm, ga_done, gah_done, gal_done = sem("v_mm"), sem("vhi_done"), sem("vlo_done"), sem("pv_mm"), sem("ga_done"), sem("gah_done"), sem("gal_done")
        qe_done, ke_done, ve_done, sz_done, zs_done = sem("qe_done"), sem("ke_done"), sem("ve_done"), sem("sz_done"), sem("zs_done")
        u_in, zsig, zb_done, d_done, dhi_done, dlo_done = sem("u_in"), sem("zsig"), sem("zb_done"), sem("d_done"), sem("dhi_done"), sem("dlo_done")
        pw_mm, yb_t, ybh_done, ybl_done = sem("pw_mm"), sem("yb_t"), sem("ybh_done"), sem("ybl_done")
        sm_done, m_done, mg_done = sem("sm_done"), sem("m_done"), sem("mg_done")
        ot_mm, ot_done, out_done = sem("ot_mm"), sem("ot_done"), sem("out_done")

        vectors = [("norm_ffn1_pre", 8), ("norm_ffn1_post", 8), ("norm_mix_pre", 8), ("norm_mix_post", 8),
                   ("norm_ffn2_pre", 8), ("norm_ffn2_post", 8), ("norm_gain_2", 8), ("final_gain_2", 8),
                   ("c_2", 8), ("b_ada_2", 24), ("pool_scale_2", 8), ("conv_w", 12), ("conv_b", 4), ("mlstm_norm", 4)]
        col, n_par = {}, 0
        for name, rows in vectors:
            col[name] = n_par
            n_par += rows

        def pcol(name, k):
            return par[:, col[name] + k:col[name] + k + 1]

        def flat(ap):
            n = len(ap.shape)
            letters = " ".join("abc"[:n])
            return ap if n == 1 else ap.rearrange(f"{letters} -> ({letters})")

        def wview(name, k0=None):
            w = a[name]
            w = w.rearrange("o r c -> (o r) c") if len(w.shape) == 3 else w
            return w.rearrange("(k p) c -> p k c", p=P)

        W1I, W1O = wview("w_ffn1_in"), wview("w_ffn1_out")
        W2I, W2O = wview("w_ffn2_in"), wview("w_ffn2_out")
        WMI, WMO = wview("w_mix_in"), wview("w_mix_out")
        WHI, WHO = wview("w_in_2"), wview("w_out_2")
        WBA, WBB = wview("w_branch_a_2"), wview("w_branch_b_2")
        WAD = wview("w_ada_2")
        PWV = a["pool_w_2"].rearrange("o g (k p) c -> p (o g k) c", p=P)

        block = ctx.enter_context(nc.Block())

        @block.sync
        def _(sp):
            for b in range(TB):
                sp.dma_start(xtok[:, b, :], a["x"][0, b * P:(b + 1) * P, :]).then_inc(x_in, 16)

            def load(n, source):
                w = raw[n % 2][:, :].rearrange("p (k c) -> p k c", k=source.shape[1])
                sp.dma_start(w, source).then_inc(raw_full[n % 2], 16)

            def load_two(n, left, right):
                w = raw[n % 2][:, :].rearrange("p (k c) -> p k c", k=KD)
                sp.dma_start(w[:, :, 0:P], left).then_inc(raw_full[n % 2], 16)
                sp.dma_start(w[:, :, P:2 * P], right).then_inc(raw_full[n % 2], 16)

            def ffn(base_in, w_in, base_out, w_out):
                with sp.Fori(0, NFI // 2) as i:
                    gate, up = sp.snap(i * CB), sp.snap(i * CB + FF)
                    sp.wait_ge(lo_done, i * 2 + max(base_in - 1, 0))
                    load(base_in, w_in[:, :, bass.ds(gate, CB)])
                    sp.wait_ge(lo_done, i * 2 + base_in)
                    load(base_in + 1, w_in[:, :, bass.ds(up, CB)])
                with sp.Fori(0, NFO // 2) as i:
                    chunk = [sp.snap(i * 4), sp.snap(i * 4 + 2)]
                    for j in range(2):
                        sp.wait_ge(lo_done, i * 2 + (base_out + j - 1))
                        load(base_out + j, w_out[:, bass.ds(chunk[j], 2), :])
                sp.wait_ge(lo_done, base_out + NFO - 2)
                load(base_out + NFO - 1, w_out[:, 2 * (NFO - 1):2 * NFO, :])

            ffn(S_F1I, W1I, S_F1O, W1O)
            for j, (_, p, kind) in enumerate(MSLOTS):
                n = S_MIX + j
                sp.wait_ge(lo_done, n - 1)
                if kind == "qk":
                    load_two(n, WMI[:, :, QO + P * p:QO + P * p + P], WMI[:, :, KO + P * p:KO + P * p + P])
                else:
                    c0 = {"v": VO, "o": OO, "cg": CONV, "hc": 2 * CONV, "bg": 0}[kind] + CB * p
                    load(n, WMI[:, :, c0:c0 + CB])
            for j in range(4):
                sp.wait_ge(lo_done, S_MO + j - 1)
                load(S_MO + j, WMO[:, 2 * j:2 * j + 2, :])
            ffn(S_F2I, W2I, S_F2O, W2O)
            with sp.Fori(0, PAIRS) as p:
                at = [sp.snap(p * P + m * D) for m in range(4)]
                for j in range(2):
                    sp.wait_ge(lo_done, p * 2 + (S_ATT + j - 1))
                    load_two(S_ATT + j, WHI[:, :, bass.ds(at[2 * j], P)], WHI[:, :, bass.ds(at[2 * j + 1], P)])
            for j, (kind, g) in enumerate(POOL_ORDER):
                sp.wait_ge(lo_done, S_POOL + j - 1)
                c0 = (4 if kind == "u" else 5) * D + g * CB
                if j < 2:
                    load_two(S_POOL + j, WHI[:, :, c0:c0 + P], WHI[:, :, c0 + P:c0 + CB])
                else:
                    load(S_POOL + j, WHI[:, :, c0:c0 + CB])
            sp.wait_ge(lo_done, S_POOL + 7)
            load(S_POOL + 8, PWV)
            with sp.Fori(1, 5) as c:
                at = [sp.snap(c * CB + (c0 - CB)) for c0 in (6 * D, 0, 7 * D, 0)]
                for j, w in enumerate((WHI, WBA, WHI, WBB)):
                    sp.wait_ge(lo_done, c * 4 + (S_FIN + j - 5))
                    load(S_FIN + j, w[:, :, bass.ds(at[j], CB)])
            for j in range(4):
                sp.wait_ge(lo_done, S_OUT + j - 1)
                load(S_OUT + j, WHO[:, 2 * j:2 * j + 2, :])
            sp.wait_ge(ot_done, KD)
            for b in range(TB):
                sp.dma_start(out[0, b * P:(b + 1) * P, :], outS[:, b, :]).then_inc(out_done, 16)
            sp.wait_ge(out_done, 16 * TB)

        double = {S_MIX + j for j, s in enumerate(MSLOTS) if s[2] == "qk"} | set(range(S_ATT, S_POOL + 2))
        landed = {}
        for n in range(S_END):
            landed[n] = landed.get(n - 2, 0) + 16 * (2 if n in double else 1)

        @block.gpsimd
        def _(pool):
            chain = Chain(pool, pool_self)
            nc.gpsimd.memset(zero1[:], 0.0)
            nc.gpsimd.memset(ones[:], 1.0)
            nc.gpsimd.memset(ident[:], 0.0)
            nc.gpsimd.memset(identb[:], 0.0)
            nc.gpsimd.memset(maskF[:], 0.0)
            nc.gpsimd.memset(maskB[:], 0.0)
            for w in range(4):
                for t in range(WINDOWS[w]):
                    nc.gpsimd.memset(invc[:, w, t:t + 1], 1.0 / (t + 1))
            chain.link(nc.gpsimd.memset(maskS[:], 0.0))
            for m in (ident, identb):
                nc.gpsimd.affine_select(out=m[:], in_=m[:], compare_op=ALU.not_equal, fill=1.0, base=0,
                                        pattern=[[-1, P]], channel_multiplier=1)
            nc.gpsimd.affine_select(out=maskF[:], in_=maskF[:], compare_op=ALU.is_ge, fill=NEG, base=0,
                                    pattern=[[1, P]], channel_multiplier=-1)
            nc.gpsimd.affine_select(out=maskB[:], in_=maskB[:], compare_op=ALU.is_ge, fill=NEG, base=0,
                                    pattern=[[-1, P]], channel_multiplier=1)
            nc.gpsimd.affine_select(out=maskS[:], in_=maskS[:], compare_op=ALU.is_ge, fill=NEG, base=-1,
                                    pattern=[[-1, P]], channel_multiplier=1).then_inc(const_done, 1)

            pool.wait_ge(sc_done, 1)
            with pool.Fori(0, 3 * KD) as j:
                chain.enter(j, 3)
                pool.dma_start(ada_raw[:, :, :], WAD[:, :, bass.ds(j * P, P)]).then_inc(ada_in, 16)
                pool.wait_ge(ada_in, j * 16 + 16)
                chain.link(nc.gpsimd.tensor_tensor(ada_raw[:, :, :], ada_raw[:, :, :],
                                                   sc[:, :].unsqueeze(2).to_broadcast([P, KD, P]), ALU.mult))
                chain.link(nc.gpsimd.tensor_tensor(ada_raw[:, 0:4, :], ada_raw[:, 0:4, :], ada_raw[:, 4:8, :], ALU.add))
                chain.link(nc.gpsimd.tensor_tensor(ada_raw[:, 0:2, :], ada_raw[:, 0:2, :], ada_raw[:, 2:4, :], ALU.add))
                nc.gpsimd.tensor_tensor(ada[:, bass.ds(j * P, P)], ada_raw[:, 0, :], ada_raw[:, 1, :],
                                        ALU.add).then_inc(ada_step, 1)
                pool.wait_ge(ada_step, j + 1)
            chain.leave(3 * KD)

            pool.wait_ge(slot_used, S_MIX)
            pool.wait_ge(ada_mm, 1)
            nc.gpsimd.memset(gh[:].bitcast(fp32), 0.0)
            nc.gpsimd.memset(ux[:, :, 0:1], 0.0)
            nc.gpsimd.memset(ux[:, :, T + 1:T + 2], 0.0)
            nc.gpsimd.memset(gl[:].bitcast(fp32), 0.0).then_inc(gpad, 1)

            pool.wait_ge(slot_used, S_ATT)
            nc.gpsimd.memset(vph[:].bitcast(fp32), 0.0)
            for i in range(TB):
                nc.gpsimd.memset(Gc[:, i, (i + 1) * P:(i + 1) * P + 1], 1.0)
            nc.gpsimd.memset(vpl[:].bitcast(fp32), 0.0).then_inc(att_init, 1)

        work_uses = {"S": TB, "cols": 1, "bc": 8, "vt": 2, "hn": 1}
        work_first, work_n = {}, 0
        for step in MIXER:
            work_first[step] = work_n
            work_n += work_uses.get(step[0], 0)

        def work_end(*step):
            return work_first[step] + work_uses[step[0]]

        evacuated, tally = [], {True: 0, False: 0}
        for s in MSLOTS:
            tally[s[2] in DVE_EVAC] += 1
            evacuated.append((pf_dve if s[2] in DVE_EVAC else pf_act, tally[s[2] in DVE_EVAC]))

        R_F1, R_MO, R_F2, R_OUT = 0, NFO, NFO + 4, 2 * NFO + 4
        LAST = [7, 0, 1, 2, 3, 4, 5, 6]

        def span(direction, b):
            return (b * P, T) if direction == 0 else (0, (b + 1) * P)

        @block.scalar
        def _(act):
            chain = Chain(act, act_self)

            at = 0
            for name, rows in vectors:
                act.dma_start(par_rows[at:at + rows, :], flat(a[name]).rearrange("(r p) -> r p", p=P)).then_inc(par_in, 16)
                at += rows
            act.dma_start(gw[:, :, :], WMI[:, :, GO:GO + 16]).then_inc(par_in, 16)
            act.wait_ge(par_cols, 1)
            for d in range(2):
                act.dma_start(gbias[32 * d:32 * d + HEADS, :],
                              a["gate_i_bias"][0:1, HEADS * d:HEADS * d + HEADS].rearrange("o h -> h o")).then_inc(par_in, 16)
                act.dma_start(gbias[64 + 32 * d:64 + 32 * d + HEADS, :],
                              a["gate_f_bias"][0:1, HEADS * d:HEADS * d + HEADS].rearrange("o h -> h o")).then_inc(par_in, 16)

            def hi(n, i=0):
                step = landed[n] - landed[n - 2] if n >= 2 else 16
                act.wait_ge(raw_full[n % 2], i * step + landed[n])
                if n >= 2:
                    act.wait_ge(slot_used, i * 2 + (n - 1))
                nc.scalar.activation(wh[n % 2][:], raw[n % 2][:], ACT.Copy).then_inc(hi_done, 1)

            def squares(stage, ready, order=range(KD), banks=False):
                for j, k in enumerate(order):
                    ready(j, k)
                    if 8 * stage + j >= 2:
                        act.wait_ge(sum_acc, 8 * stage + j - 1)
                    source = xT[:, k, :] if not banks else ps[:, k, :] if k < 7 else h7[:]
                    nc.scalar.activation(sq[:, j % 2, :], source, ACT.Square).then_inc(sq_done, 1)
                act.wait_ge(var_done, stage + 1)
                nc.scalar.activation(rstd[:], rstd[:], ACT.Sqrt).then_inc(rstd_done, 1)

            def pre_norm(stage, pre, x_stage, shift=False):
                squares(stage, lambda j, k: act.wait_ge(x_ready, 8 * x_stage + j + 1))
                for k in range(KD):
                    act.wait_ge(t_done, 8 * stage + k + 1)
                    if shift:
                        nc.scalar.activation(ah[:, k, :], tt[:, k % 2, :], ACT.Identity, bias=mod[:, k:k + 1]).then_inc(ah_done, 1)
                    else:
                        nc.scalar.activation(ah[:, k, :], tt[:, k % 2, :], ACT.Copy).then_inc(ah_done, 1)

            def post_norm(stage, last):
                def ready(j, k):
                    if j == 0:
                        act.wait_ge(slot_used, last + 1)
                    if k == 7:
                        act.wait_ge(h7_done, (stage + 1) // 2)
                squares(stage, ready, banks=True)

            def out_hi(first, j, source, target, ready):
                ready()
                nc.scalar.activation(target, source, ACT.Copy).then_inc(rhi_done, 1)

            def ffn(f, base_in, base_out):
                with act.Fori(0, NFI // 2) as i:
                    hi(base_in + 2, i)
                    act.wait_ge(hid_ready, i + f * NFO)
                    nc.scalar.activation(sg[:], ps[:, 0:2, :], ACT.Silu).then_inc(silu_done, 1)
                    hi(base_in + 3, i)

                def unit(j, i=0):
                    act.wait_ge(hid_ready, i * 2 + (f * NFO + j + 1))
                    act.wait_ge(slot_used, i * 2 + (base_out + j - 1))
                    nc.scalar.activation(rh[:, j % 2, :, :], hid[:, bass.ds(i * 4 + 2 * j, 2), :], ACT.Copy).then_inc(rhi_done, 1)

                unit(0)
                unit(1)
                with act.Fori(0, 4) as i:
                    for j in range(2):
                        hi(base_out + j + 2, i)
                        unit(j + 2, i)
                hi(base_out + 10)
                unit(10)
                hi(base_out + 11)
                hi(base_out + 12)

            hi(0)
            hi(1)
            act.wait_ge(par_ready, 1)
            nc.scalar.activation(sc[:], par[:, col["c_2"]:col["c_2"] + KD], ACT.Silu).then_inc(sc_done, 1)
            pre_norm(0, 0, 0)
            ffn(0, S_F1I, S_F1O)
            post_norm(1, S_MIX - 1)

            act.wait_ge(gpad, 1)
            for q in range(4):
                instruction = nc.scalar.activation(gh[:, :, 32 * q:32 * q + HEADS], gw[:, :, HEADS * q:HEADS * q + HEADS], ACT.Copy)
            instruction.then_inc(gw_hi, 1)
            pre_norm(2, 1, 1)
            work = [0]

            def from_work(target, view=None, scale=1.0):
                work[0] += 1
                act.wait_ge(wk_mm, work[0])
                source = ps[:, 4 + (work[0] - 1) % 2, :]
                nc.scalar.activation(target, source if view is None else view(source), ACT.Copy, scale=scale).then_inc(wk_free, 1)

            n_slot = 0
            for step in MIXER:
                kind = step[0]
                if kind == "slot":
                    p, what = step[1:]
                    b = 2 * (n_slot % 2)
                    hi(S_MIX + n_slot + 2)
                    act.wait_ge(slot_used, S_MIX + n_slot + 1)
                    n_slot += 1
                    if what == "qk":
                        nc.scalar.activation(kS[:], ps[:, b + 1, :], ACT.Copy)
                        nc.scalar.activation(qS[:], ps[:, b, :], ACT.Copy, scale=ZSCALE).then_inc(pf_act, 1)
                    elif what == "v":
                        nc.scalar.activation(vT[:], ps[:, b:b + 2, :], ACT.Copy).then_inc(pf_act, 1)
                    elif what == "o":
                        act.wait_ge(y_done, 2 * p)
                        nc.scalar.activation(sgo[:], ps[:, b:b + 2, :], ACT.Sigmoid).then_inc(pf_act, 1)
                    elif what == "cg":
                        act.wait_ge(pf_dve, 2 * p)
                        nc.scalar.activation(cgS[:], ps[:, b:b + 2, :], ACT.Copy).then_inc(pf_act, 1)
                elif kind == "rows":
                    act.wait_ge(gate_mm, 1)
                    nc.scalar.activation(zrow, ps[:, 6, :], ACT.Identity, bias=gbias[:]).then_inc(z_done, 1)
                    act.wait_ge(abs_done, 1)
                    chain.link(nc.scalar.activation(lrow, lrow, ACT.Exp))
                    nc.scalar.activation(lrow, lrow, ACT.Ln, bias=1.0).then_inc(ln_done, 1)
                    act.wait_ge(rows_done, 1)
                    nc.scalar.activation(erow[:], erow[:], ACT.Exp).then_inc(erow_done, 1)
                elif kind == "cols":
                    from_work(cT[:], lambda s: s[:, 0:4 * 64].rearrange("p (b r) -> p b r", r=64))
                elif kind == "bc":
                    act.wait_ge(h_done, 4 * step[1])
                    for u in range(4):
                        from_work(Mb[:, u, :])
                        from_work(Nm[:, u, :])
                elif kind == "S":
                    act.wait_ge(p_ready, 4 * step[1] + 2 * step[2])
                    for b in range(TB):
                        from_work(Sx[:, b, :])
                elif kind == "vt":
                    act.wait_ge(u_mm, 4 * step[1])
                    for h in range(2):
                        from_work(vS[:, h, :, :], lambda s: s.rearrange("p (b d) -> p b d", d=P))
                elif kind == "prep":
                    p, h, d = step[1:]
                    u, row = 4 * p + 2 * h + d, 32 * d + 2 * p + h
                    if u >= 2:
                        act.wait_ge(u_mm, u - 1)
                    act.wait_ge(dg_done, u + 1)
                    for b in range(TB):
                        bias = cT[:, b, row:row + 1]
                        t0, t1 = ((b + 1) * P, T) if d == 0 else (0, b * P)
                        if t1 > t0:
                            nc.scalar.activation(E[:, u % 2, b, t0:t1], Mb[:, 2 * h + d, t0:t1], ACT.Exp, bias=bias, scale=-1.0)
                        last = nc.scalar.activation(E[:, u % 2, b, b * P:(b + 1) * P], dg[:, b, :], ACT.Exp, bias=bias)
                    last.then_inc(E_done, 1)
                elif kind == "hn":
                    p, h = step[1:]
                    act.wait_ge(h_done, 4 * p + 2 * h + 2)
                    nc.scalar.activation(sq[:, h, :], hs[:, h, :], ACT.Square).then_inc(hsq_done, 1)
                    from_work(tt[:, h, :], scale=1.0 / DV)
                    act.wait_ge(hr_done, 2 * p + h + 1)
                    nc.scalar.activation(tt[:, h, :], tt[:, h, :], ACT.Sqrt).then_inc(hsr_done, 1)
            act.wait_ge(slot_used, S_MO)
            for j in range(4):
                act.wait_ge(pf_dve if j < 2 else y_done, 2 * (j + 1) if j < 2 else 2 * (j - 1))
                nc.scalar.activation(ah[:, 2 * j:2 * j + 2, :], yT[:, 2 * j:2 * j + 2, :], ACT.Copy).then_inc(rhi_done, 1)
            for j in range(4):
                hi(S_MO + j + 2)
            post_norm(3, S_F2I - 1)

            pre_norm(4, 2, 2)
            ffn(1, S_F2I, S_F2O)
            post_norm(5, S_ATT - 1)

            pre_norm(6, 3, 3, shift=True)
            act.wait_ge(att_init, 1)

            def att_step(step, r):
                kind, h = step[0], step[1] if len(step) > 1 else 0
                if kind == "Q":
                    i = step[2]
                    idx, n = 4 * h + i, (i + 1) * P
                    act.wait_ge(q_mm, r * 8 + (idx + 1))
                    act.wait_ge(w_done, r * 8 + max(idx - 1, 0))
                    nc.scalar.activation(g1[:, idx % 2, 0:n], ps[:, 4 + idx % 2, 0:n], ACT.Sigmoid, scale=-1.0)
                    nc.scalar.activation(be[:, idx % 2, 0:n], ps[:, 4 + idx % 2, 0:n], ACT.Sigmoid).then_inc(sig_done, 1)
                elif kind == "V":
                    act.wait_ge(v_mm, r + 1)
                    act.wait_ge(pv_mm, r * 2)
                    bank = ps[:, 6, :].rearrange("p (b d) -> p b d", d=P)
                    for e in range(2):
                        last = nc.scalar.activation(vph[:, e, :, DK * e:DK * e + DK], bank[:, :, DK * e:DK * e + DK], ACT.Copy)
                    last.then_inc(vhi_done, 1)
                elif kind == "T":
                    i = step[2]
                    idx = 4 * h + i
                    act.wait_ge(t_mm, r * 8 + (idx + 1))
                    act.wait_ge(pv_mm, r * 2 + h)
                    nc.scalar.activation(wTh[:, 0:i + 1, i * P:(i + 1) * P],
                                         ps[:, 6, 0:(i + 1) * P].rearrange("p (b t) -> p b t", t=P), ACT.Copy).then_inc(thi_done, 1)

            def att_out(r):
                act.wait_ge(ga_done, r + 1)
                nc.scalar.activation(gah[:, bass.ds(r, 1), :] if not isinstance(r, int) else gah[:, r:r + 1, :],
                                     ga[:].unsqueeze(1), ACT.Copy).then_inc(gah_done, 1)

            def att_slot(i, j):
                hi(S_ATT + j + 2, i)
                act.wait_ge(slot_used, i * 2 + (S_ATT + j + 1))
                if j == 0:
                    nc.scalar.activation(q2[:], ps[:, 0, :], ACT.Copy, scale=ZSCALE).then_inc(qe_done, 1)
                else:
                    nc.scalar.activation(v2[:], ps[:, 2, :], ACT.Copy).then_inc(ve_done, 1)
                    act.wait_ge(zs_done, i)
                    nc.scalar.activation(sz[:], ps[:, 3, :], ACT.Sigmoid).then_inc(sz_done, 1)

            att_slot(0, 0)
            att_slot(0, 1)
            with act.Fori(0, PAIRS - 1) as r:
                for j in range(2):
                    for s in range(8):
                        for step in ATT_STEPS.get(8 * j + s, []):
                            att_step(step, r)
                    if j == 1:
                        att_out(r)
                    att_slot(r + 1, j)

            def pool_slot(j):
                kind, g = POOL_ORDER[j]
                b = 2 * (j % 2)
                hi(S_POOL + j + 2)
                act.wait_ge(slot_used, S_POOL + j + 1)
                if kind == "u":
                    if g == 0:
                        act.wait_ge(w_done, 8 * PAIRS)
                    else:
                        act.wait_ge(d_done, g)
                    nc.scalar.activation(uS[:], ps[:, b:b + 2, :], ACT.Copy).then_inc(u_in, 1)
                else:
                    act.wait_ge(zb_done, g)
                    nc.scalar.activation(sb2[:], ps[:, b:b + 2, :], ACT.Sigmoid).then_inc(zsig, 1)

            def pool_hi(g):
                act.wait_ge(d_done, g + 1)
                source = p1 if g in (1, 3) else p2
                nc.scalar.activation(dh[:, 2 * g:2 * g + 2, :], source[:], ACT.Copy).then_inc(dhi_done, 1)

            for j in range(2):
                for s in range(8):
                    for step in ATT_STEPS.get(8 * j + s, []):
                        att_step(step, PAIRS - 1)
                if j == 1:
                    att_out(PAIRS - 1)
                    pool_hi(0)
                pool_slot(j)
            for j in range(2, 8):
                kind, g = POOL_ORDER[j - 1]
                if kind == "u":
                    pool_hi(g)
                pool_slot(j)
            for g in range(4):
                act.wait_ge(yb_t, g + 1)
                nc.scalar.activation(dh[:, 2 * g:2 * g + 2, :], (p1 if g % 2 == 0 else p2)[:], ACT.Copy).then_inc(ybh_done, 1)
            hi(S_FIN + 1)
            with act.Fori(0, 4) as c:
                for j in range(4):
                    n = S_FIN + j
                    act.wait_ge(raw_full[n % 2], c * 32 + landed[n + 2])
                    act.wait_ge(slot_used, c * 4 + (n + 1))
                    nc.scalar.activation(wh[n % 2][:], raw[n % 2][:], ACT.Copy).then_inc(hi_done, 1)
                    if j == 0:
                        act.wait_ge(m_done, c * 2)
                        nc.scalar.activation(sm[:], ps[:, 0:2, :], ACT.Sigmoid).then_inc(sm_done, 1)
                    elif j == 2:
                        act.wait_ge(ybl_done, 4)
                        act.wait_ge(m_done, c * 2)
                        nc.scalar.activation(sn[:], ps[:, 0:2, :], ACT.Sigmoid).then_inc(sm_done, 1)
            for j in range(4):
                act.wait_ge(mg_done, j + 1)
                nc.scalar.activation(ah[:, 2 * j:2 * j + 2, :], mg[:, 2 * j:2 * j + 2, :], ACT.Copy).then_inc(rhi_done, 1)
            for j in range(2):
                hi(S_OUT + j + 2)
            squares(7, lambda j, k: act.wait_ge(x_ready, 8 * 4 + j + 1), order=LAST)
            for k in range(KD):
                act.wait_ge(ot_mm, k + 1)
                nc.scalar.activation(outS[:, :, k * P:(k + 1) * P], ps[:, 4 + k % 2, :].rearrange("p (b d) -> p b d", d=P),
                                     ACT.Copy).then_inc(ot_done, 1)

        @block.vector
        def _(dve):
            chain = Chain(dve, dve_self)

            def lo(n, i=0):
                dve.wait_ge(hi_done, i * 2 + (n + 1))
                nc.vector.tensor_tensor(wl[n % 2][:], raw[n % 2][:], wh[n % 2][:].bitcast(fp32), ALU.subtract).then_inc(lo_done, 1)

            def variance(stage):
                dve.wait_ge(sum_acc, 8 * stage + 8)
                chain.link(nc.vector.tensor_scalar(rstd[:], ps[:, 7, :], 1.0 / D, EPS, ALU.mult, ALU.add))
                nc.vector.reciprocal(rstd[:], rstd[:]).then_inc(var_done, 1)
                dve.wait_ge(rstd_done, stage + 1)

            def pre_norm(stage, pre, gain, shift=False):
                variance(stage)

                def scaled(k):
                    if k >= 2:
                        dve.wait_ge(a_ready, 8 * pre + k - 1)
                    nc.vector.scalar_tensor_tensor(tt[:, k % 2, :], xT[:, k, :], gain(k), rstd[:], ALU.mult, ALU.mult).then_inc(t_done, 1)

                scaled(0)
                for k in range(KD):
                    if k + 1 < KD:
                        scaled(k + 1)
                    dve.wait_ge(ah_done, 8 * pre + k + 1)
                    if shift:
                        nc.vector.scalar_tensor_tensor(al[:, k, :], tt[:, k % 2, :], mod[:, k:k + 1], ah[:, k, :].bitcast(fp32),
                                                       ALU.add, ALU.subtract).then_inc(a_ready, 1)
                    else:
                        nc.vector.tensor_tensor(al[:, k, :], tt[:, k % 2, :], ah[:, k, :].bitcast(fp32), ALU.subtract).then_inc(a_ready, 1)

            def post_norm(stage, last, gain, factor, x_stage):
                dve.wait_ge(slot_used, last + 1)
                nc.vector.tensor_copy(h7[:], ps[:, 7, :]).then_inc(h7_done, 1)
                variance(stage)

                def scaled(k):
                    if k >= 2:
                        dve.wait_ge(x_ready, 8 * x_stage + k - 1)
                    nc.vector.scalar_tensor_tensor(tt[:, k % 2, :], ps[:, k, :] if k < 7 else h7[:], pcol(gain, k), rstd[:],
                                                   ALU.mult, ALU.mult).then_inc(t_done, 1)

                scaled(0)
                for k in range(KD):
                    if k + 1 < KD:
                        scaled(k + 1)
                    dve.wait_ge(t_done, 8 * stage + k + 1)
                    nc.vector.scalar_tensor_tensor(xT[:, k, :], tt[:, k % 2, :], factor, xT[:, k, :], ALU.mult, ALU.add).then_inc(x_ready, 1)

            def ffn(f, base_in, base_out):
                with dve.Fori(0, NFI // 2) as i:
                    lo(base_in + 2, i)
                    lo(base_in + 3, i)
                    dve.wait_ge(silu_done, i + (f * NFO + 1))
                    dve.wait_ge(slot_used, i * 2 + (base_in + 2))
                    nc.vector.tensor_tensor(hid[:, bass.ds(i * 2, 2), :], sg[:], ps[:, 2:4, :], ALU.mult).then_inc(hid_ready, 1)

                def unit(j, i=0):
                    dve.wait_ge(rhi_done, i * 2 + ((R_F1, R_F2)[f] + j + 1))
                    nc.vector.tensor_tensor(rl[:, j % 2, :, :], hid[:, bass.ds(i * 4 + 2 * j, 2), :],
                                            rh[:, j % 2, :, :].bitcast(fp32), ALU.subtract).then_inc(rlo_done, 1)

                unit(0)
                unit(1)
                with dve.Fori(0, 4) as i:
                    for j in range(2):
                        lo(base_out + j + 2, i)
                        unit(j + 2, i)
                lo(base_out + 10)
                unit(10)
                lo(base_out + 11)
                lo(base_out + 12)

            nc.vector.memset(gbias[:], 0.0).then_inc(par_cols, 1)
            dve.wait_ge(xt_mm, 1)
            nc.vector.tensor_copy(par[:, 0:n_par], ps[:, 7, 0:n_par]).then_inc(par_ready, 1)
            for k in range(KD):
                dve.wait_ge(xt_mm, k + 2)
                nc.vector.tensor_copy(xT[:, k, :], ps[:, k % 4, :]).then_inc(x_ready, 1)
            lo(0)
            lo(1)
            dve.wait_ge(par_ready, 1)
            pre_norm(0, 0, lambda k: pcol("norm_ffn1_pre", k))
            ffn(0, S_F1I, S_F1O)
            post_norm(1, S_MIX - 1, "norm_ffn1_post", 0.5, 1)

            dve.wait_ge(gw_hi, 1)
            for q in range(4):
                cols = slice(32 * q, 32 * q + HEADS)
                last = nc.vector.tensor_tensor(gl[:, :, cols], gw[:, :, HEADS * q:HEADS * q + HEADS],
                                               gh[:, :, cols].bitcast(fp32), ALU.subtract)
            last.then_inc(gw_lo, 1)
            pre_norm(2, 1, lambda k: pcol("norm_mix_pre", k))
            n_slot = 0
            for step in MIXER:
                kind = step[0]
                if kind == "slot":
                    p, what = step[1:]
                    b = 2 * (n_slot % 2)
                    lo(S_MIX + n_slot + 2)
                    n_slot += 1
                    if what == "hc":
                        dve.wait_ge(slot_used, S_MIX + n_slot)
                        dve.wait_ge(pf_act, 4 * p + 4)
                        nc.vector.tensor_tensor(ux[:, :, 1:T + 1], cgS[:], ps[:, b:b + 2, :], ALU.mult).then_inc(pf_dve, 1)
                        dve.wait_ge(pf_dve, 2 * p + 1)
                        for tap in (1, 0, 2):
                            for c in range(2):
                                w = pcol("conv_w", 4 * tap + 2 * p + c)
                                if tap == 1:
                                    last = nc.vector.tensor_scalar(ct[:, c, :], ux[:, c, 1:T + 1], w, pcol("conv_b", 2 * p + c), ALU.mult, ALU.add)
                                else:
                                    last = nc.vector.scalar_tensor_tensor(ct[:, c, :], ux[:, c, tap:tap + T], w, ct[:, c, :], ALU.mult, ALU.add)
                            chain.link(last)
                    elif what == "bg":
                        dve.wait_ge(slot_used, S_MIX + n_slot)
                        nc.vector.tensor_tensor(yT[:, 2 * p:2 * p + 2, :], ct[:], ps[:, b:b + 2, :], ALU.mult).then_inc(pf_dve, 1)
                elif kind == "gates":
                    dve.wait_ge(ada_mm, 1)
                    nc.vector.tensor_tensor(mod[:], ps[:, 0, 0:24], par[:, col["b_ada_2"]:col["b_ada_2"] + 24], ALU.add).then_inc(mod_done, 1)
                    dve.wait_ge(mod_done, 1)
                    chain.link(nc.vector.tensor_scalar(gmod[:], mod[:, 8:16], 1.0, None, ALU.add))
                    chain.link(nc.vector.tensor_tensor(gmod[:], gmod[:], par[:, col["norm_gain_2"]:col["norm_gain_2"] + 8], ALU.mult))
                elif kind == "rows":
                    dve.wait_ge(z_done, 1)
                    nc.vector.scalar_tensor_tensor(lrow, zrow, -1.0, zrow, ALU.mult, ALU.min).then_inc(abs_done, 1)
                    dve.wait_ge(ln_done, 1)
                    chain.link(nc.vector.scalar_tensor_tensor(frow, zrow[64:128, :], 0.0, lrow[64:128, :], ALU.min, ALU.subtract))
                    f, r = slice(0, 32), slice(32, 64)
                    zeros = zero1[0:32, :].to_broadcast([32, T])
                    zeros_r = zero1[32:64, :].to_broadcast([32, T])
                    nc.vector.tensor_tensor_scan(brow[f, :], frow[f, :], zeros, 0.0, ALU.add, ALU.add)
                    chain.link(nc.vector.tensor_tensor_scan(brow[r, ::-1], frow[r, ::-1], zeros_r, 0.0, ALU.add, ALU.add))
                    chain.link(nc.vector.tensor_tensor(crow, zrow[0:64, :], brow, ALU.subtract))
                    nc.vector.tensor_tensor_scan(mrow[f, :], crow[f, :], crow[f, :], NEG, ALU.max, ALU.max)
                    chain.link(nc.vector.tensor_tensor_scan(mrow[r, ::-1], crow[r, ::-1], crow[r, ::-1], NEG, ALU.max, ALU.max))
                    chain.link(nc.vector.scalar_tensor_tensor(erow[:], brow, -1.0, mrow[:], ALU.mult, ALU.subtract))
                    nc.vector.tensor_scalar(erow[:], erow[:], 88.0, None, ALU.min).then_inc(rows_done, 1)
                elif kind == "prep":
                    p, h, d = step[1:]
                    u = 4 * p + 2 * h + d
                    dve.wait_ge(wk_free, work_end("bc", p))
                    dve.wait_ge(E_done, u)
                    mask = (maskF, maskB)[d]
                    nc.vector.scalar_tensor_tensor(dg[:], Mb[:, 2 * h + d, :].rearrange("p (b t) -> p b t", t=P), -1.0,
                                                   mask[:].unsqueeze(1).to_broadcast([P, TB, P]), ALU.mult, ALU.add).then_inc(dg_done, 1)
                    dve.wait_ge(E_done, u + 1)
                    dve.wait_ge(wk_free, work_end("S", p, h))
                    for b in range(TB):
                        t0, t1 = span(d, b)
                        last = nc.vector.tensor_tensor(E[:, u % 2, b, t0:t1], E[:, u % 2, b, t0:t1], Sx[:, b, t0:t1], ALU.mult)
                    last.then_inc(p_ready, 1)
                elif kind == "mm":
                    p, h, d = step[1:]
                    u = 4 * p + 2 * h + d
                    dve.wait_ge(u_mm, u + 1)
                    chain.link(nc.vector.tensor_tensor(dt_[:], ps[:, 7, :], Nm[:, 2 * h + d, :], ALU.max))
                    chain.link(nc.vector.scalar_tensor_tensor(dt_[:], ps[:, 7, :], -1.0, dt_[:], ALU.mult, ALU.max))
                    chain.link(nc.vector.reciprocal(dt_[:], dt_[:]))
                    if d == 0:
                        nc.vector.tensor_tensor(hs[:, h, :], ps[:, 6, :], dt_[:], ALU.mult).then_inc(h_done, 1)
                    else:
                        chain.link(nc.vector.tensor_tensor(dt_[:], ps[:, 6, :], dt_[:], ALU.mult))
                        nc.vector.tensor_tensor(hs[:, h, :], hs[:, h, :], dt_[:], ALU.add).then_inc(h_done, 1)
                elif kind == "hn":
                    p, h = step[1:]
                    head = 2 * p + h
                    dve.wait_ge(wk_free, work_end("hn", p, h))
                    chain.link(nc.vector.tensor_scalar(tt[:, h, :], tt[:, h, :], EPS, None, ALU.add))
                    nc.vector.reciprocal(tt[:, h, :], tt[:, h, :]).then_inc(hr_done, 1)
                    dve.wait_ge(hsr_done, head + 1)
                    chain.link(nc.vector.scalar_tensor_tensor(dt_[:], hs[:, h, :], pcol("mlstm_norm", head), tt[:, h, :], ALU.mult, ALU.mult))
                    nc.vector.tensor_tensor(yT[:, 4 + head, :], dt_[:], sgo[:, h, :], ALU.mult).then_inc(y_done, 1)
            for j in range(4):
                dve.wait_ge(rhi_done, R_MO + j + 1)
                nc.vector.tensor_tensor(al[:, 2 * j:2 * j + 2, :], yT[:, 2 * j:2 * j + 2, :], ah[:, 2 * j:2 * j + 2, :].bitcast(fp32),
                                        ALU.subtract).then_inc(rlo_done, 1)
            for j in range(4):
                lo(S_MO + j + 2)
            post_norm(3, S_F2I - 1, "norm_mix_post", 1.0, 2)

            pre_norm(4, 2, lambda k: pcol("norm_ffn2_pre", k))
            ffn(1, S_F2I, S_F2O)
            post_norm(5, S_ATT - 1, "norm_ffn2_post", 0.5, 3)

            pre_norm(6, 3, lambda k: gmod[:, k:k + 1], shift=True)
            dve.wait_ge(att_init, 1)

            def att_step(step, r):
                kind, h = step[0], step[1] if len(step) > 1 else 0
                if kind == "Q":
                    i = step[2]
                    idx, n = 4 * h + i, (i + 1) * P
                    dve.wait_ge(sig_done, r * 8 + (idx + 1))
                    chain.link(nc.vector.tensor_tensor_scan(Gc[:, i, 0:n][:, ::-1], g1[:, idx % 2, 0:n][:, ::-1],
                                                            zero1[:].to_broadcast([P, n]), 1.0, ALU.mult, ALU.add))
                    dve.wait_ge(t_mm, r * 8 + max(idx - 3, 0))
                    nc.vector.tensor_tensor(Wt[:, idx % 4, 0:n], be[:, idx % 2, 0:n], Gc[:, i, 1:n + 1], ALU.mult).then_inc(w_done, 1)
                elif kind == "V":
                    dve.wait_ge(vhi_done, r + 1)
                    bank = ps[:, 6, :].rearrange("p (b d) -> p b d", d=P)
                    for e in range(2):
                        cols = slice(DK * e, DK * e + DK)
                        last = nc.vector.tensor_tensor(vpl[:, e, :, cols], bank[:, :, cols], vph[:, e, :, cols].bitcast(fp32), ALU.subtract)
                    last.then_inc(vlo_done, 1)
                elif kind == "T":
                    i = step[2]
                    idx = 4 * h + i
                    dve.wait_ge(thi_done, r * 8 + (idx + 1))
                    place = (slice(None), slice(0, i + 1), slice(i * P, (i + 1) * P))
                    nc.vector.tensor_tensor(wTl[place], ps[:, 6, 0:(i + 1) * P].rearrange("p (b t) -> p b t", t=P),
                                            wTh[place].bitcast(fp32), ALU.subtract).then_inc(tlo_done, 1)

            def att_out(r):
                one = slice(r, r + 1) if isinstance(r, int) else bass.ds(r, 1)
                dve.wait_ge(pv_mm, r * 2 + 2)
                dve.wait_ge(gah_done, r)
                nc.vector.tensor_tensor(ga[:], ps[:, 7, :], zs[:], ALU.mult).then_inc(ga_done, 1)
                dve.wait_ge(gah_done, r + 1)
                nc.vector.tensor_tensor(gal[:, one, :], ga[:].unsqueeze(1), gah[:, one, :].bitcast(fp32), ALU.subtract).then_inc(gal_done, 1)

            def att_slot(i, j):
                lo(S_ATT + j + 2, i)
                if j == 0:
                    dve.wait_ge(slot_used, i * 2 + (S_ATT + 1))
                    nc.vector.tensor_copy(k2[:], ps[:, 1, :]).then_inc(ke_done, 1)
                else:
                    dve.wait_ge(sz_done, i + 1)
                    nc.vector.tensor_tensor(zs[:], sz[:], ps[:, 3, :], ALU.mult).then_inc(zs_done, 1)

            att_slot(0, 0)
            att_slot(0, 1)
            with dve.Fori(0, PAIRS - 1) as r:
                chain.enter(r, 8)
                for j in range(2):
                    for s in range(8):
                        for step in ATT_STEPS.get(8 * j + s, []):
                            att_step(step, r)
                    if j == 1:
                        att_out(r)
                    att_slot(r + 1, j)
            chain.leave(PAIRS - 1)

            def pooled(g):
                dve.wait_ge(u_in, g + 1)
                if g:
                    dve.wait_ge(dlo_done, g)
                w = WINDOWS[g]
                source, target, reach = uS, p1, 1
                while reach < w:
                    nc.vector.tensor_copy(target[:, :, 0:reach], source[:, :, 0:reach])
                    chain.link(nc.vector.tensor_tensor(target[:, :, reach:T], source[:, :, reach:T], source[:, :, 0:T - reach], ALU.add))
                    source, target, reach = target, (p2 if target is p1 else p1), 2 * reach
                chain.link(nc.vector.tensor_tensor(target[:, :, 0:w], source[:, :, 0:w],
                                                   invc[:, g, 0:w].unsqueeze(1).to_broadcast([P, 2, w]), ALU.mult))
                nc.vector.tensor_tensor(target[:, :, 0:w], target[:, :, 0:w], uS[:, :, 0:w], ALU.subtract)
                nc.vector.scalar_tensor_tensor(target[:, :, w:T], source[:, :, w:T], 1.0 / w, uS[:, :, w:T],
                                               ALU.mult, ALU.subtract).then_inc(d_done, 1)
                dve.wait_ge(dhi_done, g + 1)
                nc.vector.tensor_tensor(dl[:, 2 * g:2 * g + 2, :], target[:], dh[:, 2 * g:2 * g + 2, :].bitcast(fp32),
                                        ALU.subtract).then_inc(dlo_done, 1)

            def pool_slot(j):
                kind, g = POOL_ORDER[j]
                lo(S_POOL + j + 2)
                if kind == "z":
                    dve.wait_ge(zsig, g + 1)
                    nc.vector.tensor_tensor(zb[:, 2 * g:2 * g + 2, :], sb2[:], ps[:, 2 * (j % 2):2 * (j % 2) + 2, :], ALU.mult).then_inc(zb_done, 1)

            for j in range(2):
                for s in range(8):
                    for step in ATT_STEPS.get(8 * j + s, []):
                        att_step(step, PAIRS - 1)
                if j == 1:
                    att_out(PAIRS - 1)
                    pooled(0)
                pool_slot(j)
            for j in range(2, 8):
                kind, g = POOL_ORDER[j - 1]
                if kind == "u":
                    pooled(g)
                pool_slot(j)
            for g in range(4):
                if g < 3:
                    dve.wait_ge(pw_mm, g + 1)
                else:
                    dve.wait_ge(slot_used, S_FIN)
                part = p1 if g % 2 == 0 else p2
                dve.wait_ge(dlo_done, 4)
                if g >= 2:
                    dve.wait_ge(ybl_done, g - 1)
                for c in range(2):
                    last = nc.vector.scalar_tensor_tensor(part[:, c, :], ps[:, 2 * (g % 2) + c, :], pcol("pool_scale_2", 2 * g + c),
                                                          zb[:, 2 * g + c, :], ALU.mult, ALU.mult)
                last.then_inc(yb_t, 1)
                dve.wait_ge(ybh_done, g + 1)
                nc.vector.tensor_tensor(dl[:, 2 * g:2 * g + 2, :], part[:], dh[:, 2 * g:2 * g + 2, :].bitcast(fp32),
                                        ALU.subtract).then_inc(ybl_done, 1)
            lo(S_FIN + 1)
            with dve.Fori(0, 4) as c:
                for j in range(4):
                    n = S_FIN + j
                    dve.wait_ge(hi_done, c * 4 + (n + 3))
                    nc.vector.tensor_tensor(wl[n % 2][:], raw[n % 2][:], wh[n % 2][:].bitcast(fp32), ALU.subtract).then_inc(lo_done, 1)
                    if j == 1:
                        dve.wait_ge(sm_done, c * 2 + 1)
                        dve.wait_ge(mg_done, c)
                        dve.wait_ge(slot_used, c * 4 + (n + 1))
                        nc.vector.tensor_tensor(m1[:], sm[:], ps[:, 2:4, :], ALU.mult).then_inc(m_done, 1)
                    elif j == 3:
                        dve.wait_ge(sm_done, c * 2 + 2)
                        dve.wait_ge(slot_used, c * 4 + (n + 1))
                        nc.vector.tensor_tensor(m2[:], sn[:], ps[:, 2:4, :], ALU.mult).then_inc(m_done, 1)
                        dve.wait_ge(m_done, c * 2 + 2)
                        nc.vector.tensor_tensor(mg[:, bass.ds(c * 2, 2), :], m1[:], m2[:], ALU.add).then_inc(mg_done, 1)
            for j in range(4):
                dve.wait_ge(rhi_done, R_OUT + j + 1)
                nc.vector.tensor_tensor(al[:, 2 * j:2 * j + 2, :], mg[:, 2 * j:2 * j + 2, :], ah[:, 2 * j:2 * j + 2, :].bitcast(fp32),
                                        ALU.subtract).then_inc(rlo_done, 1)
            for j in range(2):
                lo(S_OUT + j + 2)
            dve.wait_ge(slot_used, S_END)
            for k in LAST:
                nc.vector.scalar_tensor_tensor(xT[:, k, :], ps[:, k, :], mod[:, 16 + k:17 + k], xT[:, k, :], ALU.mult, ALU.add).then_inc(x_ready, 1)
            variance(7)
            for k in range(KD):
                if k >= 2:
                    dve.wait_ge(ot_mm, k - 1)
                nc.vector.scalar_tensor_tensor(tt[:, k % 2, :], xT[:, k, :], pcol("final_gain_2", k), rstd[:], ALU.mult, ALU.mult).then_inc(t_done, 1)

        @block.tensor
        def _(pe):
            def three(bank, w, m, start, stop):
                nc.tensor.matmul(bank, w[0], m[0], start=start, stop=False)
                nc.tensor.matmul(bank, w[0], m[1], start=False, stop=False)
                return nc.tensor.matmul(bank, w[1], m[0], start=False, stop=stop)

            def in_slot(n, i, banks, moving, steps=None, ready=None, each=2):
                pe.wait_ge(lo_done, i * each + (n + 1))
                for k in range(KD):
                    if steps:
                        steps(k)
                    if ready is not None:
                        pe.wait_ge(a_ready, 8 * ready + k + 1)
                    for c in range(2):
                        at = slice(k * CB + c * P, k * CB + (c + 1) * P)
                        last = three(ps[:, banks + c, :], (wh[n % 2][:, at], wl[n % 2][:, at]),
                                     (moving[0][:, k, :], moving[1][:, k, :]), k == 0, k == KD - 1)
                last.then_inc(slot_used, 1)

            def out_slot(n, i, moving, ready, first=False, last=False, blocks=range(KD), before=None):
                pe.wait_ge(lo_done, i * 2 + (n + 1))
                pe.wait_ge(rlo_done, ready)
                for kk in range(2):
                    for c in blocks:
                        if kk == 0 and before:
                            before(c)
                        at = slice(kk * D + c * P, kk * D + (c + 1) * P)
                        end = three(ps[:, c, :], (wh[n % 2][:, at], wl[n % 2][:, at]), (moving[0][:, kk, :], moving[1][:, kk, :]),
                                    first and kk == 0, last and kk == 1)
                end.then_inc(slot_used, 1)

            def sums(stage, before=None):
                for j in range(KD):
                    pe.wait_ge(sq_done, 8 * stage + j + 1)
                    if j == 0 and before:
                        before()
                    nc.tensor.matmul(ps[:, 7, :], ones[:], sq[:, j % 2, :], start=j == 0, stop=j == KD - 1).then_inc(sum_acc, 1)

            def ffn(f, pre, base_in, base_out):
                with pe.Fori(0, NFI // 2) as i:
                    pe.wait_ge(silu_done, i + f * NFO)
                    in_slot(base_in, i, 0, (ah, al), ready=pre)
                    pe.wait_ge(hid_ready, i + f * NFO)
                    in_slot(base_in + 1, i, 2, (ah, al))

                def unit(j, i=0, **more):
                    out_slot(base_out + j, i, (rh[:, j % 2, :, :], rl[:, j % 2, :, :]), i * 2 + ((R_F1, R_F2)[f] + j + 1), **more)

                def free(c):
                    if c == 0:
                        pe.wait_ge(silu_done, (f + 1) * NFO)
                    if c == 2:
                        pe.wait_ge(hid_ready, (f + 1) * NFO)

                unit(0, first=True, blocks=[4, 5, 6, 7, 0, 1, 2, 3], before=free)
                with pe.Fori(0, 4) as i:
                    unit(1, i)
                    unit(2, i)
                unit(9)
                unit(10, last=True)

            pe.wait_ge(const_done, 1)
            pe.wait_ge(par_in, 16 * (len(vectors) + 5))
            nc.tensor.transpose(ps[:, 7, 0:n_par], par_rows[0:n_par, :], ident[0:n_par, 0:n_par]).then_inc(xt_mm, 1)
            pe.wait_ge(x_in, 16 * TB)
            for k in range(KD):
                if k >= 4:
                    pe.wait_ge(x_ready, k - 3)
                for b in range(TB):
                    last = nc.tensor.transpose(ps[:, k % 4, b * P:(b + 1) * P], xtok[:, b, k * P:(k + 1) * P], ident[:])
                last.then_inc(xt_mm, 1)
            sums(0, lambda: pe.wait_ge(par_ready, 1))
            ffn(0, 0, S_F1I, S_F1O)
            sums(1, lambda: pe.wait_ge(h7_done, 1))
            pe.wait_ge(ada_step, 3 * KD)
            pe.wait_ge(t_done, 8 * 1 + 1)
            for j in range(3 * KD):
                last = nc.tensor.matmul(ps[:, 0, j:j + 1], ada[:, j * P:(j + 1) * P], ones[:, 0:1], start=True, stop=True)
            last.then_inc(ada_mm, 1)
            sums(2)

            work = [0]

            def use_work():
                work[0] += 1
                if work[0] > 2:
                    pe.wait_ge(wk_free, work[0] - 2)
                return ps[:, 4 + (work[0] - 1) % 2, :]

            n_slot = 0
            for step in MIXER:
                kind = step[0]
                if kind == "slot":
                    if n_slot >= 2:
                        pe.wait_ge(*evacuated[n_slot - 2])
                    elif n_slot == 0:
                        pe.wait_ge(mod_done, 1)
                    in_slot(S_MIX + n_slot, 0, 2 * (n_slot % 2), (ah, al))
                    n_slot += 1
                elif kind == "gates":
                    pe.wait_ge(gw_lo, 1)
                    for k in range(KD):
                        pe.wait_ge(a_ready, 8 * 1 + k + 1)
                        last = three(ps[:, 6, :], (gh[:, k, :], gl[:, k, :]), (ah[:, k, :], al[:, k, :]), k == 0, k == KD - 1)
                    last.then_inc(gate_mm, 1)
                elif kind == "cols":
                    pe.wait_ge(rows_done, 1)
                    bank = use_work()
                    for b in range(TB):
                        last = nc.tensor.transpose(bank[:, b * 64:(b + 1) * 64], crow[:, b * P:(b + 1) * P], ident[0:64, 0:64])
                    last.then_inc(wk_mm, 1)
                elif kind == "bc":
                    pe.wait_ge(erow_done, 1)
                    for u in range(4):
                        row = 32 * (u % 2) + 2 * step[1] + u // 2
                        pick = ident[0:64, row:row + 1].to_broadcast([64, P])
                        for source in (mrow, erow):
                            nc.tensor.matmul(use_work(), pick, source[:], start=True, stop=True).then_inc(wk_mm, 1)
                elif kind == "S":
                    p, h = step[1:]
                    pe.wait_ge(pf_act, 4 * p + 1)
                    d = slice(DK * h, DK * h + DK)
                    for b in range(TB):
                        nc.tensor.matmul(use_work(), kS[d, b * P:(b + 1) * P], qS[d, :], start=True, stop=True).then_inc(wk_mm, 1)
                elif kind == "vt":
                    pe.wait_ge(pf_act, 4 * step[1] + 2)
                    for h in range(2):
                        bank = use_work()
                        for b in range(TB):
                            last = nc.tensor.transpose(bank[:, b * P:(b + 1) * P], vT[:, h, b * P:(b + 1) * P], ident[:])
                        last.then_inc(wk_mm, 1)
                elif kind == "mm":
                    p, h, d = step[1:]
                    u = 4 * p + 2 * h + d
                    pe.wait_ge(p_ready, u + 1)
                    pe.wait_ge(wk_free, work_end("vt", p))
                    pe.wait_ge(h_done, u)
                    order = range(TB) if d == 0 else range(TB - 1, -1, -1)
                    for bank, stationary in ((6, lambda b: vS[:, h, b, :]), (7, lambda b: ones[:])):
                        for j, b in enumerate(order):
                            t0, t1 = span(d, b)
                            last = nc.tensor.matmul(ps[:, bank, t0:t1], stationary(b), E[:, u % 2, b, t0:t1], start=j == 0, stop=j == TB - 1)
                    last.then_inc(u_mm, 1)
                elif kind == "hn":
                    p, h = step[1:]
                    pe.wait_ge(hsq_done, 2 * p + h + 1)
                    nc.tensor.matmul(use_work(), ones[:], sq[:, h, :], start=True, stop=True).then_inc(wk_mm, 1)
            pe.wait_ge(pf_dve, 4)
            pe.wait_ge(y_done, 4)
            for j in range(4):
                out_slot(S_MO + j, 0, (ah[:, 2 * j:2 * j + 2, :], al[:, 2 * j:2 * j + 2, :]), R_MO + j + 1, first=j == 0, last=j == 3)
            sums(3, lambda: pe.wait_ge(h7_done, 2))

            sums(4)
            ffn(1, 2, S_F2I, S_F2O)
            sums(5, lambda: pe.wait_ge(h7_done, 3))

            sums(6)

            def att_step(step, r):
                kind, h = step[0], step[1] if len(step) > 1 else 0
                if kind == "Q":
                    i = step[2]
                    idx, n = 4 * h + i, (i + 1) * P
                    if idx == 0:
                        pe.wait_ge(qe_done, r + 1)
                        pe.wait_ge(ke_done, r + 1)
                    pe.wait_ge(sig_done, r * 8 + max(idx - 1, 0))
                    bank, d = ps[:, 4 + idx % 2, :], slice(DK * h, DK * h + DK)
                    nc.tensor.matmul(bank[:, 0:n], q2[d, i * P:n], k2[d, 0:n], start=True, stop=False)
                    nc.tensor.matmul(bank[:, i * P:n], identb[:], maskS[:], start=False, stop=True).then_inc(q_mm, 1)
                elif kind == "V":
                    pe.wait_ge(ve_done, r + 1)
                    pe.wait_ge(tlo_done, r * 8)
                    for b in range(TB):
                        last = nc.tensor.transpose(ps[:, 6, b * P:(b + 1) * P], v2[:, b * P:(b + 1) * P], ident[:])
                    last.then_inc(v_mm, 1)
                elif kind == "T":
                    i = step[2]
                    idx = 4 * h + i
                    pe.wait_ge(w_done, r * 8 + (idx + 1))
                    if idx == 0:
                        pe.wait_ge(vlo_done, r + 1)
                    else:
                        pe.wait_ge(tlo_done, r * 8 + idx)
                    for b in range(i + 1):
                        last = nc.tensor.transpose(ps[:, 6, b * P:(b + 1) * P], Wt[:, idx % 4, b * P:(b + 1) * P], ident[:])
                    last.then_inc(t_mm, 1)
                elif kind == "PV":
                    pe.wait_ge(tlo_done, r * 8 + (4 * h + 4))
                    if h == 0:
                        pe.wait_ge(ga_done, r)
                    for b in range(TB):
                        last = three(ps[:, 7, b * P:T], (vph[:, h, b, :], vpl[:, h, b, :]), (wTh[:, b, b * P:T], wTl[:, b, b * P:T]),
                                     h == 0 and b == 0, h == 1 and b == TB - 1)
                    last.then_inc(pv_mm, 1)

            def steps_of(j, r):
                def steps(k):
                    for step in ATT_STEPS.get(8 * j + k, []):
                        att_step(step, r)
                return steps

            in_slot(S_ATT, 0, 0, (ah, al), ready=3)
            in_slot(S_ATT + 1, 0, 2, (ah, al))
            with pe.Fori(0, PAIRS - 1) as r:
                pe.wait_ge(qe_done, r + 1)
                pe.wait_ge(ke_done, r + 1)
                in_slot(S_ATT + 2, r, 0, (ah, al), steps=steps_of(0, r))
                pe.wait_ge(ve_done, r + 1)
                pe.wait_ge(zs_done, r + 1)
                in_slot(S_ATT + 3, r, 2, (ah, al), steps=steps_of(1, r))
            pool_read = {"u": u_in, "z": zb_done}
            for j in range(8):
                if j < 2:
                    for s in ((qe_done, ke_done), (ve_done, zs_done))[j]:
                        pe.wait_ge(s, PAIRS)
                else:
                    kind, g = POOL_ORDER[j - 2]
                    pe.wait_ge(pool_read[kind], g + 1)
                in_slot(S_POOL + j, 0, 2 * (j % 2), (ah, al), steps=steps_of(j, PAIRS - 1) if j < 2 else None)
            n = S_POOL + 8
            pe.wait_ge(lo_done, n + 1)
            for g in range(4):
                pe.wait_ge(dlo_done, g + 1)
                if g < 2:
                    pe.wait_ge(pool_read[POOL_ORDER[6 + g][0]], POOL_ORDER[6 + g][1] + 1)
                else:
                    pe.wait_ge(yb_t, g - 1)
                for c in range(2):
                    for k in range(2):
                        at = slice((2 * g + k) * CB + c * P, (2 * g + k) * CB + (c + 1) * P)
                        last = three(ps[:, 2 * (g % 2) + c, :], (wh[n % 2][:, at], wl[n % 2][:, at]),
                                     (dh[:, 2 * g + k, :], dl[:, 2 * g + k, :]), k == 0, k == 1)
                last.then_inc(pw_mm if g < 3 else slot_used, 1)

            with pe.Fori(0, 4) as c:
                for j, moving in enumerate(((ah, al), (gah, gal), (ah, al), (dh, dl))):
                    if j % 2 == 0:
                        pe.wait_ge(yb_t, 3)
                        pe.wait_ge(sm_done, c * 2 + j // 2)
                    else:
                        pe.wait_ge(yb_t, 4)
                        pe.wait_ge(m_done, c * 2 + j // 2)
                        pe.wait_ge(gal_done, PAIRS)
                    if j == 3:
                        pe.wait_ge(ybl_done, 4)
                    in_slot(S_FIN + j, c, 2 * (j % 2), moving, each=4)
            pe.wait_ge(m_done, 8)
            for j in range(4):
                out_slot(S_OUT + j, 0, (ah[:, 2 * j:2 * j + 2, :], al[:, 2 * j:2 * j + 2, :]), R_OUT + j + 1, first=j == 0, last=j == 3)
            sums(7)
            for k in range(KD):
                pe.wait_ge(t_done, 8 * 7 + k + 1)
                if k >= 2:
                    pe.wait_ge(ot_done, k - 1)
                for b in range(TB):
                    last = nc.tensor.transpose(ps[:, 4 + k % 2, b * P:(b + 1) * P], tt[:, k % 2, b * P:(b + 1) * P], ident[:])
                last.then_inc(ot_mm, 1)


def kernel(**inputs):
    import numpy as np
    import concourse.bacc as bacc
    from concourse import mybir as m
    from concourse.bass_utils import run_bass_kernel_spmd as run

    nc = bacc.Bacc("TRN2", target_bir_lowering=False, num_devices=1)
    arrays, aps = {}, {}
    for name, value in inputs.items():
        value = np.ascontiguousarray(value)
        arrays["in_" + name] = value
        aps[name] = nc.dram_tensor("in_" + name, value.shape, m.dt.from_np(value.dtype), kind="ExternalInput").ap()
    out = nc.dram_tensor("out_0", (1, T, D), m.dt.float32, kind="ExternalOutput").ap()
    program(nc, aps, out)
    return run(nc, [arrays], core_ids=[0]).results[0]["out_0"]
```

```python
import concourse.bass as bass
from concourse import mybir
from contextlib import ExitStack

fp32 = mybir.dt.float32
f32r = mybir.dt.float32r
bf16 = mybir.dt.bfloat16
ALU = mybir.AluOpType
ACT = mybir.ActivationFunctionType
AX = mybir.AxisListType

P = 128
T = 512
TB = T // P
D = 1024
KD = D // P
FF = 2816
KF = FF // P
SLOT = 2048
CB = SLOT // KD
EPS = 1e-6
NEG = -1e30
ORDER = [7, 6, 4, 0, 1, 2, 3, 5]

HEADS = 4
DK = 64
DV = 128
CONV = 512
QO, KO, VO, OO, GO = 3 * CONV, 3 * CONV + 256, 3 * CONV + 512, 3 * CONV + 1024, 3 * CONV + 1536
PAIRS = 8
WINDOWS = (2, 4, 8, 16)
ZSCALE = 0.125

NFI = 2 * FF // CB
NFO = KF // 2
S_F1I = 0
S_F1O = S_F1I + NFI
S_MIX = S_F1O + NFO
S_MO = S_MIX + 12
S_F2I = S_MO + 4
S_F2O = S_F2I + NFI
S_ATT = S_F2O + NFO
S_POOL = S_ATT + 2 * PAIRS
S_FIN = S_POOL + 9
S_OUT = S_FIN + 16
S_END = S_OUT + 4
POOL_ORDER = [("u", 0), ("u", 1), ("z", 0), ("u", 2), ("z", 1), ("u", 3), ("z", 2), ("z", 3)]

MIXER = [(0, "qk", {0: [("gates",)], 1: [("rows",)]}),
         (0, "v", {1: [("S", 0, 0, 0)], 2: [("S", 0, 0, 1)], 3: [("S", 0, 0, 2)], 4: [("S", 0, 0, 3)], 5: [("cols",)],
                   6: [("bc", 0, 0)], 7: [("bc", 0, 1)]}),
         (0, "cg", {0: [("bc", 0, 2)], 1: [("bc", 0, 3)], 2: [("vt", 0, 0)], 3: [("vt", 0, 1)], 4: [("prep", 0, 0, 0)],
                    6: [("prep", 0, 0, 1)]}),
         (0, "o", {2: [("mm", 0, 0, 0)], 3: [("S", 0, 1, 0)], 4: [("S", 0, 1, 1)], 5: [("mm", 0, 0, 1)], 6: [("S", 0, 1, 2)],
                   7: [("S", 0, 1, 3)]}),
         (1, "qk", {0: [("prep", 0, 1, 0)], 1: [("prep", 0, 1, 1)], 4: [("mm", 0, 1, 0)], 7: [("mm", 0, 1, 1)]}),
         (1, "v", {0: [("hn", 0, 0)], 1: [("hn", 0, 1), ("bc", 1, 0)], 2: [("bc", 1, 1)], 3: [("bc", 1, 2)], 4: [("bc", 1, 3), ("S", 1, 0, 0)],
                   5: [("S", 1, 0, 1)], 6: [("S", 1, 0, 2)], 7: [("S", 1, 0, 3)]}),
         (0, "hc", {1: [("hy", 0, 0)], 2: [("hy", 0, 1)], 3: [("vt", 1, 0)], 4: [("vt", 1, 1)], 5: [("prep", 1, 0, 0)],
                    6: [("hz", 0, 0)], 7: [("prep", 1, 0, 1), ("hz", 0, 1)]}),
         (0, "bg", {2: [("mm", 1, 0, 0)], 3: [("S", 1, 1, 0)], 4: [("S", 1, 1, 1)], 5: [("mm", 1, 0, 1)], 6: [("S", 1, 1, 2)],
                    7: [("S", 1, 1, 3)]}),
         (1, "o", {0: [("prep", 1, 1, 0)], 1: [("prep", 1, 1, 1)], 4: [("mm", 1, 1, 0)], 7: [("mm", 1, 1, 1)]}),
         (1, "cg", {0: [("hn", 1, 0)], 1: [("hn", 1, 1)], 5: [("hy", 1, 0)], 6: [("hy", 1, 1)]}),
         (1, "hc", {0: [("hz", 1, 0)], 1: [("hz", 1, 1)]}),
         (1, "bg", {0: [("split", 0)], 1: [("split", 1)]})]
WORK = {}
for _, _, during in MIXER:
    for k in sorted(during):
        for step in during[k]:
            if step[0] in ("S", "cols", "bc", "vt", "hy"):
                WORK[step] = len(WORK) + 1
MIX_OUT = (0, 2, 3, 1)
DVE_EVAC = ("hc", "bg")

ATT_STEPS = {0: [("Q", 0, 0)], 1: [("Q", 0, 1), ("V",)], 2: [("Q", 0, 2)], 3: [("Q", 0, 3), ("T", 0, 0)],
             4: [("T", 0, 1), ("Q", 1, 0)], 5: [("T", 0, 2), ("Q", 1, 1)], 6: [("T", 0, 3), ("Q", 1, 2)],
             7: [("Q", 1, 3)], 8: [("PV", 0)], 9: [("T", 1, 0)], 10: [("T", 1, 1)], 11: [("T", 1, 2)],
             12: [("T", 1, 3)], 14: [("PV", 1)]}


class Chain:

    def __init__(self, engine, sem):
        self.engine, self.sem, self.base, self.n, self.i, self.per = engine, sem, 0, 0, None, 0

    def enter(self, i, per):
        self.base, self.n, self.i, self.per = self.base + self.n, 0, i, per

    def leave(self, times):
        assert self.n == self.per, self.n
        self.base, self.n, self.i = self.base + times * self.per, 0, None

    def link(self, instruction):
        self.n += 1
        at = self.base + self.n
        if self.i is not None:
            at = self.i * self.per + at
        instruction.then_inc(self.sem, 1)
        self.engine.wait_ge(self.sem, at)


def program(nc, a, out):
    with ExitStack() as ctx:
        keep = ctx

        def sb(name, shape, dt=fp32, where=None):
            return (where or keep).enter_context(nc.sbuf_tensor(name, shape, dt))

        def sem(name):
            return ctx.enter_context(nc.semaphore(name))

        xT = sb("xT", [P, KD, T])
        ah = sb("ah", [P, KD, T], f32r)
        al = sb("al", [P, KD, T], f32r)
        raw = [sb(f"raw{i}", [P, SLOT]) for i in range(2)]
        wh = [sb(f"wh{i}", [P, SLOT], f32r) for i in range(2)]
        wl = [sb(f"wl{i}", [P, SLOT], f32r) for i in range(2)]
        sq = sb("sq", [P, 2, T])
        rstd = sb("rstd", [P, T])
        r4 = sb("r4", [P, TB])
        diag = sb("diag", [P, TB, P])
        scrap = sb("scrap", [P, 4])
        tt = sb("tt", [P, 2, T])
        ident = sb("ident", [P, P])
        ones = sb("ones", [P, P])
        maskF = sb("maskF", [P, P])
        maskB = sb("maskB", [P, P])
        identb = sb("identb", [P, P], bf16)
        maskS = sb("maskS", [P, P], bf16)
        zero1 = sb("zero1", [P, 1])
        par_rows = sb("par_rows", [P, P])
        par = sb("par", [P, P])
        gbias = sb("gbias", [P, 1])
        gw = sb("gw", [P, KD, 16])
        sc = sb("sc", [P, KD])
        mod = sb("mod", [P, 24])
        gmod = sb("gmod", [P, KD])
        cT = sb("cT", [P, 2, TB, 64])
        d4 = sb("d4", [P, TB])
        h4 = sb("h4", [P, HEADS, TB])
        invc = sb("invc", [P, 4, 16])
        h7 = sb("h7", [P, T])

        with ExitStack() as phase:
            hid = sb("hid", [P, KF, T], where=phase)
            sg = sb("sg", [P, 2, T], where=phase)
            gt = sb("gt", [P, 2, T], where=phase)
            rh = sb("rh", [P, 2, 2, T], f32r, where=phase)
            rl = sb("rl", [P, 2, 2, T], f32r, where=phase)
            ada_raw = sb("ada_raw", [P, KD, P], where=phase)
            ada = sb("ada", [P, 3 * D], where=phase)
        with ExitStack() as phase:
            xtok = sb("xtok", [P, TB, D], where=phase)
        with ExitStack() as phase:
            outS = sb("outS", [P, TB, D], where=phase)
        with ExitStack() as phase:
            with ExitStack() as inner:
                gh = sb("gh", [P, KD, P], f32r, where=inner)
                gl = sb("gl", [P, KD, P], f32r, where=inner)
            with ExitStack() as inner:
                yh = sb("yh", [P, 2, 2, T], f32r, where=inner)
                yl = sb("yl", [P, 2, 2, T], f32r, where=inner)
            E = sb("E", [P, 2, TB, T], where=phase)
            Sx = sb("Sx", [P, TB, T], where=phase)
            Mb = sb("Mb", [P, 4, T], where=phase)
            mrow = sb("mrow", [64, T], where=phase)
            erow = sb("erow", [64, T], where=phase)
            vT = sb("vT", [P, 2, T], where=phase)
            vS = sb("vS", [P, 2, TB, P], where=phase)
            qS = sb("qS", [P, T], where=phase)
            kS = sb("kS", [P, T], where=phase)
            cgS = sb("cgS", [P, 2, T], where=phase)
            ux = sb("ux", [P, 2, T + 2], where=phase)
            ct = sb("ct", [P, 2, T], where=phase)
            sgo = sb("sgo", [P, HEADS, T], where=phase)
            hs = sb("hs", [P, 2, T], where=phase)
            yT = sb("yT", [P, KD, T], where=phase)
        dt_, dg = h7, diag
        zrow, lrow = E[:, 0, 0, :], E[:, 0, 1, :]
        frow, brow, crow = E[0:64, 0, 2, :], E[0:64, 0, 3, :], E[0:64, 1, 0, :]
        with ExitStack() as phase:
            gah = sb("gah", [P, KD, T], f32r, where=phase)
            gal = sb("gal", [P, KD, T], f32r, where=phase)
            with ExitStack() as inner:
                wTh = sb("wTh", [P, TB, T], f32r, where=inner)
                wTl = sb("wTl", [P, TB, T], f32r, where=inner)
                Gc = sb("Gc", [P, TB, T + 1], where=inner)
                Wt = sb("Wt", [P, 4, T], where=inner)
                vph = sb("vph", [P, 2, TB, P], f32r, where=inner)
                vpl = sb("vpl", [P, 2, TB, P], f32r, where=inner)
                zs = sb("zs", [P, T], where=inner)
                ga = sb("ga", [P, T], where=inner)
                be = sb("be", [P, 2, T], where=inner)
                g1 = sb("g1", [P, 2, T], where=inner)
                q2 = sb("q2", [P, T], where=inner)
                k2 = sb("k2", [P, T], where=inner)
                v2 = sb("v2", [P, T], where=inner)
            dh = sb("dh", [P, KD, T], f32r, where=phase)
            dl = sb("dl", [P, KD, T], f32r, where=phase)
            with ExitStack() as inner:
                zb = sb("zb", [P, KD, T], where=inner)
                uS = sb("uS", [P, 2, T], where=inner)
                p1 = sb("p1", [P, 2, T], where=inner)
            mg = sb("mg", [P, KD, T], where=phase)
            sm = sb("sm", [P, 2, T], where=phase)
            sn = sb("sn", [P, 2, T], where=phase)
        sb2, m1, p2, m2, sz = tt, tt, sq, sq, h7
        ps = ctx.enter_context(nc.psum_tensor("ps", [P, 8, T], fp32))

        raw_full = [sem(f"raw_full{i}") for i in range(2)]
        hi_done, lo_done = sem("hi_done"), sem("lo_done")
        slot_used = sem("slot_used")
        x_in, par_in = sem("x_in"), sem("par_in")
        const_done, par_cols, par_ready = sem("const_done"), sem("par_cols"), sem("par_ready")
        xt_mm = sem("xt_mm")
        x_ready = sem("x_ready")
        sq_done, sum_acc, var_done, rstd_done = sem("sq_done"), sem("sum_acc"), sem("var_done"), sem("rstd_done")
        diag_done, rb_done = sem("diag_done"), sem("rb_done")
        bank_done = sem("bank_done")
        gt_done, ut_done = sem("gt_done"), sem("ut_done")
        t_done, ah_done, a_ready = sem("t_done"), sem("ah_done"), sem("a_ready")
        silu_done, hid_ready = sem("silu_done"), sem("hid_ready")
        rhi_done, rlo_done = sem("rhi_done"), sem("rlo_done")
        h7_done = sem("h7_done")
        sc_done, ada_in, ada_step, ada_mm, mod_done = sem("sc_done"), sem("ada_in"), sem("ada_step"), sem("ada_mm"), sem("mod_done")
        act_self, dve_self, pool_self = sem("act_self"), sem("dve_self"), sem("pool_self")
        gpad, gw_hi, gw_lo, gate_mm = sem("gpad"), sem("gw_hi"), sem("gw_lo"), sem("gate_mm")
        z_done, abs_done, ln_done, rows_done, erow_done = sem("z_done"), sem("abs_done"), sem("ln_done"), sem("rows_done"), sem("erow_done")
        wk_mm, wk_free = sem("wk_mm"), sem("wk_free")
        pf_act, pf_dve = sem("pf_act"), sem("pf_dve")
        dg_done, E_done, p_ready = sem("dg_done"), sem("E_done"), sem("p_ready")
        u_mm, h_done, hr_done, hsr_done, hn_done = sem("u_mm"), sem("h_done"), sem("hr_done"), sem("hsr_done"), sem("hn_done")
        y_done = sem("y_done")
        att_init = sem("att_init")
        q_mm, sig_done, w_done, t_mm, thi_done, tlo_done = sem("q_mm"), sem("sig_done"), sem("w_done"), sem("t_mm"), sem("thi_done"), sem("tlo_done")
        v_mm, vhi_done, vlo_done, pv_mm, ga_done, gah_done, gal_done = sem("v_mm"), sem("vhi_done"), sem("vlo_done"), sem("pv_mm"), sem("ga_done"), sem("gah_done"), sem("gal_done")
        qe_done, ke_done, ve_done, sz_done, zs_done = sem("qe_done"), sem("ke_done"), sem("ve_done"), sem("sz_done"), sem("zs_done")
        u_in, zsig, zb_done, d_done, dhi_done, dlo_done = sem("u_in"), sem("zsig"), sem("zb_done"), sem("d_done"), sem("dhi_done"), sem("dlo_done")
        pw_mm, yb_t, ybh_done, ybl_done = sem("pw_mm"), sem("yb_t"), sem("ybh_done"), sem("ybl_done")
        sm_done, m_done, mg_done = sem("sm_done"), sem("m_done"), sem("mg_done")
        ot_mm, ota_done, otv_done, out_done = sem("ot_mm"), sem("ota_done"), sem("otv_done"), sem("out_done")

        vectors = [("norm_ffn1_pre", 8), ("norm_ffn1_post", 8), ("norm_mix_pre", 8), ("norm_mix_post", 8),
                   ("norm_ffn2_pre", 8), ("norm_ffn2_post", 8), ("norm_gain_2", 8), ("final_gain_2", 8),
                   ("c_2", 8), ("b_ada_2", 24), ("pool_scale_2", 8), ("conv_w", 12), ("conv_b", 4), ("mlstm_norm", 4)]
        col, n_par = {}, 0
        for name, rows in vectors:
            col[name] = n_par
            n_par += rows

        def pcol(name, k):
            return par[:, col[name] + k:col[name] + k + 1]

        def flat(ap):
            n = len(ap.shape)
            letters = " ".join("abc"[:n])
            return ap if n == 1 else ap.rearrange(f"{letters} -> ({letters})")

        def wview(name, k0=None):
            w = a[name]
            w = w.rearrange("o r c -> (o r) c") if len(w.shape) == 3 else w
            return w.rearrange("(k p) c -> p k c", p=P)

        W1I, W1O = wview("w_ffn1_in"), wview("w_ffn1_out")
        W2I, W2O = wview("w_ffn2_in"), wview("w_ffn2_out")
        WMI, WMO = wview("w_mix_in"), wview("w_mix_out")
        WHI, WHO = wview("w_in_2"), wview("w_out_2")
        WBA, WBB = wview("w_branch_a_2"), wview("w_branch_b_2")
        WAD = wview("w_ada_2")
        PWV = a["pool_w_2"].rearrange("o g (k p) c -> p (o g k) c", p=P)

        block = ctx.enter_context(nc.Block())

        @block.sync
        def _(sp):
            for b in range(TB):
                sp.dma_start(xtok[:, b, :], a["x"][0, b * P:(b + 1) * P, :]).then_inc(x_in, 16)

            def load(n, source):
                w = raw[n % 2][:, :].rearrange("p (k c) -> p k c", k=source.shape[1])
                sp.dma_start(w, source).then_inc(raw_full[n % 2], 16)

            def load_two(n, left, right):
                w = raw[n % 2][:, :].rearrange("p (k c) -> p k c", k=KD)
                sp.dma_start(w[:, :, 0:P], left).then_inc(raw_full[n % 2], 16)
                sp.dma_start(w[:, :, P:2 * P], right).then_inc(raw_full[n % 2], 16)

            def ffn(base_in, w_in, base_out, w_out):
                with sp.Fori(0, NFI // 2) as i:
                    gate, up = sp.snap(i * CB), sp.snap(i * CB + FF)
                    sp.wait_ge(lo_done, i * 2 + max(base_in - 1, 0))
                    load(base_in, w_in[:, :, bass.ds(gate, CB)])
                    sp.wait_ge(lo_done, i * 2 + base_in)
                    load(base_in + 1, w_in[:, :, bass.ds(up, CB)])
                with sp.Fori(0, NFO // 2) as i:
                    chunk = [sp.snap(i * 4), sp.snap(i * 4 + 2)]
                    for j in range(2):
                        sp.wait_ge(lo_done, i * 2 + (base_out + j - 1))
                        load(base_out + j, w_out[:, bass.ds(chunk[j], 2), :])
                sp.wait_ge(lo_done, base_out + NFO - 2)
                load(base_out + NFO - 1, w_out[:, 2 * (NFO - 1):2 * NFO, :])

            ffn(S_F1I, W1I, S_F1O, W1O)
            for j, (p, kind, _) in enumerate(MIXER):
                n = S_MIX + j
                sp.wait_ge(lo_done, n - 1)
                if kind == "qk":
                    load_two(n, WMI[:, :, QO + P * p:QO + P * p + P], WMI[:, :, KO + P * p:KO + P * p + P])
                else:
                    c0 = {"v": VO, "o": OO, "cg": CONV, "hc": 2 * CONV, "bg": 0}[kind] + CB * p
                    load(n, WMI[:, :, c0:c0 + CB])
            for j in range(4):
                sp.wait_ge(lo_done, S_MO + j - 1)
                load(S_MO + j, WMO[:, 2 * MIX_OUT[j]:2 * MIX_OUT[j] + 2, :])
            ffn(S_F2I, W2I, S_F2O, W2O)
            with sp.Fori(0, PAIRS) as p:
                at = [sp.snap(p * P + m * D) for m in range(4)]
                for j in range(2):
                    sp.wait_ge(lo_done, p * 2 + (S_ATT + j - 1))
                    load_two(S_ATT + j, WHI[:, :, bass.ds(at[2 * j], P)], WHI[:, :, bass.ds(at[2 * j + 1], P)])
            for j, (kind, g) in enumerate(POOL_ORDER):
                sp.wait_ge(lo_done, S_POOL + j - 1)
                c0 = (4 if kind == "u" else 5) * D + g * CB
                if j < 2:
                    load_two(S_POOL + j, WHI[:, :, c0:c0 + P], WHI[:, :, c0 + P:c0 + CB])
                else:
                    load(S_POOL + j, WHI[:, :, c0:c0 + CB])
            sp.wait_ge(lo_done, S_POOL + 7)
            load(S_POOL + 8, PWV)
            with sp.Fori(1, 5) as c:
                at = [sp.snap(c * CB + (c0 - CB)) for c0 in (6 * D, 0, 7 * D, 0)]
                for j, w in enumerate((WHI, WBA, WHI, WBB)):
                    sp.wait_ge(lo_done, c * 4 + (S_FIN + j - 5))
                    load(S_FIN + j, w[:, :, bass.ds(at[j], CB)])
            for j in range(4):
                sp.wait_ge(lo_done, S_OUT + j - 1)
                load(S_OUT + j, WHO[:, 2 * j:2 * j + 2, :])
            view = out.rearrange("o (b p) c -> p (o b) c", p=P)
            half = slice(0, D // 2), slice(D // 2, D)
            sp.wait_ge(ota_done, 3)
            sp.wait_ge(otv_done, 5)
            for c in half:
                sp.dma_start(view[:, :, c], outS[:, :, c]).then_inc(out_done, 16)
            sp.wait_ge(out_done, 16 * 2)

        double = {S_MIX + j for j, s in enumerate(MIXER) if s[1] == "qk"} | set(range(S_ATT, S_POOL + 2))
        landed = {}
        for n in range(S_END):
            landed[n] = landed.get(n - 2, 0) + 16 * (2 if n in double else 1)

        @block.gpsimd
        def _(pool):
            chain = Chain(pool, pool_self)
            nc.gpsimd.memset(zero1[:], 0.0)
            nc.gpsimd.memset(ones[:], 1.0)
            nc.gpsimd.memset(ident[:], 0.0)
            nc.gpsimd.memset(identb[:], 0.0)
            nc.gpsimd.memset(maskF[:], 0.0)
            nc.gpsimd.memset(maskB[:], 0.0)
            for w in range(4):
                for t in range(WINDOWS[w]):
                    nc.gpsimd.memset(invc[:, w, t:t + 1], 1.0 / (t + 1))
            chain.link(nc.gpsimd.memset(maskS[:], 0.0))
            for m in (ident, identb):
                nc.gpsimd.affine_select(out=m[:], in_=m[:], compare_op=ALU.not_equal, fill=1.0, base=0,
                                        pattern=[[-1, P]], channel_multiplier=1)
            nc.gpsimd.affine_select(out=maskF[:], in_=maskF[:], compare_op=ALU.is_ge, fill=NEG, base=0,
                                    pattern=[[1, P]], channel_multiplier=-1)
            nc.gpsimd.affine_select(out=maskB[:], in_=maskB[:], compare_op=ALU.is_ge, fill=NEG, base=0,
                                    pattern=[[-1, P]], channel_multiplier=1)
            nc.gpsimd.affine_select(out=maskS[:], in_=maskS[:], compare_op=ALU.is_ge, fill=NEG, base=-1,
                                    pattern=[[-1, P]], channel_multiplier=1).then_inc(const_done, 1)

            pool.wait_ge(sc_done, 1)
            with pool.Fori(0, 3 * KD) as j:
                chain.enter(j, 3)
                pool.dma_start(ada_raw[:, :, :], WAD[:, :, bass.ds(j * P, P)]).then_inc(ada_in, 16)
                pool.wait_ge(ada_in, j * 16 + 16)
                chain.link(nc.gpsimd.tensor_tensor(ada_raw[:, :, :], ada_raw[:, :, :],
                                                   sc[:, :].unsqueeze(2).to_broadcast([P, KD, P]), ALU.mult))
                chain.link(nc.gpsimd.tensor_tensor(ada_raw[:, 0:4, :], ada_raw[:, 0:4, :], ada_raw[:, 4:8, :], ALU.add))
                chain.link(nc.gpsimd.tensor_tensor(ada_raw[:, 0:2, :], ada_raw[:, 0:2, :], ada_raw[:, 2:4, :], ALU.add))
                nc.gpsimd.tensor_tensor(ada[:, bass.ds(j * P, P)], ada_raw[:, 0, :], ada_raw[:, 1, :],
                                        ALU.add).then_inc(ada_step, 1)
                pool.wait_ge(ada_step, j + 1)
            chain.leave(3 * KD)

            pool.wait_ge(slot_used, S_MIX)
            nc.gpsimd.memset(gh[:].bitcast(fp32), 0.0)
            nc.gpsimd.memset(ux[:, :, 0:1], 0.0)
            nc.gpsimd.memset(ux[:, :, T + 1:T + 2], 0.0)
            nc.gpsimd.memset(gl[:].bitcast(fp32), 0.0).then_inc(gpad, 1)

            pool.wait_ge(slot_used, S_ATT)
            nc.gpsimd.memset(vph[:].bitcast(fp32), 0.0)
            for i in range(TB):
                nc.gpsimd.memset(Gc[:, i, (i + 1) * P:(i + 1) * P + 1], 1.0)
            nc.gpsimd.memset(vpl[:].bitcast(fp32), 0.0).then_inc(att_init, 1)

        evacuated = {}
        for p, what, _ in MIXER:
            reader = pf_dve if what in DVE_EVAC else pf_act
            evacuated[p, what] = reader, 1 + sum(r is reader for r, _ in evacuated.values())

        R_F1, R_MO, R_F2, R_OUT = 0, NFO, NFO + 4, 2 * NFO + 4

        def whole(o, last, j):
            return (bank_done, 7 * o + j + 1) if j < 7 else (slot_used, last + 1)

        T_OF = {1: 0, 2: 1, 3: 2, 5: 3, 6: 4, 7: 5}
        OUT_ORDER = ORDER[1:] + ORDER[:1]
        OUT_ACT, OUT_DVE = [1, 4, 7], [0, 2, 3, 5, 6]

        def span(direction, b):
            return (b * P, T) if direction == 0 else (0, (b + 1) * P)

        @block.scalar
        def _(act):
            chain = Chain(act, act_self)

            at = 0
            for name, rows in vectors:
                act.dma_start(par_rows[at:at + rows, :], flat(a[name]).rearrange("(r p) -> r p", p=P)).then_inc(par_in, 16)
                at += rows
            act.dma_start(gw[:, :, :], WMI[:, :, GO:GO + 16]).then_inc(par_in, 16)
            act.wait_ge(par_cols, 1)
            for d in range(2):
                act.dma_start(gbias[32 * d:32 * d + HEADS, :],
                              a["gate_i_bias"][0:1, HEADS * d:HEADS * d + HEADS].rearrange("o h -> h o")).then_inc(par_in, 16)
                act.dma_start(gbias[64 + 32 * d:64 + 32 * d + HEADS, :],
                              a["gate_f_bias"][0:1, HEADS * d:HEADS * d + HEADS].rearrange("o h -> h o")).then_inc(par_in, 16)

            def hi(n, i=0):
                step = landed[n] - landed[n - 2] if n >= 2 else 16
                act.wait_ge(raw_full[n % 2], i * step + landed[n])
                if n >= 2:
                    act.wait_ge(slot_used, i * 2 + (n - 1))
                nc.scalar.activation(wh[n % 2][:], raw[n % 2][:], ACT.Copy).then_inc(hi_done, 1)

            def squares(stage, ready, banks=False):
                for j, k in enumerate(ORDER):
                    ready(j, k)
                    if 8 * stage + j >= 2:
                        act.wait_ge(sum_acc, 8 * stage + j - 1)
                    source = xT[:, k, :] if not banks else ps[:, k, :] if k < 7 else h7[:]
                    nc.scalar.activation(sq[:, j % 2, :], source, ACT.Square).then_inc(sq_done, 1)

            def root(stage):
                act.wait_ge(var_done, stage + 1)
                nc.scalar.activation(r4[:], r4[:], ACT.Sqrt).then_inc(rstd_done, 1)

            def load_root(n):
                nc.scalar.activation(scrap[:, n:n + 1], zero1[:], ACT.Sqrt)

            def pre_norm(stage, pre, x_stage, shift=False):
                squares(stage, lambda j, k: act.wait_ge(x_ready, 8 * x_stage + j + 1))
                root(stage)
                for j, k in enumerate(ORDER):
                    act.wait_ge(t_done, 8 * T_OF[stage] + j + 1)
                    if shift:
                        nc.scalar.activation(ah[:, k, :], tt[:, j % 2, :], ACT.Identity, bias=mod[:, k:k + 1]).then_inc(ah_done, 1)
                    else:
                        nc.scalar.activation(ah[:, k, :], tt[:, j % 2, :], ACT.Copy).then_inc(ah_done, 1)

            def scaled_hi(pre, x_stage, gain):
                for j, k in enumerate(ORDER):
                    act.wait_ge(x_ready, 8 * x_stage + j + 1)
                    nc.scalar.activation(ah[:, k, :], xT[:, k, :], ACT.Copy, scale=pcol(gain, k)).then_inc(ah_done, 1)

            def post_norm(stage, o, last):
                load_root(o)

                def ready(j, k):
                    if k == 7:
                        act.wait_ge(h7_done, o + 1)
                    else:
                        act.wait_ge(*whole(o, last, j))
                squares(stage, ready, banks=True)
                root(stage)

            def ffn(f, stage, base_in, base_out):
                def unit(j, i=0):
                    act.wait_ge(hid_ready, i * 2 + (f * NFO + j + 1))
                    if j >= 2:
                        act.wait_ge(slot_used, i * 2 + (base_out + j - 1))
                    nc.scalar.activation(rh[:, j % 2, :, :], hid[:, bass.ds(i * 4 + 2 * j, 2), :], ACT.Copy).then_inc(rhi_done, 1)

                def pair(i, units=()):
                    hi(base_in + 2, i)
                    if isinstance(i, int) and i == 0:
                        root(stage)
                    for j in units:
                        unit(j)
                    act.wait_ge(gt_done, i + (f * NFO + 1))
                    nc.scalar.activation(sg[:], gt[:], ACT.Silu).then_inc(silu_done, 1)
                    hi(base_in + 3, i)

                pair(0)
                with act.Fori(1, NFO - 1) as i:
                    pair(i)
                pair(NFO - 1, (0, 1))
                with act.Fori(0, 4) as i:
                    for j in range(2):
                        hi(base_out + j + 2, i)
                        unit(j + 2, i)
                hi(base_out + 10)
                unit(10)
                hi(base_out + 11)

            hi(0)
            act.wait_ge(par_ready, 1)
            scaled_hi(0, 0, "norm_ffn1_pre")
            hi(1)
            squares(0, lambda j, k: None)
            nc.scalar.activation(sc[:], par[:, col["c_2"]:col["c_2"] + KD], ACT.Silu).then_inc(sc_done, 1)
            act.wait_ge(const_done, 1)
            load_root(3)
            ffn(0, 0, S_F1I, S_F1O)
            post_norm(1, 0, S_MIX - 1)

            act.wait_ge(gpad, 1)
            for q in range(4):
                instruction = nc.scalar.activation(gh[:, :, 32 * q:32 * q + HEADS], gw[:, :, HEADS * q:HEADS * q + HEADS], ACT.Copy)
            instruction.then_inc(gw_hi, 1)
            pre_norm(2, 1, 1)
            hi(S_MIX + 1)

            def from_work(step, target, view=None):
                act.wait_ge(wk_mm, WORK[step])
                source = ps[:, 4 + WORK[step] % 2, :]
                nc.scalar.activation(target, source if view is None else view(source), ACT.Copy).then_inc(wk_free, 1)

            def mixer_step(kind, *step):
                if kind == "rows":
                    act.wait_ge(gate_mm, 1)
                    nc.scalar.activation(zrow, ps[:, 6, :], ACT.Identity, bias=gbias[:]).then_inc(z_done, 1)
                    act.wait_ge(abs_done, 1)
                    chain.link(nc.scalar.activation(lrow, lrow, ACT.Exp))
                    nc.scalar.activation(lrow, lrow, ACT.Ln, bias=1.0).then_inc(ln_done, 1)
                    act.wait_ge(rows_done, 1)
                    nc.scalar.activation(erow[:], erow[:], ACT.Exp).then_inc(erow_done, 1)
                elif kind == "cols":
                    from_work(("cols",), cT[:], lambda s: s.rearrange("p (w b r) -> p w b r", b=TB, r=64))
                elif kind == "bc":
                    act.wait_ge(p_ready, 4 * step[0])
                    from_work((kind, *step), Mb[:, step[1], :])
                elif kind == "S":
                    act.wait_ge(p_ready, 4 * step[0] + 2 * step[1])
                    from_work((kind, *step), Sx[:, step[2], :])
                elif kind == "vt":
                    act.wait_ge(u_mm, 4 * step[0])
                    from_work((kind, *step), vS[:, step[1], :, :], lambda s: s.rearrange("p (b d) -> p b d", d=P))
                elif kind == "prep":
                    p, h, d = step
                    u, row = 4 * p + 2 * h + d, 32 * d + 2 * p + h
                    if u >= 2:
                        act.wait_ge(u_mm, u - 1)
                    act.wait_ge(dg_done, u + 1)
                    for b in range(TB):
                        bias = cT[:, 0, b, row:row + 1]
                        t0, t1 = ((b + 1) * P, T) if d == 0 else (0, b * P)
                        if t1 > t0:
                            nc.scalar.activation(E[:, u % 2, b, t0:t1], Mb[:, 2 * h + d, t0:t1], ACT.Exp, bias=bias, scale=-1.0)
                        last = nc.scalar.activation(E[:, u % 2, b, b * P:(b + 1) * P], dg[:, b, :], ACT.Exp, bias=bias)
                    last.then_inc(E_done, 1)
                elif kind == "hn":
                    head = 2 * step[0] + step[1]
                    act.wait_ge(hr_done, head + 1)
                    nc.scalar.activation(h4[:, head, :], h4[:, head, :], ACT.Sqrt).then_inc(hsr_done, 1)
                elif kind == "hy":
                    from_work((kind, *step), tt[:, step[1], :])
                elif kind == "split":
                    unit = MIX_OUT[step[0]]
                    act.wait_ge(u_mm, 8)
                    act.wait_ge(*(evacuated[0, "bg"] if step[0] == 0 else (y_done, 2)))
                    nc.scalar.activation(yh[:, step[0], :, :], yT[:, 2 * unit:2 * unit + 2, :], ACT.Copy).then_inc(rhi_done, 1)

            for n, (p, what, during) in enumerate(MIXER):
                b = 2 * (n % 2)
                for k in range(KD):
                    if k == 3 and n:
                        hi(S_MIX + n + 1)
                    for step in during.get(k, ()):
                        mixer_step(*step)
                act.wait_ge(slot_used, S_MIX + n + 1)
                if what == "qk":
                    nc.scalar.activation(kS[:], ps[:, b + 1, :], ACT.Copy)
                    nc.scalar.activation(qS[:], ps[:, b, :], ACT.Copy, scale=ZSCALE).then_inc(pf_act, 1)
                elif what == "v":
                    nc.scalar.activation(vT[:], ps[:, b:b + 2, :], ACT.Copy).then_inc(pf_act, 1)
                elif what == "o":
                    nc.scalar.activation(sgo[:, 2 * p:2 * p + 2, :], ps[:, b:b + 2, :], ACT.Sigmoid).then_inc(pf_act, 1)
                elif what == "cg":
                    if p:
                        act.wait_ge(*evacuated[0, "hc"])
                    nc.scalar.activation(cgS[:], ps[:, b:b + 2, :], ACT.Copy).then_inc(pf_act, 1)
            act.wait_ge(y_done, 4)
            nc.scalar.activation(ah[:, 0:2, :], yT[:, 6:8, :], ACT.Copy).then_inc(rhi_done, 1)
            hi(S_MO + 1)
            act.wait_ge(*evacuated[1, "bg"])
            nc.scalar.activation(ah[:, 2:4, :], yT[:, 2:4, :], ACT.Copy).then_inc(rhi_done, 1)
            hi(S_MO + 2)
            hi(S_MO + 3)
            hi(S_MO + 4)
            post_norm(3, 1, S_F2I - 1)

            scaled_hi(2, 2, "norm_ffn2_pre")
            hi(S_F2I + 1)
            squares(4, lambda j, k: None)
            ffn(1, 4, S_F2I, S_F2O)
            post_norm(5, 2, S_ATT - 1)

            pre_norm(6, 3, 3, shift=True)
            hi(S_ATT + 1)
            act.wait_ge(att_init, 1)

            def att_step(step, r):
                kind, h = step[0], step[1] if len(step) > 1 else 0
                if kind == "Q":
                    i = step[2]
                    idx, n = 4 * h + i, (i + 1) * P
                    act.wait_ge(q_mm, r * 8 + (idx + 1))
                    act.wait_ge(w_done, r * 8 + max(idx - 1, 0))
                    nc.scalar.activation(g1[:, idx % 2, 0:n], ps[:, 4 + idx % 2, 0:n], ACT.Sigmoid, scale=-1.0)
                    nc.scalar.activation(be[:, idx % 2, 0:n], ps[:, 4 + idx % 2, 0:n], ACT.Sigmoid).then_inc(sig_done, 1)
                elif kind == "V":
                    act.wait_ge(v_mm, r + 1)
                    act.wait_ge(pv_mm, r * 2)
                    bank = ps[:, 6, :].rearrange("p (b d) -> p b d", d=P)
                    for e in range(2):
                        last = nc.scalar.activation(vph[:, e, :, DK * e:DK * e + DK], bank[:, :, DK * e:DK * e + DK], ACT.Copy)
                    last.then_inc(vhi_done, 1)
                elif kind == "T":
                    i = step[2]
                    idx = 4 * h + i
                    act.wait_ge(t_mm, r * 8 + (idx + 1))
                    act.wait_ge(pv_mm, r * 2 + h)
                    nc.scalar.activation(wTh[:, 0:i + 1, i * P:(i + 1) * P],
                                         ps[:, 6, 0:(i + 1) * P].rearrange("p (b t) -> p b t", t=P), ACT.Copy).then_inc(thi_done, 1)

            def att_out(r):
                act.wait_ge(ga_done, r + 1)
                nc.scalar.activation(gah[:, bass.ds(r, 1), :] if not isinstance(r, int) else gah[:, r:r + 1, :],
                                     ga[:].unsqueeze(1), ACT.Copy).then_inc(gah_done, 1)

            def att_slot(i, j):
                hi(S_ATT + j + 2, i)
                act.wait_ge(slot_used, i * 2 + (S_ATT + j + 1))
                if j == 0:
                    nc.scalar.activation(q2[:], ps[:, 0, :], ACT.Copy, scale=ZSCALE).then_inc(qe_done, 1)
                else:
                    nc.scalar.activation(v2[:], ps[:, 2, :], ACT.Copy).then_inc(ve_done, 1)
                    act.wait_ge(zs_done, i)
                    nc.scalar.activation(sz[:], ps[:, 3, :], ACT.Sigmoid).then_inc(sz_done, 1)

            att_slot(0, 0)
            att_slot(0, 1)
            with act.Fori(0, PAIRS - 1) as r:
                for j in range(2):
                    for s in range(8):
                        for step in ATT_STEPS.get(8 * j + s, []):
                            att_step(step, r)
                    if j == 1:
                        att_out(r)
                    att_slot(r + 1, j)

            def pool_slot(j):
                kind, g = POOL_ORDER[j]
                b = 2 * (j % 2)
                hi(S_POOL + j + 2)
                act.wait_ge(slot_used, S_POOL + j + 1)
                if kind == "u":
                    if g == 0:
                        act.wait_ge(w_done, 8 * PAIRS)
                    else:
                        act.wait_ge(d_done, g)
                    nc.scalar.activation(uS[:], ps[:, b:b + 2, :], ACT.Copy).then_inc(u_in, 1)
                else:
                    act.wait_ge(zb_done, g)
                    nc.scalar.activation(sb2[:], ps[:, b:b + 2, :], ACT.Sigmoid).then_inc(zsig, 1)

            def pool_hi(g):
                act.wait_ge(d_done, g + 1)
                source = p1 if g in (1, 3) else p2
                nc.scalar.activation(dh[:, 2 * g:2 * g + 2, :], source[:], ACT.Copy).then_inc(dhi_done, 1)

            for j in range(2):
                for s in range(8):
                    for step in ATT_STEPS.get(8 * j + s, []):
                        att_step(step, PAIRS - 1)
                if j == 1:
                    att_out(PAIRS - 1)
                    pool_hi(0)
                pool_slot(j)
            for j in range(2, 8):
                kind, g = POOL_ORDER[j - 1]
                if kind == "u":
                    pool_hi(g)
                pool_slot(j)
            for g in range(4):
                act.wait_ge(yb_t, g + 1)
                nc.scalar.activation(dh[:, 2 * g:2 * g + 2, :], (p1 if g % 2 == 0 else p2)[:], ACT.Copy).then_inc(ybh_done, 1)
            hi(S_FIN + 1)
            with act.Fori(0, 4) as c:
                for j in range(4):
                    n = S_FIN + j
                    act.wait_ge(raw_full[n % 2], c * 32 + landed[n + 2])
                    act.wait_ge(slot_used, c * 4 + (n + 1))
                    nc.scalar.activation(wh[n % 2][:], raw[n % 2][:], ACT.Copy).then_inc(hi_done, 1)
                    if j == 0:
                        act.wait_ge(m_done, c * 2)
                        nc.scalar.activation(sm[:], ps[:, 0:2, :], ACT.Sigmoid).then_inc(sm_done, 1)
                    elif j == 2:
                        act.wait_ge(ybl_done, 4)
                        act.wait_ge(m_done, c * 2)
                        nc.scalar.activation(sn[:], ps[:, 0:2, :], ACT.Sigmoid).then_inc(sm_done, 1)
            for j in range(4):
                act.wait_ge(mg_done, j + 1)
                nc.scalar.activation(ah[:, 2 * j:2 * j + 2, :], mg[:, 2 * j:2 * j + 2, :], ACT.Copy).then_inc(rhi_done, 1)
            for j in range(2):
                hi(S_OUT + j + 2)
            load_root(3)
            squares(7, lambda j, k: act.wait_ge(x_ready, 8 * 4 + j + 1))
            root(7)
            act.wait_ge(rstd_done, 8)
            for n in OUT_ACT:
                act.wait_ge(ot_mm, n + 1)
                k = OUT_ORDER[n]
                for b in range(TB):
                    last = nc.scalar.activation(outS[:, b, k * P:(k + 1) * P], ps[:, k, b * P:(b + 1) * P], ACT.Copy, scale=r4[:, b:b + 1])
                last.then_inc(ota_done, 1)

        @block.vector
        def _(dve):
            chain = Chain(dve, dve_self)

            def lo(n, i=0):
                dve.wait_ge(hi_done, i * 2 + (n + 1))
                nc.vector.tensor_tensor(wl[n % 2][:], raw[n % 2][:], wh[n % 2][:].bitcast(fp32), ALU.subtract).then_inc(lo_done, 1)

            def variance(stage, bank, spread=True):
                dve.wait_ge(sum_acc, 8 * stage + 8)
                chain.link(nc.vector.tensor_scalar(r4[:], ps[:, bank, 0:TB], 1.0 / D, EPS, ALU.mult, ALU.add))
                nc.vector.reciprocal(r4[:], r4[:]).then_inc(var_done, 1)
                dve.wait_ge(rstd_done, stage + 1)
                if spread:
                    nc.vector.tensor_tensor(diag[:], ident[:].unsqueeze(1).to_broadcast([P, TB, P]),
                                            r4[:].unsqueeze(2).to_broadcast([P, TB, P]), ALU.mult).then_inc(diag_done, 1)
                    dve.wait_ge(rb_done, stage + 1)

            def pre_norm(stage, pre, gain, shift=False):
                variance(stage, 4)

                def scaled(j):
                    if j >= 2:
                        dve.wait_ge(a_ready, 8 * pre + j - 1)
                    k = ORDER[j]
                    nc.vector.scalar_tensor_tensor(tt[:, j % 2, :], xT[:, k, :], gain(k), ps[:, 4, :], ALU.mult, ALU.mult).then_inc(t_done, 1)

                scaled(0)
                for j, k in enumerate(ORDER):
                    if j + 1 < KD:
                        scaled(j + 1)
                    dve.wait_ge(ah_done, 8 * pre + j + 1)
                    if shift:
                        nc.vector.scalar_tensor_tensor(al[:, k, :], tt[:, j % 2, :], mod[:, k:k + 1], ah[:, k, :].bitcast(fp32),
                                                       ALU.add, ALU.subtract).then_inc(a_ready, 1)
                    else:
                        nc.vector.tensor_tensor(al[:, k, :], tt[:, j % 2, :], ah[:, k, :].bitcast(fp32), ALU.subtract).then_inc(a_ready, 1)

            def scaled_lo(j, pre, gain):
                k = ORDER[j]
                dve.wait_ge(ah_done, 8 * pre + j + 1)
                nc.vector.scalar_tensor_tensor(al[:, k, :], xT[:, k, :], pcol(gain, k), ah[:, k, :].bitcast(fp32),
                                               ALU.mult, ALU.subtract).then_inc(a_ready, 1)

            def post_norm(stage, o, last, gain, factor, x_stage, after=None):
                dve.wait_ge(*whole(o, last, 0))
                nc.vector.tensor_copy(h7[:], ps[:, 7, :]).then_inc(h7_done, 1)
                variance(stage, 7)
                chain.link(nc.vector.tensor_copy(rstd[:], ps[:, 7, :]))

                def scaled(j):
                    if j >= 2:
                        dve.wait_ge(x_ready, 8 * x_stage + j - 1)
                    k = ORDER[j]
                    dve.wait_ge(*whole(o, last, j))
                    nc.vector.scalar_tensor_tensor(tt[:, j % 2, :], ps[:, k, :] if k < 7 else h7[:], pcol(gain, k), rstd[:],
                                                   ALU.mult, ALU.mult).then_inc(t_done, 1)

                scaled(0)
                for j, k in enumerate(ORDER):
                    if j + 1 < KD:
                        scaled(j + 1)
                    dve.wait_ge(t_done, 8 * T_OF[stage] + j + 1)
                    nc.vector.scalar_tensor_tensor(xT[:, k, :], tt[:, j % 2, :], factor, xT[:, k, :], ALU.mult, ALU.add).then_inc(x_ready, 1)
                    if after and j:
                        after(j - 1)
                if after:
                    after(KD - 1)

            def ffn(f, stage, base_in, base_out):
                r2 = rstd[:].unsqueeze(1).to_broadcast([P, 2, T])

                def unit(j, i=0):
                    dve.wait_ge(rhi_done, i * 2 + ((R_F1, R_F2)[f] + j + 1))
                    nc.vector.tensor_tensor(rl[:, j % 2, :, :], hid[:, bass.ds(i * 4 + 2 * j, 2), :],
                                            rh[:, j % 2, :, :].bitcast(fp32), ALU.subtract).then_inc(rlo_done, 1)

                def pair(i, units=()):
                    lo(base_in + 2, i)
                    if isinstance(i, int) and i == 0:
                        variance(stage, 4)
                        chain.link(nc.vector.tensor_copy(rstd[:], ps[:, 4, :]))
                    else:
                        dve.wait_ge(hid_ready, i + f * NFO)
                    dve.wait_ge(slot_used, i * 2 + (base_in + 1))
                    gate = ps[:, 6:8, :] if isinstance(i, int) and i == 0 else ps[:, 0:2, :]
                    nc.vector.tensor_tensor(gt[:], gate, r2, ALU.mult).then_inc(gt_done, 1)
                    for j in units:
                        unit(j)
                    dve.wait_ge(silu_done, i + (f * NFO + 1))
                    dve.wait_ge(slot_used, i * 2 + (base_in + 2))
                    nc.vector.tensor_tensor(gt[:], sg[:], ps[:, 2:4, :], ALU.mult).then_inc(ut_done, 1)
                    dve.wait_ge(ut_done, i + (f * NFO + 1))
                    nc.vector.tensor_tensor(hid[:, bass.ds(i * 2, 2), :], gt[:], r2, ALU.mult).then_inc(hid_ready, 1)
                    lo(base_in + 3, i)

                pair(0)
                with dve.Fori(1, NFO - 1) as i:
                    pair(i)
                pair(NFO - 1, (0, 1))
                with dve.Fori(0, 4) as i:
                    for j in range(2):
                        lo(base_out + j + 2, i)
                        unit(j + 2, i)
                lo(base_out + 10)
                unit(10)
                lo(base_out + 11)

            nc.vector.memset(gbias[:], 0.0).then_inc(par_cols, 1)
            for j, k in enumerate(ORDER):
                dve.wait_ge(xt_mm, j + 1)
                nc.vector.tensor_copy(xT[:, k, :], ps[:, j % 4, :]).then_inc(x_ready, 1)
            dve.wait_ge(xt_mm, KD + 1)
            nc.vector.tensor_copy(par[:, 0:n_par], ps[:, 7, 0:n_par]).then_inc(par_ready, 1)
            lo(0)
            dve.wait_ge(par_ready, 1)
            for j in range(KD):
                scaled_lo(j, 0, "norm_ffn1_pre")
            lo(1)
            ffn(0, 0, S_F1I, S_F1O)
            post_norm(1, 0, S_MIX - 1, "norm_ffn1_post", 0.5, 1)

            dve.wait_ge(gw_hi, 1)
            for q in range(4):
                cols = slice(32 * q, 32 * q + HEADS)
                last = nc.vector.tensor_tensor(gl[:, :, cols], gw[:, :, HEADS * q:HEADS * q + HEADS],
                                               gh[:, :, cols].bitcast(fp32), ALU.subtract)
            last.then_inc(gw_lo, 1)
            pre_norm(2, 1, lambda k: pcol("norm_mix_pre", k))
            lo(S_MIX + 1)

            def mixer_step(kind, *step):
                if kind == "gates":
                    dve.wait_ge(ada_mm, 1)
                    chain.link(nc.vector.tensor_tensor(mod[:], ps[:, 7, 0:24], par[:, col["b_ada_2"]:col["b_ada_2"] + 24], ALU.add))
                    chain.link(nc.vector.tensor_scalar(gmod[:], mod[:, 8:16], 1.0, None, ALU.add))
                    nc.vector.tensor_tensor(gmod[:], gmod[:], par[:, col["norm_gain_2"]:col["norm_gain_2"] + 8], ALU.mult).then_inc(mod_done, 1)
                elif kind == "rows":
                    dve.wait_ge(z_done, 1)
                    nc.vector.scalar_tensor_tensor(lrow, zrow, -1.0, zrow, ALU.mult, ALU.min).then_inc(abs_done, 1)
                    dve.wait_ge(ln_done, 1)
                    chain.link(nc.vector.scalar_tensor_tensor(frow, zrow[64:128, :], 0.0, lrow[64:128, :], ALU.min, ALU.subtract))
                    f, r = slice(0, 32), slice(32, 64)
                    zeros = zero1[0:32, :].to_broadcast([32, T])
                    zeros_r = zero1[32:64, :].to_broadcast([32, T])
                    nc.vector.tensor_tensor_scan(brow[f, :], frow[f, :], zeros, 0.0, ALU.add, ALU.add)
                    chain.link(nc.vector.tensor_tensor_scan(brow[r, ::-1], frow[r, ::-1], zeros_r, 0.0, ALU.add, ALU.add))
                    chain.link(nc.vector.tensor_tensor(crow, zrow[0:64, :], brow, ALU.subtract))
                    nc.vector.tensor_tensor_scan(mrow[f, :], crow[f, :], crow[f, :], NEG, ALU.max, ALU.max)
                    chain.link(nc.vector.tensor_tensor_scan(mrow[r, ::-1], crow[r, ::-1], crow[r, ::-1], NEG, ALU.max, ALU.max))
                    chain.link(nc.vector.scalar_tensor_tensor(erow[:], brow, -1.0, mrow[:], ALU.mult, ALU.subtract))
                    nc.vector.tensor_scalar(erow[:], erow[:], 88.0, None, ALU.min).then_inc(rows_done, 1)
                elif kind == "prep":
                    p, h, d = step
                    u = 4 * p + 2 * h + d
                    dve.wait_ge(wk_free, WORK["bc", p, 2 * h + d])
                    dve.wait_ge(E_done, u)
                    mask = (maskF, maskB)[d]
                    nc.vector.scalar_tensor_tensor(dg[:], Mb[:, 2 * h + d, :].rearrange("p (b t) -> p b t", t=P), -1.0,
                                                   mask[:].unsqueeze(1).to_broadcast([P, TB, P]), ALU.mult, ALU.add).then_inc(dg_done, 1)
                    dve.wait_ge(E_done, u + 1)
                    dve.wait_ge(wk_free, WORK["S", p, h, TB - 1])
                    for b in range(TB):
                        t0, t1 = span(d, b)
                        last = nc.vector.tensor_tensor(E[:, u % 2, b, t0:t1], E[:, u % 2, b, t0:t1], Sx[:, b, t0:t1], ALU.mult)
                    last.then_inc(p_ready, 1)
                elif kind == "mm":
                    p, h, d = step
                    u, row = 4 * p + 2 * h + d, 32 * d + 2 * p + h
                    dve.wait_ge(u_mm, u + 1)
                    den, numer = ps[:, 7, 0:TB], ps[:, 6, :].rearrange("p (b d) -> p b d", d=DV)
                    each = d4[:].unsqueeze(2).to_broadcast([P, TB, DV])
                    chain.link(nc.vector.tensor_tensor(d4[:], den, cT[:, 1, :, row], ALU.max))
                    chain.link(nc.vector.scalar_tensor_tensor(d4[:], den, -1.0, d4[:], ALU.mult, ALU.max))
                    chain.link(nc.vector.reciprocal(d4[:], d4[:]))
                    target = hs[:, h, :].rearrange("p (b d) -> p b d", d=DV)
                    if d == 0:
                        nc.vector.tensor_tensor(target, numer, each, ALU.mult).then_inc(h_done, 1)
                    else:
                        chain.link(nc.vector.tensor_tensor(dt_[:].rearrange("p (b d) -> p b d", d=DV), numer, each, ALU.mult))
                        nc.vector.tensor_tensor(hs[:, h, :], hs[:, h, :], dt_[:], ALU.add).then_inc(h_done, 1)
                    dve.wait_ge(h_done, u + 1)
                elif kind == "hn":
                    p, h = step
                    mean = h4[:, 2 * p + h, :]
                    chain.link(nc.vector.tensor_tensor(dt_[:], hs[:, h, :], hs[:, h, :], ALU.mult))
                    chain.link(nc.vector.tensor_reduce(mean, dt_[:].rearrange("p (b d) -> p b d", d=DV), AX.X, ALU.add))
                    chain.link(nc.vector.tensor_scalar(mean, mean, 1.0 / DV, EPS, ALU.mult, ALU.add))
                    nc.vector.reciprocal(mean, mean).then_inc(hr_done, 1)
                elif kind == "hy":
                    p, h = step
                    head = 2 * p + h
                    dve.wait_ge(hsr_done, head + 1)
                    target = hs[:, h, :].rearrange("p (b d) -> p b d", d=DV)
                    nc.vector.tensor_tensor(target, target, h4[:, head, :].unsqueeze(2).to_broadcast([P, TB, DV]), ALU.mult).then_inc(hn_done, 1)
                elif kind == "hz":
                    p, h = step
                    head = 2 * p + h
                    dve.wait_ge(wk_free, WORK["hy", p, h])
                    dve.wait_ge(*evacuated[p, "o"])
                    nc.vector.scalar_tensor_tensor(yT[:, 4 + head, :], tt[:, h, :], pcol("mlstm_norm", head), sgo[:, head, :],
                                                   ALU.mult, ALU.mult).then_inc(y_done, 1)
                elif kind == "split":
                    unit = MIX_OUT[step[0]]
                    dve.wait_ge(rhi_done, R_MO + step[0] + 1)
                    nc.vector.tensor_tensor(yl[:, step[0], :, :], yT[:, 2 * unit:2 * unit + 2, :], yh[:, step[0], :, :].bitcast(fp32),
                                            ALU.subtract).then_inc(rlo_done, 1)

            for n, (p, what, during) in enumerate(MIXER):
                b = 2 * (n % 2)
                for k in range(KD):
                    if k == 3 and n:
                        lo(S_MIX + n + 1)
                    for step in during.get(k, ()):
                        mixer_step(*step)
                if what == "hc":
                    dve.wait_ge(slot_used, S_MIX + n + 1)
                    dve.wait_ge(*evacuated[p, "cg"])
                    nc.vector.tensor_tensor(ux[:, :, 1:T + 1], cgS[:], ps[:, b:b + 2, :], ALU.mult).then_inc(pf_dve, 1)
                    dve.wait_ge(*evacuated[p, "hc"])
                    for tap in (1, 0, 2):
                        for c in range(2):
                            w = pcol("conv_w", 4 * tap + 2 * p + c)
                            if tap == 1:
                                last = nc.vector.tensor_scalar(ct[:, c, :], ux[:, c, 1:T + 1], w, pcol("conv_b", 2 * p + c), ALU.mult, ALU.add)
                            else:
                                last = nc.vector.scalar_tensor_tensor(ct[:, c, :], ux[:, c, tap:tap + T], w, ct[:, c, :], ALU.mult, ALU.add)
                        chain.link(last)
                elif what == "bg":
                    dve.wait_ge(slot_used, S_MIX + n + 1)
                    nc.vector.tensor_tensor(yT[:, 2 * p:2 * p + 2, :], ct[:], ps[:, b:b + 2, :], ALU.mult).then_inc(pf_dve, 1)
            for j in range(2):
                unit = MIX_OUT[2 + j]
                dve.wait_ge(rhi_done, R_MO + j + 3)
                nc.vector.tensor_tensor(al[:, 2 * j:2 * j + 2, :], yT[:, 2 * unit:2 * unit + 2, :], ah[:, 2 * j:2 * j + 2, :].bitcast(fp32),
                                        ALU.subtract).then_inc(rlo_done, 1)
                lo(S_MO + j + 1)
            lo(S_MO + 3)
            lo(S_MO + 4)

            post_norm(3, 1, S_F2I - 1, "norm_mix_post", 1.0, 2, after=lambda j: scaled_lo(j, 2, "norm_ffn2_pre"))
            lo(S_F2I + 1)
            ffn(1, 4, S_F2I, S_F2O)
            post_norm(5, 2, S_ATT - 1, "norm_ffn2_post", 0.5, 3)

            pre_norm(6, 3, lambda k: gmod[:, k:k + 1], shift=True)
            lo(S_ATT + 1)
            dve.wait_ge(att_init, 1)

            def att_step(step, r):
                kind, h = step[0], step[1] if len(step) > 1 else 0
                if kind == "Q":
                    i = step[2]
                    idx, n = 4 * h + i, (i + 1) * P
                    dve.wait_ge(sig_done, r * 8 + (idx + 1))
                    chain.link(nc.vector.tensor_tensor_scan(Gc[:, i, 0:n][:, ::-1], g1[:, idx % 2, 0:n][:, ::-1],
                                                            zero1[:].to_broadcast([P, n]), 1.0, ALU.mult, ALU.add))
                    dve.wait_ge(t_mm, r * 8 + max(idx - 3, 0))
                    nc.vector.tensor_tensor(Wt[:, idx % 4, 0:n], be[:, idx % 2, 0:n], Gc[:, i, 1:n + 1], ALU.mult).then_inc(w_done, 1)
                elif kind == "V":
                    dve.wait_ge(vhi_done, r + 1)
                    bank = ps[:, 6, :].rearrange("p (b d) -> p b d", d=P)
                    for e in range(2):
                        cols = slice(DK * e, DK * e + DK)
                        last = nc.vector.tensor_tensor(vpl[:, e, :, cols], bank[:, :, cols], vph[:, e, :, cols].bitcast(fp32), ALU.subtract)
                    last.then_inc(vlo_done, 1)
                elif kind == "T":
                    i = step[2]
                    idx = 4 * h + i
                    dve.wait_ge(thi_done, r * 8 + (idx + 1))
                    place = (slice(None), slice(0, i + 1), slice(i * P, (i + 1) * P))
                    nc.vector.tensor_tensor(wTl[place], ps[:, 6, 0:(i + 1) * P].rearrange("p (b t) -> p b t", t=P),
                                            wTh[place].bitcast(fp32), ALU.subtract).then_inc(tlo_done, 1)

            def att_out(r):
                one = slice(r, r + 1) if isinstance(r, int) else bass.ds(r, 1)
                dve.wait_ge(pv_mm, r * 2 + 2)
                dve.wait_ge(gah_done, r)
                nc.vector.tensor_tensor(ga[:], ps[:, 7, :], zs[:], ALU.mult).then_inc(ga_done, 1)
                dve.wait_ge(gah_done, r + 1)
                nc.vector.tensor_tensor(gal[:, one, :], ga[:].unsqueeze(1), gah[:, one, :].bitcast(fp32), ALU.subtract).then_inc(gal_done, 1)

            def att_slot(i, j):
                lo(S_ATT + j + 2, i)
                if j == 0:
                    dve.wait_ge(slot_used, i * 2 + (S_ATT + 1))
                    nc.vector.tensor_copy(k2[:], ps[:, 1, :]).then_inc(ke_done, 1)
                else:
                    dve.wait_ge(sz_done, i + 1)
                    nc.vector.tensor_tensor(zs[:], sz[:], ps[:, 3, :], ALU.mult).then_inc(zs_done, 1)

            att_slot(0, 0)
            att_slot(0, 1)
            with dve.Fori(0, PAIRS - 1) as r:
                chain.enter(r, 8)
                for j in range(2):
                    for s in range(8):
                        for step in ATT_STEPS.get(8 * j + s, []):
                            att_step(step, r)
                    if j == 1:
                        att_out(r)
                    att_slot(r + 1, j)
            chain.leave(PAIRS - 1)

            def pooled(g):
                dve.wait_ge(u_in, g + 1)
                if g:
                    dve.wait_ge(dlo_done, g)
                w = WINDOWS[g]
                source, target, reach = uS, p1, 1
                while reach < w:
                    nc.vector.tensor_copy(target[:, :, 0:reach], source[:, :, 0:reach])
                    chain.link(nc.vector.tensor_tensor(target[:, :, reach:T], source[:, :, reach:T], source[:, :, 0:T - reach], ALU.add))
                    source, target, reach = target, (p2 if target is p1 else p1), 2 * reach
                chain.link(nc.vector.tensor_tensor(target[:, :, 0:w], source[:, :, 0:w],
                                                   invc[:, g, 0:w].unsqueeze(1).to_broadcast([P, 2, w]), ALU.mult))
                nc.vector.tensor_tensor(target[:, :, 0:w], target[:, :, 0:w], uS[:, :, 0:w], ALU.subtract)
                nc.vector.scalar_tensor_tensor(target[:, :, w:T], source[:, :, w:T], 1.0 / w, uS[:, :, w:T],
                                               ALU.mult, ALU.subtract).then_inc(d_done, 1)
                dve.wait_ge(dhi_done, g + 1)
                nc.vector.tensor_tensor(dl[:, 2 * g:2 * g + 2, :], target[:], dh[:, 2 * g:2 * g + 2, :].bitcast(fp32),
                                        ALU.subtract).then_inc(dlo_done, 1)

            def pool_slot(j):
                kind, g = POOL_ORDER[j]
                lo(S_POOL + j + 2)
                if kind == "z":
                    dve.wait_ge(zsig, g + 1)
                    nc.vector.tensor_tensor(zb[:, 2 * g:2 * g + 2, :], sb2[:], ps[:, 2 * (j % 2):2 * (j % 2) + 2, :], ALU.mult).then_inc(zb_done, 1)

            for j in range(2):
                for s in range(8):
                    for step in ATT_STEPS.get(8 * j + s, []):
                        att_step(step, PAIRS - 1)
                if j == 1:
                    att_out(PAIRS - 1)
                    pooled(0)
                pool_slot(j)
            for j in range(2, 8):
                kind, g = POOL_ORDER[j - 1]
                if kind == "u":
                    pooled(g)
                pool_slot(j)
            for g in range(4):
                if g < 3:
                    dve.wait_ge(pw_mm, g + 1)
                else:
                    dve.wait_ge(slot_used, S_FIN)
                part = p1 if g % 2 == 0 else p2
                dve.wait_ge(dlo_done, 4)
                if g >= 2:
                    dve.wait_ge(ybl_done, g - 1)
                for c in range(2):
                    last = nc.vector.scalar_tensor_tensor(part[:, c, :], ps[:, 2 * (g % 2) + c, :], pcol("pool_scale_2", 2 * g + c),
                                                          zb[:, 2 * g + c, :], ALU.mult, ALU.mult)
                last.then_inc(yb_t, 1)
                dve.wait_ge(ybh_done, g + 1)
                nc.vector.tensor_tensor(dl[:, 2 * g:2 * g + 2, :], part[:], dh[:, 2 * g:2 * g + 2, :].bitcast(fp32),
                                        ALU.subtract).then_inc(ybl_done, 1)
            lo(S_FIN + 1)
            with dve.Fori(0, 4) as c:
                for j in range(4):
                    n = S_FIN + j
                    dve.wait_ge(hi_done, c * 4 + (n + 3))
                    nc.vector.tensor_tensor(wl[n % 2][:], raw[n % 2][:], wh[n % 2][:].bitcast(fp32), ALU.subtract).then_inc(lo_done, 1)
                    if j == 1:
                        dve.wait_ge(sm_done, c * 2 + 1)
                        dve.wait_ge(mg_done, c)
                        dve.wait_ge(slot_used, c * 4 + (n + 1))
                        nc.vector.tensor_tensor(m1[:], sm[:], ps[:, 2:4, :], ALU.mult).then_inc(m_done, 1)
                    elif j == 3:
                        dve.wait_ge(sm_done, c * 2 + 2)
                        dve.wait_ge(slot_used, c * 4 + (n + 1))
                        nc.vector.tensor_tensor(m2[:], sn[:], ps[:, 2:4, :], ALU.mult).then_inc(m_done, 1)
                        dve.wait_ge(m_done, c * 2 + 2)
                        nc.vector.tensor_tensor(mg[:, bass.ds(c * 2, 2), :], m1[:], m2[:], ALU.add).then_inc(mg_done, 1)
            for j in range(4):
                dve.wait_ge(rhi_done, R_OUT + j + 1)
                nc.vector.tensor_tensor(al[:, 2 * j:2 * j + 2, :], mg[:, 2 * j:2 * j + 2, :], ah[:, 2 * j:2 * j + 2, :].bitcast(fp32),
                                        ALU.subtract).then_inc(rlo_done, 1)
            for j in range(2):
                lo(S_OUT + j + 2)
            def gained(j):
                k = ORDER[j]
                dve.wait_ge(x_ready, 8 * 4 + j + 1)
                if j >= 3:
                    dve.wait_ge(ot_mm, j - 2)
                target = h7[:] if k == 7 else tt[:, j % 2, :]
                nc.vector.tensor_scalar(target, xT[:, k, :], pcol("final_gain_2", k), None, ALU.mult).then_inc(t_done, 1)

            for j, k in enumerate(ORDER):
                dve.wait_ge(*whole(3, S_END - 1, j))
                nc.vector.scalar_tensor_tensor(xT[:, k, :], ps[:, k, :], mod[:, 16 + k:17 + k], xT[:, k, :], ALU.mult, ALU.add).then_inc(x_ready, 1)
                if j:
                    gained(j - 1)
            gained(KD - 1)
            variance(7, 7, spread=False)
            for n in OUT_DVE:
                dve.wait_ge(ot_mm, n + 1)
                k = OUT_ORDER[n]
                nc.vector.tensor_tensor(outS[:, :, k * P:(k + 1) * P], ps[:, k, :].rearrange("p (b d) -> p b d", d=P),
                                        r4[:].unsqueeze(2).to_broadcast([P, TB, P]), ALU.mult).then_inc(otv_done, 1)

        @block.tensor
        def _(pe):
            def three(bank, w, m, start, stop):
                nc.tensor.matmul(bank, w[0], m[0], start=start, stop=False)
                nc.tensor.matmul(bank, w[0], m[1], start=False, stop=False)
                return nc.tensor.matmul(bank, w[1], m[0], start=False, stop=stop)

            def in_slot(n, i, banks, moving, steps=None, ready=None, each=2):
                pe.wait_ge(lo_done, i * each + (n + 1))
                for j, k in enumerate(ORDER):
                    if steps:
                        steps(j)
                    if ready is not None:
                        pe.wait_ge(a_ready, 8 * ready + j + 1)
                    for c in range(2):
                        at = slice(k * CB + c * P, k * CB + (c + 1) * P)
                        last = three(ps[:, banks + c, :], (wh[n % 2][:, at], wl[n % 2][:, at]),
                                     (moving[0][:, k, :], moving[1][:, k, :]), j == 0, j == KD - 1)
                last.then_inc(slot_used, 1)

            def out_slot(n, i, moving, ready, first=False, blocks=range(KD), before=None):
                pe.wait_ge(lo_done, i * 2 + (n + 1))
                pe.wait_ge(rlo_done, ready)
                for kk in range(2):
                    for c in blocks:
                        if kk == 0 and before:
                            before(c)
                        at = slice(kk * D + c * P, kk * D + (c + 1) * P)
                        end = three(ps[:, c, :], (wh[n % 2][:, at], wl[n % 2][:, at]), (moving[0][:, kk, :], moving[1][:, kk, :]),
                                    first and kk == 0, False)
                end.then_inc(slot_used, 1)

            def last_slot(n, moving, ready, o, stage, before=None, whole_bank=None):
                pe.wait_ge(lo_done, n + 1)
                pe.wait_ge(rlo_done, ready)
                for j, c in enumerate(ORDER):
                    for kk in range(2):
                        at = slice(kk * D + c * P, kk * D + (c + 1) * P)
                        end = three(ps[:, c, :], (wh[n % 2][:, at], wl[n % 2][:, at]), (moving[0][:, kk, :], moving[1][:, kk, :]),
                                    False, kk == 1)
                    end.then_inc(bank_done if j < 7 else slot_used, 1)
                    if j >= 2:
                        if j == 2:
                            before()
                        sum_of(stage, 7, j - 2)
                        if whole_bank:
                            whole_bank(j - 2)
                for j in (6, 7):
                    sum_of(stage, 7, j)
                    if whole_bank:
                        whole_bank(j)

            def sum_of(stage, bank, j):
                pe.wait_ge(sq_done, 8 * stage + j + 1)
                for b in range(TB):
                    last = nc.tensor.matmul(ps[:, bank, b:b + 1], sq[:, j % 2, b * P:(b + 1) * P], ones[:, 0:1],
                                            start=j == 0 and b == 0, stop=j == KD - 1 and b == TB - 1)
                last.then_inc(sum_acc, 1)

            def sums(stage, bank):
                for j in range(KD):
                    sum_of(stage, bank, j)

            def spread(stage, bank):
                pe.wait_ge(diag_done, stage + 1)
                nc.tensor.matmul(ps[:, bank, :], ones[:], diag[:].rearrange("p b t -> p (b t)"), start=True, stop=True).then_inc(rb_done, 1)

            def ffn(f, pre, stage, base_in, base_out, o):
                def pair(i):
                    first = isinstance(i, int) and i == 0
                    if not first:
                        pe.wait_ge(gt_done, i + f * NFO)
                        in_slot(base_in, i, 0, (ah, al))
                    else:
                        if f:
                            pe.wait_ge(t_done, 8 * T_OF[3] + 2)
                        in_slot(base_in, 0, 6, (ah, al), ready=pre)
                        sums(stage, 4)
                    if f or not first:
                        pe.wait_ge(ut_done, i + f * NFO)
                    in_slot(base_in + 1, i, 2, (ah, al), steps=(lambda j: spread(stage, 4) if j == 3 else None) if first else None)

                pair(0)
                with pe.Fori(1, NFO) as i:
                    pair(i)

                def unit(j, i=0, **more):
                    out_slot(base_out + j, i, (rh[:, j % 2, :, :], rl[:, j % 2, :, :]), i * 2 + ((R_F1, R_F2)[f] + j + 1), **more)

                def free(c):
                    if c == 0:
                        pe.wait_ge(gt_done, (f + 1) * NFO)
                    if c == 2:
                        pe.wait_ge(ut_done, (f + 1) * NFO)

                unit(0, first=True, blocks=[4, 5, 6, 7, 0, 1, 2, 3], before=free)
                with pe.Fori(0, 4) as i:
                    unit(1, i)
                    unit(2, i)
                unit(9)
                last_slot(base_out + 10, (rh[:, 0, :, :], rl[:, 0, :, :]), (R_F1, R_F2)[f] + 11, o, stage + 1,
                          lambda: pe.wait_ge(h7_done, o + 1))
                spread(stage + 1, 7)

            pe.wait_ge(const_done, 1)
            pe.wait_ge(x_in, 16 * TB)
            for j, k in enumerate(ORDER):
                if j >= 4:
                    pe.wait_ge(x_ready, j - 3)
                for b in range(TB):
                    last = nc.tensor.transpose(ps[:, j % 4, b * P:(b + 1) * P], xtok[:, b, k * P:(k + 1) * P], ident[:])
                last.then_inc(xt_mm, 1)
            pe.wait_ge(par_in, 16 * (len(vectors) + 5))
            nc.tensor.transpose(ps[:, 7, 0:n_par], par_rows[0:n_par, :], ident[0:n_par, 0:n_par]).then_inc(xt_mm, 1)
            ffn(0, 0, 0, S_F1I, S_F1O, 0)
            pe.wait_ge(t_done, 8 * T_OF[1] + 3)
            sums(2, 4)
            spread(2, 4)


            def use_work(*step):
                if WORK[step] > 2:
                    pe.wait_ge(wk_free, WORK[step] - 2)
                return ps[:, 4 + WORK[step] % 2, :]

            def mixer_step(kind, *step):
                if kind == "gates":
                    pe.wait_ge(gw_lo, 1)
                    for j, k in enumerate(ORDER):
                        pe.wait_ge(a_ready, 8 * 1 + j + 1)
                        last = three(ps[:, 6, :], (gh[:, k, :], gl[:, k, :]), (ah[:, k, :], al[:, k, :]), j == 0, j == KD - 1)
                    last.then_inc(gate_mm, 1)
                    pe.wait_ge(ada_step, 3 * KD)
                    for j in range(3 * KD):
                        last = nc.tensor.matmul(ps[:, 7, j:j + 1], ada[:, j * P:(j + 1) * P], ones[:, 0:1], start=True, stop=True)
                    last.then_inc(ada_mm, 1)
                elif kind == "cols":
                    pe.wait_ge(erow_done, 1)
                    bank = use_work(kind)
                    for w, source in enumerate((crow, erow)):
                        for b in range(TB):
                            at = (w * TB + b) * 64
                            last = nc.tensor.transpose(bank[:, at:at + 64], source[:, b * P:(b + 1) * P], ident[0:64, 0:64])
                    last.then_inc(wk_mm, 1)
                elif kind == "bc":
                    p, u = step
                    row = 32 * (u % 2) + 2 * p + u // 2
                    nc.tensor.matmul(use_work(kind, *step), ident[0:64, row:row + 1].to_broadcast([64, P]), mrow[:],
                                     start=True, stop=True).then_inc(wk_mm, 1)
                elif kind == "S":
                    p, h, b = step
                    pe.wait_ge(*evacuated[p, "qk"])
                    d = slice(DK * h, DK * h + DK)
                    nc.tensor.matmul(use_work(kind, *step), kS[d, b * P:(b + 1) * P], qS[d, :], start=True, stop=True).then_inc(wk_mm, 1)
                elif kind == "vt":
                    p, h = step
                    pe.wait_ge(*evacuated[p, "v"])
                    bank = use_work(kind, *step)
                    for b in range(TB):
                        last = nc.tensor.transpose(bank[:, b * P:(b + 1) * P], vT[:, h, b * P:(b + 1) * P], ident[:])
                    last.then_inc(wk_mm, 1)
                elif kind == "mm":
                    p, h, d = step
                    u = 4 * p + 2 * h + d
                    pe.wait_ge(p_ready, u + 1)
                    pe.wait_ge(wk_free, WORK["vt", p, h])
                    pe.wait_ge(mod_done, 1)
                    pe.wait_ge(h_done, u)
                    seen = [(t, b) for t in range(TB) for b in (range(t + 1) if d == 0 else range(t, TB))]
                    for sums_of in ("numerator", "denominator"):
                        for j, (t, b) in enumerate(seen):
                            if sums_of == "numerator":
                                target, moving = ps[:, 6, t * P:(t + 1) * P], vS[:, h, b, :]
                            else:
                                target, moving = ps[:, 7, t:t + 1], ones[:, 0:1]
                            last = nc.tensor.matmul(target, E[:, u % 2, b, t * P:(t + 1) * P], moving, start=j == 0, stop=j == len(seen) - 1)
                    last.then_inc(u_mm, 1)
                elif kind == "hy":
                    p, h = step
                    pe.wait_ge(hn_done, 2 * p + h + 1)
                    bank = use_work(kind, *step)
                    for b in range(TB):
                        last = nc.tensor.transpose(bank[:, b * P:(b + 1) * P], hs[:, h, b * P:(b + 1) * P], ident[:])
                    last.then_inc(wk_mm, 1)

            for n, (p, what, during) in enumerate(MIXER):
                if n >= 2:
                    pe.wait_ge(*evacuated[MIXER[n - 2][:2]])

                def steps(k):
                    for step in during.get(k, ()):
                        mixer_step(*step)
                in_slot(S_MIX + n, 0, 2 * (n % 2), (ah, al), steps=steps)

            def free(c):
                if c == 4:
                    pe.wait_ge(wk_free, len(WORK))
                    pe.wait_ge(h_done, 8)
                if c == 0:
                    pe.wait_ge(*evacuated[1, "hc"])
                if c == 2:
                    pe.wait_ge(*evacuated[1, "bg"])

            for j in range(3):
                moving = (yh[:, j, :, :], yl[:, j, :, :]) if j < 2 else (ah[:, 0:2, :], al[:, 0:2, :])
                out_slot(S_MO + j, 0, moving, R_MO + j + 1, first=j == 0, blocks=[4, 5, 6, 7, 0, 1, 2, 3], before=free if j == 0 else None)
            last_slot(S_F2I - 1, (ah[:, 2:4, :], al[:, 2:4, :]), R_MO + 4, 1, 3, lambda: pe.wait_ge(h7_done, 2))
            spread(3, 7)

            ffn(1, 2, 4, S_F2I, S_F2O, 2)

            pe.wait_ge(t_done, 8 * T_OF[5] + 3)
            sums(6, 4)
            spread(6, 4)

            def att_step(step, r):
                kind, h = step[0], step[1] if len(step) > 1 else 0
                if kind == "Q":
                    i = step[2]
                    idx, n = 4 * h + i, (i + 1) * P
                    if idx == 0:
                        pe.wait_ge(qe_done, r + 1)
                        pe.wait_ge(ke_done, r + 1)
                    pe.wait_ge(sig_done, r * 8 + max(idx - 1, 0))
                    bank, d = ps[:, 4 + idx % 2, :], slice(DK * h, DK * h + DK)
                    nc.tensor.matmul(bank[:, 0:n], q2[d, i * P:n], k2[d, 0:n], start=True, stop=False)
                    nc.tensor.matmul(bank[:, i * P:n], identb[:], maskS[:], start=False, stop=True).then_inc(q_mm, 1)
                elif kind == "V":
                    pe.wait_ge(ve_done, r + 1)
                    pe.wait_ge(tlo_done, r * 8)
                    for b in range(TB):
                        last = nc.tensor.transpose(ps[:, 6, b * P:(b + 1) * P], v2[:, b * P:(b + 1) * P], ident[:])
                    last.then_inc(v_mm, 1)
                elif kind == "T":
                    i = step[2]
                    idx = 4 * h + i
                    pe.wait_ge(w_done, r * 8 + (idx + 1))
                    if idx == 0:
                        pe.wait_ge(vlo_done, r + 1)
                    else:
                        pe.wait_ge(tlo_done, r * 8 + idx)
                    for b in range(i + 1):
                        last = nc.tensor.transpose(ps[:, 6, b * P:(b + 1) * P], Wt[:, idx % 4, b * P:(b + 1) * P], ident[:])
                    last.then_inc(t_mm, 1)
                elif kind == "PV":
                    pe.wait_ge(tlo_done, r * 8 + (4 * h + 4))
                    if h == 0:
                        pe.wait_ge(ga_done, r)
                    for b in range(TB):
                        last = three(ps[:, 7, b * P:T], (vph[:, h, b, :], vpl[:, h, b, :]), (wTh[:, b, b * P:T], wTl[:, b, b * P:T]),
                                     h == 0 and b == 0, h == 1 and b == TB - 1)
                    last.then_inc(pv_mm, 1)

            def steps_of(j, r):
                def steps(k):
                    for step in ATT_STEPS.get(8 * j + k, []):
                        att_step(step, r)
                return steps

            in_slot(S_ATT, 0, 0, (ah, al), ready=3)
            in_slot(S_ATT + 1, 0, 2, (ah, al))
            with pe.Fori(0, PAIRS - 1) as r:
                pe.wait_ge(qe_done, r + 1)
                pe.wait_ge(ke_done, r + 1)
                in_slot(S_ATT + 2, r, 0, (ah, al), steps=steps_of(0, r))
                pe.wait_ge(ve_done, r + 1)
                pe.wait_ge(zs_done, r + 1)
                in_slot(S_ATT + 3, r, 2, (ah, al), steps=steps_of(1, r))
            pool_read = {"u": u_in, "z": zb_done}
            for j in range(8):
                if j < 2:
                    for s in ((qe_done, ke_done), (ve_done, zs_done))[j]:
                        pe.wait_ge(s, PAIRS)
                else:
                    kind, g = POOL_ORDER[j - 2]
                    pe.wait_ge(pool_read[kind], g + 1)
                in_slot(S_POOL + j, 0, 2 * (j % 2), (ah, al), steps=steps_of(j, PAIRS - 1) if j < 2 else None)
            n = S_POOL + 8
            pe.wait_ge(lo_done, n + 1)
            for g in range(4):
                pe.wait_ge(dlo_done, g + 1)
                if g < 2:
                    pe.wait_ge(pool_read[POOL_ORDER[6 + g][0]], POOL_ORDER[6 + g][1] + 1)
                else:
                    pe.wait_ge(yb_t, g - 1)
                for c in range(2):
                    for k in range(2):
                        at = slice((2 * g + k) * CB + c * P, (2 * g + k) * CB + (c + 1) * P)
                        last = three(ps[:, 2 * (g % 2) + c, :], (wh[n % 2][:, at], wl[n % 2][:, at]),
                                     (dh[:, 2 * g + k, :], dl[:, 2 * g + k, :]), k == 0, k == 1)
                last.then_inc(pw_mm if g < 3 else slot_used, 1)

            with pe.Fori(0, 4) as c:
                for j, moving in enumerate(((ah, al), (gah, gal), (ah, al), (dh, dl))):
                    if j % 2 == 0:
                        pe.wait_ge(yb_t, 3)
                        pe.wait_ge(sm_done, c * 2 + j // 2)
                    else:
                        pe.wait_ge(yb_t, 4)
                        pe.wait_ge(m_done, c * 2 + j // 2)
                        pe.wait_ge(gal_done, PAIRS)
                    if j == 3:
                        pe.wait_ge(ybl_done, 4)
                    in_slot(S_FIN + j, c, 2 * (j % 2), moving, each=4)
            pe.wait_ge(m_done, 8)
            for j in range(3):
                out_slot(S_OUT + j, 0, (ah[:, 2 * j:2 * j + 2, :], al[:, 2 * j:2 * j + 2, :]), R_OUT + j + 1, first=j == 0)

            def turn(j):
                k = ORDER[j]
                pe.wait_ge(t_done, 8 * T_OF[7] + j + 1)
                for b in range(TB):
                    source = h7[:, b * P:(b + 1) * P] if k == 7 else tt[:, j % 2, b * P:(b + 1) * P]
                    last = nc.tensor.transpose(ps[:, k, b * P:(b + 1) * P], source, ident[:])
                last.then_inc(ot_mm, 1)

            last_slot(S_END - 1, (ah[:, 6:8, :], al[:, 6:8, :]), R_OUT + 4, 3, 7, lambda: None, lambda j: turn(j) if j else None)
            pe.wait_ge(var_done, 8)
            turn(0)


def kernel(**inputs):
    import numpy as np
    import concourse.bacc as bacc
    from concourse import mybir as m
    from concourse.bass_utils import run_bass_kernel_spmd as run

    nc = bacc.Bacc("TRN2", target_bir_lowering=False, num_devices=1)
    arrays, aps = {}, {}
    for name, value in inputs.items():
        value = np.ascontiguousarray(value)
        arrays["in_" + name] = value
        aps[name] = nc.dram_tensor("in_" + name, value.shape, m.dt.from_np(value.dtype), kind="ExternalInput").ap()
    out = nc.dram_tensor("out_0", (1, T, D), m.dt.float32, kind="ExternalOutput").ap()
    program(nc, aps, out)
    return run(nc, [arrays], core_ids=[0]).results[0]["out_0"]
```

```python
import concourse.bass as bass
from concourse import mybir
from contextlib import ExitStack

fp32 = mybir.dt.float32
f32r = mybir.dt.float32r
bf16 = mybir.dt.bfloat16
ALU = mybir.AluOpType
ACT = mybir.ActivationFunctionType
AX = mybir.AxisListType

P = 128
T = 512
TB = T // P
D = 1024
KD = D // P
FF = 2816
KF = FF // P
SLOT = 2048
CB = SLOT // KD
EPS = 1e-6
NEG = -1e30
ORDER = [7, 6, 4, 0, 1, 2, 3, 5]

HEADS = 4
DK = 64
DV = 128
CONV = 512
QO, KO, VO, OO, GO = 3 * CONV, 3 * CONV + 256, 3 * CONV + 512, 3 * CONV + 1024, 3 * CONV + 1536
PAIRS = 8
WINDOWS = (2, 4, 8, 16)
ZSCALE = 0.125

NFI = 2 * FF // CB
NFO = KF // 2
S_F1I = 0
S_F1O = S_F1I + NFI
S_MIX = S_F1O + NFO
S_MO = S_MIX + 12
S_F2I = S_MO + 4
S_F2O = S_F2I + NFI
S_ATT = S_F2O + NFO
S_POOL = S_ATT + 2 * PAIRS
S_FIN = S_POOL + 9
S_OUT = S_FIN + 16
S_END = S_OUT + 4
POOL_ORDER = [("u", 0), ("u", 1), ("z", 0), ("u", 2), ("z", 1), ("u", 3), ("z", 2), ("z", 3)]

MIXER = [(0, "qk", {0: [("gates",), ("ada", 0)], 1: [("ada", 1)], 2: [("ada", 2)], 3: [("ada", 3)], 4: [("ada", 4), ("sums",)],
                    5: [("ada", 5)], 6: [("ada", 6), ("spread",)], 7: [("ada", 7), ("rows", 0)]}),
         (0, "v", {3: [("rows", 1)]}),
         (0, "cg", {1: [("S", 0, 0, 0), ("S", 0, 0, 1)], 2: [("S", 0, 0, 2), ("S", 0, 0, 3), ("rows", 2)], 3: [("bc", 0, 0)],
                    4: [("bc", 0, 1)], 5: [("cols",), ("bc", 0, 2)], 6: [("bc", 0, 3), ("prep", 0, 0, 0)],
                    7: [("vt", 0, 0), ("vt", 0, 1), ("prep", 0, 0, 1), ("weigh", 0, 0, 0)]}),
         (0, "o", {0: [("weigh", 0, 0, 1)], 2: [("mm", 0, 0, 0), ("div", 0, 0, 0)], 3: [("S", 0, 1, 0)],
                   4: [("mm", 0, 0, 1), ("S", 0, 1, 1), ("div", 0, 0, 1)], 5: [("S", 0, 1, 2), ("prep", 0, 1, 0)], 6: [("S", 0, 1, 3)],
                   7: [("prep", 0, 1, 1), ("weigh", 0, 1, 0)]}),
         (1, "qk", {0: [("weigh", 0, 1, 1)], 2: [("mm", 0, 1, 0), ("div", 0, 1, 0)], 4: [("mm", 0, 1, 1), ("div", 0, 1, 1)],
                    5: [("bc", 1, 0), ("hn", 0, 0)], 6: [("bc", 1, 1), ("hn", 0, 1)], 7: [("bc", 1, 2)]}),
         (1, "v", {0: [("bc", 1, 3), ("hx", 0, 0), ("hx", 0, 1)], 5: [("S", 1, 0, 0), ("S", 1, 0, 1)],
                   6: [("S", 1, 0, 2), ("hy", 0, 0), ("prep", 1, 0, 0)],
                   7: [("S", 1, 0, 3), ("hy", 0, 1), ("prep", 1, 0, 1)]}),
         (0, "hc", {0: [("weigh", 1, 0, 0), ("weigh", 1, 0, 1)], 1: [("hz", 0, 0), ("hz", 0, 1)], 2: [("vt", 1, 0), ("vt", 1, 1)],
                    4: [("mm", 1, 0, 0), ("S", 1, 1, 0), ("div", 1, 0, 0)], 5: [("S", 1, 1, 1)], 6: [("mm", 1, 0, 1), ("S", 1, 1, 2), ("div", 1, 0, 1)],
                    7: [("S", 1, 1, 3), ("prep", 1, 1, 0)]}),
         (0, "bg", {0: [("prep", 1, 1, 1), ("weigh", 1, 1, 0)], 1: [("weigh", 1, 1, 1)], 3: [("mm", 1, 1, 0), ("div", 1, 1, 0)],
                    4: [("conv", 0)], 6: [("mm", 1, 1, 1), ("div", 1, 1, 1), ("hn", 1, 0)], 7: [("hn", 1, 1)]}),
         (1, "o", {2: [("hx", 1, 0), ("hx", 1, 1)], 6: [("hy", 1, 0)], 7: [("hy", 1, 1)]}),
         (1, "cg", {0: [("hz", 1, 0)], 1: [("hz", 1, 1)], 2: [("split", 0)], 4: [("split", 1)]}),
         (1, "hc", {}),
         (1, "bg", {0: [("conv", 1)]})]
WORK = {}
for _, _, during in MIXER:
    for k in sorted(during):
        for step in during[k]:
            if step[0] in ("S", "cols", "bc", "vt", "hy"):
                WORK[step] = len(WORK) + 1
MIX_OUT = (0, 2, 3, 1)
MIX_READ = {entry[:2]: n + 1 for n, entry in enumerate(MIXER)}

ATT_STEPS = {0: [("Q", 0, 0)], 1: [("V",), ("Q", 0, 1)], 2: [("Q", 0, 2)], 3: [("Q", 0, 3)],
             4: [("T", 0, 0), ("Q", 1, 0)], 5: [("T", 0, 1), ("Q", 1, 1)], 6: [("T", 0, 2), ("Q", 1, 2)],
             7: [("T", 0, 3), ("Q", 1, 3)], 8: [("PV", 0)], 10: [("T", 1, 0), ("sum", 0)], 12: [("T", 1, 1)], 13: [("T", 1, 2)],
             14: [("T", 1, 3)], 15: [("PV", 1)]}
ATT_SPLIT = (1, 0)


class Chain:

    def __init__(self, engine, sem):
        self.engine, self.sem, self.base, self.n, self.i, self.per = engine, sem, 0, 0, None, 0

    def enter(self, i, per, start=0):
        self.base, self.n, self.i, self.per = self.base + self.n - start * per, 0, i, per

    def leave(self, end):
        assert self.n == self.per, self.n
        self.base, self.n, self.i = self.base + end * self.per, 0, None

    def link(self, instruction):
        self.n += 1
        at = self.base + self.n
        if self.i is not None:
            at = self.i * self.per + at
        instruction.then_inc(self.sem, 1)
        self.engine.wait_ge(self.sem, at)


def program(nc, a, out):
    with ExitStack() as ctx:
        keep = ctx

        def sb(name, shape, dt=fp32, where=None):
            return (where or keep).enter_context(nc.sbuf_tensor(name, shape, dt))

        def sem(name):
            return ctx.enter_context(nc.semaphore(name))

        xT = sb("xT", [P, KD, T])
        ah = sb("ah", [P, KD, T], f32r)
        al = sb("al", [P, KD, T], f32r)
        raw = [sb(f"raw{i}", [P, SLOT]) for i in range(2)]
        wh = [sb(f"wh{i}", [P, SLOT], f32r) for i in range(2)]
        wl = [sb(f"wl{i}", [P, SLOT], f32r) for i in range(2)]
        sq = sb("sq", [P, 2, T])
        rstd = sb("rstd", [P, T])
        r4 = sb("r4", [P, TB])
        acc = sb("acc", [P, T])
        scrap = sb("scrap", [P, 4])
        tt = sb("tt", [P, 2, T])
        ident = sb("ident", [P, P])
        ones = sb("ones", [P, P])
        maskF = sb("maskF", [P, P])
        maskB = sb("maskB", [P, P])
        identb = sb("identb", [P, P], bf16)
        maskS = sb("maskS", [P, P], bf16)
        zero1 = sb("zero1", [P, 1])
        par_rows = sb("par_rows", [P, P])
        par = sb("par", [P, P])
        gbias = sb("gbias", [P, 1])
        gw = sb("gw", [P, KD, 16])
        sc = sb("sc", [P, KD])
        mod = sb("mod", [P, 24])
        gmod = sb("gmod", [P, KD])
        cT = sb("cT", [P, 2, TB, 64])
        d4 = sb("d4", [P, 2, TB // 2])
        h4 = sb("h4", [P, HEADS, TB])
        invc = sb("invc", [P, 4, 16])
        h7 = sb("h7", [P, T])

        with ExitStack() as phase:
            hid = sb("hid", [P, KF, T], where=phase)
            sg = sb("sg", [P, 2, T], where=phase)
            gt = sb("gt", [P, 2, T], where=phase)
            rh = sb("rh", [P, 2, 2, T], f32r, where=phase)
            rl = sb("rl", [P, 2, 2, T], f32r, where=phase)
            ada_raw = sb("ada_raw", [P, KD, P], where=phase)
            ada = sb("ada", [P, 3 * D], where=phase)
        with ExitStack() as phase:
            xtok = sb("xtok", [P, TB, D], where=phase)
        with ExitStack() as phase:
            outS = sb("outS", [P, TB, D], where=phase)
        with ExitStack() as phase:
            with ExitStack() as inner:
                gh = sb("gh", [P, KD, P], f32r, where=inner)
                gl = sb("gl", [P, KD, P], f32r, where=inner)
            with ExitStack() as inner:
                yh = sb("yh", [P, 2, 2, T], f32r, where=inner)
                yl = sb("yl", [P, 2, 2, T], f32r, where=inner)
            E = sb("E", [P, 2, TB, T], where=phase)
            Sx = sb("Sx", [P, TB, T], where=phase)
            Mb = sb("Mb", [P, 4, T], where=phase)
            mrow = sb("mrow", [64, T], where=phase)
            erow = sb("erow", [64, T], where=phase)
            vT = sb("vT", [P, 2, T], where=phase)
            vS = sb("vS", [P, 2, TB, P + 1], where=phase)
            qS = sb("qS", [P, T], where=phase)
            kS = sb("kS", [P, T], where=phase)
            ql = sb("ql", [P, T], f32r, where=phase)
            cgS = sb("cgS", [P, 2, T], where=phase)
            ux = sb("ux", [P, 2, T + 2], where=phase)
            ct = sb("ct", [P, 2, T], where=phase)
            sgo = sb("sgo", [P, HEADS, T], where=phase)
            hs = sb("hs", [P, 2, T], where=phase)
            yA = sb("yA", [P, 4, T], where=phase)
            with ExitStack() as inner:
                k2m = sb("k2m", [P, 2, T], f32r, where=inner)
                q2m = sb("q2m", [P, 2, T], f32r, where=inner)
            yB = sb("yB", [P, 4, T], where=phase)
        dt_, dg = h7, acc[:].rearrange("p (b t) -> p b t", t=P)
        y_unit = yA[:, 0:2, :], yB[:, 0:2, :], yA[:, 2:4, :], yB[:, 2:4, :]
        rsq = sq[:, 0, :]
        zrow, lrow = E[:, 0, 0, :], E[:, 0, 1, :]
        frow, brow, crow = E[0:64, 0, 2, :], E[0:64, 0, 3, :], E[0:64, 1, 0, :]
        with ExitStack() as phase:
            gah = sb("gah", [P, KD, T], f32r, where=phase)
            gal = sb("gal", [P, KD, T], f32r, where=phase)
            with ExitStack() as inner:
                wTh = sb("wTh", [P, TB, T], f32r, where=inner)
                wTl = sb("wTl", [P, TB, T], f32r, where=inner)
                Gc = sb("Gc", [P, P * TB * (TB + 1) // 2 + TB], where=inner)
                Wt = sb("Wt", [P, P * TB * (TB + 1) // 2], where=inner)
                vph = sb("vph", [P, 2, TB, P], f32r, where=inner)
                vp = sb("vp", [P, 2, TB, P], f32r, where=inner)
                zs = sb("zs", [P, T], where=inner)
                ga = sb("ga", [P, T], where=inner)
                be = sb("be", [P, 2, T], where=inner)
                g1 = sb("g1", [P, 2, T], where=inner)
                q2 = sb("q2", [P, 2, T], f32r, where=inner)
                k2 = sb("k2", [P, 2, T], f32r, where=inner)
                kl = sb("kl", [P, T], f32r, where=inner)
                v2 = sb("v2", [P, T], where=inner)
            dh = sb("dh", [P, KD, T], f32r, where=phase)
            dl = sb("dl", [P, KD, T], f32r, where=phase)
            with ExitStack() as inner:
                zb = sb("zb", [P, KD, T], where=inner)
                uS = sb("uS", [P, 2, T], where=inner)
                p1 = sb("p1", [P, 2, T], where=inner)
            mg = sb("mg", [P, KD, T], where=phase)
            sm = sb("sm", [P, 2, T], where=phase)
            sn = sb("sn", [P, 2, T], where=phase)
        sb2, m1, p2, m2, sz = tt, tt, sq, sq, h7
        pvl = acc
        ps = ctx.enter_context(nc.psum_tensor("ps", [P, 8, T], fp32))

        raw_full = [sem(f"raw_full{i}") for i in range(2)]
        hi_done, lo_done = sem("hi_done"), sem("lo_done")
        raw_first, hi_first, lo_first = sem("raw_first"), sem("hi_first"), sem("lo_first")
        slot_used = sem("slot_used")
        x_in, par_in = [sem(f"x_in{b}") for b in range(TB)], sem("par_in")
        gates_in = sem("gates_in")
        const_done, par_cols, par_ready = sem("const_done"), sem("par_cols"), sem("par_ready")
        xt_mm = sem("xt_mm")
        x_ready = sem("x_ready")
        x_act = sem("x_act")
        x_odd = sem("x_odd")
        sq_done, acc_step, sum_done = sem("sq_done"), sem("acc_step"), sem("sum_done")
        var_done, rstd_done, rb_done = sem("var_done"), sem("rstd_done"), sem("rb_done")
        bank_done = sem("bank_done")
        gt_done, ut_done = sem("gt_done"), sem("ut_done")
        t_done, ah_done, a_ready = sem("t_done"), sem("ah_done"), sem("a_ready")
        silu_done, hid_ready = sem("silu_done"), sem("hid_ready")
        rhi_done, rlo_done = sem("rhi_done"), sem("rlo_done")
        h7_done = sem("h7_done")
        sc_done, ada_in, ada_step, ada_mm, mod_done = sem("sc_done"), sem("ada_in"), sem("ada_step"), sem("ada_mm"), sem("mod_done")
        act_self, dve_self, pool_self = sem("act_self"), sem("dve_self"), sem("pool_self")
        gpad, gw_hi, gw_lo, gate_mm = sem("gpad"), sem("gw_hi"), sem("gw_lo"), sem("gate_mm")
        edges = sem("edges")
        z_done, abs_done, ln_done, rows_done, erow_done = sem("z_done"), sem("abs_done"), sem("ln_done"), sem("rows_done"), sem("erow_done")
        wk_mm, wk_free = sem("wk_mm"), sem("wk_free")
        pf_done, so_done = sem("pf_done"), sem("so_done")
        zr_done, qk_hi, qk_lo = sem("zr_done"), sem("qk_hi"), sem("qk_lo")
        dg_done, E_done, p_ready = sem("dg_done"), sem("E_done"), sem("p_ready")
        u_mm, h_done, hr_done, hsr_done, hn_done = sem("u_mm"), sem("h_done"), sem("hr_done"), sem("hsr_done"), sem("hn_done")
        y_done = sem("y_done")
        att_init = sem("att_init")
        vp_done = sem("vp_done")
        pv_low, pv_sum = sem("pv_low"), sem("pv_sum")
        q_mm, sig_done, w_done, t_mm, thi_done, tlo_done = sem("q_mm"), sem("sig_done"), sem("w_done"), sem("t_mm"), sem("thi_done"), sem("tlo_done")
        v_mm, vhi_done, vlo_done, pv_mm, ga_done, gah_done, gal_done = sem("v_mm"), sem("vhi_done"), sem("vlo_done"), sem("pv_mm"), sem("ga_done"), sem("gah_done"), sem("gal_done")
        qe_done, ke_done, ve_done, sz_done, zs_done = sem("qe_done"), sem("ke_done"), sem("ve_done"), sem("sz_done"), sem("zs_done")
        u_in, zsig, zb_done, d_done, dhi_done, dlo_done = sem("u_in"), sem("zsig"), sem("zb_done"), sem("d_done"), sem("dhi_done"), sem("dlo_done")
        pw_mm, yb_t, ybh_done, ybl_done = sem("pw_mm"), sem("yb_t"), sem("ybh_done"), sem("ybl_done")
        sm_done, m_done, mg_done = sem("sm_done"), sem("m_done"), sem("mg_done")
        ot_mm, ota_done, otv_done, out_done = sem("ot_mm"), sem("ota_done"), sem("otv_done"), sem("out_done")

        vectors = [("norm_ffn1_pre", 8), ("norm_ffn1_post", 8), ("norm_mix_pre", 8), ("norm_mix_post", 8),
                   ("norm_ffn2_pre", 8), ("norm_ffn2_post", 8), ("norm_gain_2", 8), ("final_gain_2", 8),
                   ("c_2", 8), ("b_ada_2", 24), ("pool_scale_2", 8), ("conv_w", 12), ("conv_b", 4), ("mlstm_norm", 4)]
        col, n_par = {}, 0
        for name, rows in vectors:
            col[name] = n_par
            n_par += rows

        def pcol(name, k):
            return par[:, col[name] + k:col[name] + k + 1]

        def load_vectors(engine, names, loaded):
            for name, rows in names:
                at = col[name]
                engine.dma_start(par_rows[at:at + rows, :], flat(a[name]).rearrange("(r p) -> r p", p=P)).then_inc(loaded, 16)

        def flat(ap):
            n = len(ap.shape)
            letters = " ".join("abc"[:n])
            return ap if n == 1 else ap.rearrange(f"{letters} -> ({letters})")

        def wview(name):
            w = a[name]
            w = w.rearrange("o r c -> (o r) c") if len(w.shape) == 3 else w
            return w.rearrange("(k p) c -> p k c", p=P)

        W1I, W1O = wview("w_ffn1_in"), wview("w_ffn1_out")
        W2I, W2O = wview("w_ffn2_in"), wview("w_ffn2_out")
        WMI, WMO = wview("w_mix_in"), wview("w_mix_out")
        WHI, WHO = wview("w_in_2"), wview("w_out_2")
        WBA, WBB = wview("w_branch_a_2"), wview("w_branch_b_2")
        WAD = wview("w_ada_2")
        PWV = a["pool_w_2"].rearrange("o g (k p) c -> p (o g k) c", p=P)

        evacuated = {slot: (pf_done, n) for slot, n in MIX_READ.items()}

        R_F1, R_MO, R_F2, R_OUT = 0, NFO, NFO + 4, 2 * NFO + 4

        def whole(o, last, j):
            return (bank_done, 7 * o + j + 1) if j < 7 else (slot_used, last + 1)

        X_DVE = 5
        FIRST, OTHER = slice(SLOT // 2, SLOT), slice(0, SLOT // 2)
        XB = {0: 0, 1: X_DVE, 2: X_DVE + 8, 3: X_DVE + 16, 4: X_DVE + 20}

        ACC = {stage: 6 * stage - 3 * (stage > 6) for stage in range(8)}

        T_OF = {1: 0, 3: 1, 5: 2, 6: 3, 7: 4}
        OUT_ORDER = ORDER[1:] + ORDER[:1]
        OUT_ACT, OUT_DVE = [4, 1, 7], [2, 3, 5, 0, 6]

        def span(direction, b):
            return (b * P, T) if direction == 0 else (0, (b + 1) * P)

        def gc_at(i):
            return i * (i + 1) // 2 * P + i

        def wt_of(i):
            return Wt[:, i * (i + 1) // 2 * P:(i + 1) * (i + 2) // 2 * P]

        HALF = slice(0, DK), slice(DK, 2 * DK)

        def sq6(j):
            return hid[:, j, :]

        block = ctx.enter_context(nc.Block())

        @block.sync
        def _(sp):
            for b in range(TB):
                sp.dma_start(xtok[:, b, :], a["x"][0, b * P:(b + 1) * P, :]).then_inc(x_in[b], 16)

            load_vectors(sp, vectors[9:], par_in)

            def load(n, source):
                w = raw[n % 2][:, :].rearrange("p (k c) -> p k c", k=source.shape[1])
                sp.dma_start(w, source).then_inc(raw_full[n % 2], 16)

            def load_two(n, left, right):
                w = raw[n % 2][:, :].rearrange("p (k c) -> p k c", k=KD)
                sp.dma_start(w[:, :, 0:P], left).then_inc(raw_full[n % 2], 16)
                sp.dma_start(w[:, :, P:2 * P], right).then_inc(raw_full[n % 2], 16)

            def ffn(base_in, w_in, base_out, w_out):
                if base_in:
                    sp.wait_ge(lo_done, base_in - 1)
                    load(base_in, w_in[:, :, 0:CB])
                else:
                    w = raw[0][:, :].rearrange("p (k c) -> p k c", k=KD)
                    sp.dma_start(w[:, KD // 2:KD, :], w_in[:, KD // 2:KD, 0:CB]).then_inc(raw_first, 16)
                    sp.dma_start(w[:, 0:KD // 2, :], w_in[:, 0:KD // 2, 0:CB]).then_inc(raw_full[0], 16)
                if base_in:
                    sp.wait_ge(lo_done, base_in)
                load(base_in + 1, w_in[:, :, FF:FF + CB])
                with sp.Fori(1, NFI // 2) as i:
                    gate, up = sp.snap(i * CB), sp.snap(i * CB + FF)
                    sp.wait_ge(lo_done, i * 2 + (base_in - 1))
                    load(base_in, w_in[:, :, bass.ds(gate, CB)])
                    sp.wait_ge(lo_done, i * 2 + base_in)
                    load(base_in + 1, w_in[:, :, bass.ds(up, CB)])
                with sp.Fori(0, NFO // 2) as i:
                    chunk = [sp.snap(i * 4), sp.snap(i * 4 + 2)]
                    for j in range(2):
                        sp.wait_ge(lo_done, i * 2 + (base_out + j - 1))
                        load(base_out + j, w_out[:, bass.ds(chunk[j], 2), :])
                sp.wait_ge(lo_done, base_out + NFO - 2)
                load(base_out + NFO - 1, w_out[:, 2 * (NFO - 1):2 * NFO, :])

            ffn(S_F1I, W1I, S_F1O, W1O)
            for j, (p, kind, _) in enumerate(MIXER):
                n = S_MIX + j
                sp.wait_ge(lo_done, n - 1)
                if kind == "qk":
                    load_two(n, WMI[:, :, QO + P * p:QO + P * p + P], WMI[:, :, KO + P * p:KO + P * p + P])
                else:
                    c0 = {"v": VO, "o": OO, "cg": CONV, "hc": 2 * CONV, "bg": 0}[kind] + CB * p
                    load(n, WMI[:, :, c0:c0 + CB])
            for j in range(4):
                sp.wait_ge(lo_done, S_MO + j - 1)
                load(S_MO + j, WMO[:, 2 * MIX_OUT[j]:2 * MIX_OUT[j] + 2, :])
            ffn(S_F2I, W2I, S_F2O, W2O)
            with sp.Fori(0, PAIRS) as p:
                at = [sp.snap(p * P + m * D) for m in range(4)]
                for j in range(2):
                    sp.wait_ge(lo_done, p * 2 + (S_ATT + j - 1))
                    load_two(S_ATT + j, WHI[:, :, bass.ds(at[2 * j], P)], WHI[:, :, bass.ds(at[2 * j + 1], P)])
            for j, (kind, g) in enumerate(POOL_ORDER):
                sp.wait_ge(lo_done, S_POOL + j - 1)
                c0 = (4 if kind == "u" else 5) * D + g * CB
                if j < 2:
                    load_two(S_POOL + j, WHI[:, :, c0:c0 + P], WHI[:, :, c0 + P:c0 + CB])
                else:
                    load(S_POOL + j, WHI[:, :, c0:c0 + CB])
            sp.wait_ge(lo_done, S_POOL + 7)
            load(S_POOL + 8, PWV)
            with sp.Fori(1, 5) as c:
                at = [sp.snap(c * CB + (c0 - CB)) for c0 in (6 * D, 0, 7 * D, 0)]
                for j, w in enumerate((WHI, WBA, WHI, WBB)):
                    sp.wait_ge(lo_done, c * 4 + (S_FIN + j - 5))
                    load(S_FIN + j, w[:, :, bass.ds(at[j], CB)])
            for j in range(4):
                sp.wait_ge(lo_done, S_OUT + j - 1)
                load(S_OUT + j, WHO[:, 2 * j:2 * j + 2, :])
            view = out.rearrange("o (b p) c -> p (o b) c", p=P)
            half = slice(0, D // 2), slice(D // 2, D)
            for j, c in enumerate(half):
                for engine, done in ((OUT_ACT, ota_done), (OUT_DVE, otv_done)):
                    sp.wait_ge(done, len([n for n in engine if j or OUT_ORDER[n] < KD // 2]))
                sp.dma_start(view[:, :, c], outS[:, :, c]).then_inc(out_done, 16)
            sp.wait_ge(out_done, 16 * 2)

        double = {S_MIX + j for j, s in enumerate(MIXER) if s[1] == "qk"} | set(range(S_ATT, S_POOL + 2))
        landed = {}
        for n in range(S_END):
            landed[n] = landed.get(n - 2, 0) + 16 * (2 if n in double else 1)

        @block.gpsimd
        def _(pool):
            chain = Chain(pool, pool_self)
            nc.gpsimd.memset(zero1[:], 0.0)
            nc.gpsimd.memset(ones[:], 1.0)
            nc.gpsimd.memset(ident[:], 0.0)
            nc.gpsimd.memset(identb[:], 0.0)
            nc.gpsimd.memset(maskF[:], 0.0)
            nc.gpsimd.memset(maskB[:], 0.0)
            for w in range(4):
                for t in range(WINDOWS[w]):
                    nc.gpsimd.memset(invc[:, w, t:t + 1], 1.0 / (t + 1))
            chain.link(nc.gpsimd.memset(maskS[:], 0.0))
            for m in (ident, identb):
                nc.gpsimd.affine_select(out=m[:], in_=m[:], compare_op=ALU.not_equal, fill=1.0, base=0,
                                        pattern=[[-1, P]], channel_multiplier=1)
            nc.gpsimd.affine_select(out=maskF[:], in_=maskF[:], compare_op=ALU.is_ge, fill=NEG, base=0,
                                    pattern=[[1, P]], channel_multiplier=-1)
            nc.gpsimd.affine_select(out=maskB[:], in_=maskB[:], compare_op=ALU.is_ge, fill=NEG, base=0,
                                    pattern=[[-1, P]], channel_multiplier=1)
            nc.gpsimd.affine_select(out=maskS[:], in_=maskS[:], compare_op=ALU.is_ge, fill=NEG, base=-1,
                                    pattern=[[-1, P]], channel_multiplier=1).then_inc(const_done, 1)
            pool.dma_start(gw[:, :, :], WMI[:, :, GO:GO + 16]).then_inc(gates_in, 16)
            pool.wait_ge(par_cols, 1)
            for d in range(2):
                for at, name in ((32 * d, "gate_i_bias"), (64 + 32 * d, "gate_f_bias")):
                    pool.dma_start(gbias[at:at + HEADS, :],
                                   a[name][0:1, HEADS * d:HEADS * d + HEADS].rearrange("o h -> h o")).then_inc(gates_in, 16)

            def add_squares(stage):
                for j in range(1, 7):
                    pool.wait_ge(sq_done, 8 * stage + j + 1)
                    if j == 1 and stage:
                        pool.wait_ge(sum_done, stage)
                    if j > 1:
                        pool.wait_ge(acc_step, ACC[stage] + j - 1)
                    nc.gpsimd.tensor_tensor(acc[:], sq[:, 0, :] if j == 1 else acc[:], sq[:, j % 2, :], ALU.add).then_inc(acc_step, 1)

            def add_residual(stage, x_stage):
                for j, k in list(enumerate(ORDER))[1:]:
                    pool.wait_ge(t_done, 8 * T_OF[stage] + j + 1)
                    nc.gpsimd.tensor_tensor(xT[:, k, :], tt[:, j % 2, :], xT[:, k, :], ALU.add).then_inc(x_ready, 1)

            add_squares(0)
            pool.wait_ge(sc_done, 1)
            with pool.Fori(0, 3 * KD) as j:
                chain.enter(j, 3)
                pool.dma_start(ada_raw[:, :, :], WAD[:, :, bass.ds(j * P, P)]).then_inc(ada_in, 16)
                pool.wait_ge(ada_in, j * 16 + 16)
                chain.link(nc.gpsimd.tensor_tensor(ada_raw[:, :, :], ada_raw[:, :, :],
                                                   sc[:, :].unsqueeze(2).to_broadcast([P, KD, P]), ALU.mult))
                chain.link(nc.gpsimd.tensor_tensor(ada_raw[:, 0:4, :], ada_raw[:, 0:4, :], ada_raw[:, 4:8, :], ALU.add))
                chain.link(nc.gpsimd.tensor_tensor(ada_raw[:, 0:2, :], ada_raw[:, 0:2, :], ada_raw[:, 2:4, :], ALU.add))
                nc.gpsimd.tensor_tensor(ada[:, bass.ds(j * P, P)], ada_raw[:, 0, :], ada_raw[:, 1, :],
                                        ALU.add).then_inc(ada_step, 1)
                pool.wait_ge(ada_step, j + 1)
            chain.leave(3 * KD)

            pool.wait_ge(rlo_done, 2)
            nc.gpsimd.memset(gh[:].bitcast(fp32), 0.0)
            nc.gpsimd.memset(gl[:].bitcast(fp32), 0.0).then_inc(gpad, 1)
            add_residual(1, 1)
            pool.wait_ge(slot_used, S_MIX)
            nc.gpsimd.memset(vS[:, :, :, P:P + 1], 1.0)
            nc.gpsimd.memset(ux[:, :, 0:1], 0.0)
            nc.gpsimd.memset(ux[:, :, T + 1:T + 2], 0.0).then_inc(edges, 1)
            add_squares(2)
            add_residual(3, 2)

            pool.wait_ge(slot_used, S_ATT)
            nc.gpsimd.memset(vph[:].bitcast(fp32), 0.0)
            for i in range(TB):
                last = nc.gpsimd.memset(Gc[:, gc_at(i + 1) - 1:gc_at(i + 1)], 1.0)
            last.then_inc(att_init, 1)

            for j in range(1, KD, 2):
                k = ORDER[j]
                pool.wait_ge(t_done, 8 * T_OF[5] + j + 1)
                nc.gpsimd.tensor_tensor(xT[:, k, :], tt[:, j % 2, :], xT[:, k, :], ALU.add).then_inc(x_odd, 1)

            def lo(n, i=0):
                pool.wait_ge(hi_done, i * 2 + (n + 1))
                pool.wait_ge(lo_done, i * 2 + n)
                nc.gpsimd.tensor_tensor(wl[n % 2][:], raw[n % 2][:], wh[n % 2][:].bitcast(fp32), ALU.subtract).then_inc(lo_done, 1)

            with pool.Fori(0, PAIRS) as i:
                lo(S_ATT + 2, i)
                lo(S_ATT + 3, i)
                pool.wait_ge(vhi_done, i + 1)
                for e in range(2):
                    own = vph[:, e, :, HALF[e]].bitcast(fp32)
                    one = ones[:, 0:DK].unsqueeze(1).to_broadcast([P, TB, DK])
                    last = nc.gpsimd.tensor_tensor(vp[:, e, :, HALF[e]], own, one, ALU.mult)
                last.then_inc(vp_done, 1)
            lo(S_POOL + 2)
            add_squares(7)

        @block.scalar
        def _(act):
            chain = Chain(act, act_self)

            load_vectors(act, vectors[:9], par_in)

            def hi(n, i=0):
                step = landed[n] - landed[n - 2] if n >= 2 else 16
                act.wait_ge(raw_full[n % 2], i * step + landed[n])
                if n >= 2:
                    act.wait_ge(slot_used, i * 2 + (n - 1))
                nc.scalar.activation(wh[n % 2][:], raw[n % 2][:], ACT.Copy).then_inc(hi_done, 1)

            def squares(stage, ready, banks=False):
                for j, k in enumerate(ORDER):
                    ready(j, k)
                    if stage == 6:
                        target = sq6(j)
                    elif j >= 2:
                        act.wait_ge(acc_step, ACC[stage] + max(1, j - 2))
                    elif stage:
                        act.wait_ge(*((acc_step, ACC[stage]) if j == 0 else (sum_done, stage)))
                    if stage != 6:
                        target = sq[:, j % 2, :]
                    source = xT[:, k, :] if not banks else ps[:, k, :] if k < 7 else h7[:]
                    nc.scalar.activation(target, source, ACT.Square).then_inc(sq_done, 1)

            def root(stage):
                act.wait_ge(var_done, stage + 1)
                nc.scalar.activation(r4[:], r4[:], ACT.Sqrt).then_inc(rstd_done, 1)

            def load_root(n):
                nc.scalar.activation(scrap[:, n:n + 1], zero1[:], ACT.Sqrt)

            def pre_norm(stage, pre, x_stage, shift=False):
                squares(stage, lambda j, k: act.wait_ge(*((x_ready, XB[x_stage] + j // 2 + 1) if j % 2 == 0 else (x_odd, j // 2 + 1))))
                root(stage)
                for j, k in enumerate(ORDER):
                    act.wait_ge(t_done, 8 * T_OF[stage] + j + 1)
                    if shift:
                        nc.scalar.activation(ah[:, k, :], tt[:, j % 2, :], ACT.Identity, bias=mod[:, k:k + 1]).then_inc(ah_done, 1)
                    else:
                        nc.scalar.activation(ah[:, k, :], tt[:, j % 2, :], ACT.Copy).then_inc(ah_done, 1)

            def scaled_hi(pre, x_stage, gain, between=None):
                for j, k in enumerate(ORDER):
                    if between and j == 3:
                        between()
                    act.wait_ge(x_ready, XB[x_stage] + (j + 1 if x_stage else min(j + 1, X_DVE)))
                    nc.scalar.activation(ah[:, k, :], xT[:, k, :], ACT.Copy, scale=pcol(gain, k)).then_inc(ah_done, 1)

            def post_norm(stage, o, last):
                load_root(o)

                def ready(j, k):
                    if k == 7:
                        act.wait_ge(h7_done, o + 1)
                    else:
                        act.wait_ge(*whole(o, last, j))
                squares(stage, ready, banks=True)
                root(stage)

            def ffn(f, stage, base_in, base_out):
                def unit(j, i=0):
                    act.wait_ge(hid_ready, i * 2 + (f * NFO + j + 1))
                    if j >= 2:
                        act.wait_ge(slot_used, i * 2 + (base_out + j - 1))
                    nc.scalar.activation(rh[:, j % 2, :, :], hid[:, bass.ds(i * 4 + 2 * j, 2), :], ACT.Copy).then_inc(rhi_done, 1)

                def pair(i, units=()):
                    hi(base_in + 2, i)
                    if isinstance(i, int) and i == 0:
                        root(stage)
                    for j in units:
                        unit(j)
                    act.wait_ge(gt_done, i + (f * NFO + 1))
                    nc.scalar.activation(sg[:], gt[:], ACT.Silu).then_inc(silu_done, 1)
                    hi(base_in + 3, i)

                pair(0)
                with act.Fori(1, NFO - 1) as i:
                    pair(i)
                pair(NFO - 1, (0, 1))
                with act.Fori(0, 4) as i:
                    for j in range(2):
                        hi(base_out + j + 2, i)
                        unit(j + 2, i)
                hi(base_out + 10)
                unit(10)
                hi(base_out + 11)

            act.wait_ge(const_done, 1)
            nc.scalar.activation(scrap[:, 0:1], zero1[:], ACT.Copy)
            for j, k in list(enumerate(ORDER))[X_DVE:]:
                act.wait_ge(xt_mm, j + 1)
                nc.scalar.activation(xT[:, k, :], ps[:, k, :], ACT.Copy).then_inc(x_act, 1)
            act.wait_ge(raw_first, 16)
            nc.scalar.activation(wh[0][:, FIRST], raw[0][:, FIRST], ACT.Copy).then_inc(hi_first, 1)
            act.wait_ge(par_ready, 1)
            act.wait_ge(x_act, KD - X_DVE)

            def other_half():
                act.wait_ge(raw_full[0], landed[0])
                nc.scalar.activation(wh[0][:, OTHER], raw[0][:, OTHER], ACT.Copy).then_inc(hi_done, 1)

            scaled_hi(0, 0, "norm_ffn1_pre", between=other_half)
            hi(1)
            squares(0, lambda j, k: None)
            nc.scalar.activation(sc[:], par[:, col["c_2"]:col["c_2"] + KD], ACT.Silu).then_inc(sc_done, 1)
            act.wait_ge(const_done, 1)
            load_root(3)
            ffn(0, 0, S_F1I, S_F1O)
            act.wait_ge(gpad, 1)
            act.wait_ge(gates_in, 16 * 5)
            for q in range(4):
                last = nc.scalar.activation(gh[:, :, 32 * q:32 * q + HEADS], gw[:, :, HEADS * q:HEADS * q + HEADS], ACT.Copy)
            last.then_inc(gw_hi, 1)
            post_norm(1, 0, S_MIX - 1)

            scaled_hi(1, 1, "norm_mix_pre")
            squares(2, lambda j, k: None)
            hi(S_MIX + 1)

            def from_work(step, target, view=None):
                act.wait_ge(wk_mm, WORK[step])
                source = ps[:, 4 + WORK[step] % 2, :]
                nc.scalar.activation(target, source if view is None else view(source), ACT.Copy).then_inc(wk_free, 1)

            def mixer_step(kind, *step):
                if kind == "spread":
                    root(2)
                elif kind == "rows" and step[0] == 0:
                    act.wait_ge(zr_done, 1)
                    nc.scalar.activation(zrow, zrow, ACT.Identity, bias=gbias[:]).then_inc(z_done, 1)
                    act.wait_ge(abs_done, 1)
                    chain.link(nc.scalar.activation(lrow, lrow, ACT.Exp))
                    nc.scalar.activation(lrow, lrow, ACT.Ln, bias=1.0).then_inc(ln_done, 1)
                elif kind == "rows" and step[0] == 2:
                    act.wait_ge(rows_done, 1)
                    nc.scalar.activation(erow[:], erow[:], ACT.Exp).then_inc(erow_done, 1)
                elif kind == "cols":
                    from_work(("cols",), cT[:], lambda s: s.rearrange("p (w b r) -> p w b r", b=TB, r=64))
                elif kind == "bc":
                    act.wait_ge(p_ready, 4 * step[0])
                    from_work((kind, *step), Mb[:, step[1], :])
                elif kind == "S":
                    act.wait_ge(p_ready, 4 * step[0] + 2 * step[1])
                    from_work((kind, *step), Sx[:, step[2], :])
                elif kind == "vt":
                    act.wait_ge(u_mm, 4 * step[0])
                    from_work((kind, *step), vS[:, step[1], :, 0:P], lambda s: s.rearrange("p (b d) -> p b d", d=P))
                elif kind == "prep":
                    p, h, d = step
                    u, row = 4 * p + 2 * h + d, 32 * d + 2 * p + h
                    if u >= 2:
                        act.wait_ge(u_mm, u - 1)
                    act.wait_ge(dg_done, u + 1)
                    for b in range(TB):
                        bias = cT[:, 0, b, row:row + 1]
                        t0, t1 = ((b + 1) * P, T) if d == 0 else (0, b * P)
                        if t1 > t0:
                            nc.scalar.activation(E[:, u % 2, b, t0:t1], Mb[:, 2 * h + d, t0:t1], ACT.Exp, bias=bias, scale=-1.0)
                        last = nc.scalar.activation(E[:, u % 2, b, b * P:(b + 1) * P], dg[:, b, :], ACT.Exp, bias=bias)
                    last.then_inc(E_done, 1)
                elif kind == "hn":
                    head = 2 * step[0] + step[1]
                    act.wait_ge(hr_done, head + 1)
                    nc.scalar.activation(h4[:, head, :], h4[:, head, :], ACT.Sqrt).then_inc(hsr_done, 1)
                elif kind == "hy":
                    from_work((kind, *step), tt[:, step[1], :])
                elif kind == "split":
                    unit = MIX_OUT[step[0]]
                    act.wait_ge(u_mm, 8)
                    act.wait_ge(*(evacuated[0, "bg"] if step[0] == 0 else (y_done, 2)))
                    nc.scalar.activation(yh[:, step[0], :, :], y_unit[unit], ACT.Copy).then_inc(rhi_done, 1)

            for n, (p, what, during) in enumerate(MIXER):
                b = 2 * (n % 2)
                for k in range(KD):
                    if k == 3 and n and MIXER[n - 1][1] != "qk":
                        hi(S_MIX + n + 1)
                    for step in during.get(k, ()):
                        mixer_step(*step)
                if what == "qk":
                    hi(S_MIX + n + 2)
                    act.wait_ge(*evacuated[p, what])
                    for h in range(2):
                        last = nc.scalar.activation(k2m[HALF[h], h, :], kS[HALF[h], :], ACT.Copy)
                        nc.scalar.activation(q2m[HALF[h], h, :], qS[HALF[h], :], ACT.Copy)
                    last = nc.scalar.activation(q2m[HALF[1], 0, :], qS[HALF[0], :], ACT.Copy)
                    last = nc.scalar.activation(q2m[HALF[0], 1, :], qS[HALF[1], :], ACT.Copy)
                    last.then_inc(qk_hi, 1)
                elif what == "o":
                    act.wait_ge(*evacuated[p, what])
                    nc.scalar.activation(sgo[:, 2 * p:2 * p + 2, :], sgo[:, 2 * p:2 * p + 2, :], ACT.Sigmoid).then_inc(so_done, 1)
            act.wait_ge(slot_used, S_MO)
            act.wait_ge(y_done, 4)
            nc.scalar.activation(ah[:, 0:2, :], y_unit[3], ACT.Copy).then_inc(rhi_done, 1)
            hi(S_MO + 1)
            act.wait_ge(*evacuated[1, "bg"])
            nc.scalar.activation(ah[:, 2:4, :], y_unit[1], ACT.Copy).then_inc(rhi_done, 1)
            hi(S_MO + 2)
            hi(S_MO + 3)
            hi(S_MO + 4)
            post_norm(3, 1, S_F2I - 1)

            scaled_hi(2, 2, "norm_ffn2_pre")
            hi(S_F2I + 1)
            squares(4, lambda j, k: None)
            ffn(1, 4, S_F2I, S_F2O)
            post_norm(5, 2, S_ATT - 1)

            pre_norm(6, 3, 3, shift=True)
            hi(S_ATT + 1)
            act.wait_ge(att_init, 1)

            def att_step(step, r):
                kind, h = step[0], step[1] if len(step) > 1 else 0
                if kind == "Q":
                    i = step[2]
                    idx, n = 4 * h + i, (i + 1) * P
                    act.wait_ge(q_mm, r * 8 + (idx + 1))
                    act.wait_ge(w_done, r * 8 + max(idx - 1, 0))
                    nc.scalar.activation(g1[:, idx % 2, 0:n], ps[:, 4 + idx % 2, 0:n], ACT.Sigmoid, scale=-1.0)
                    nc.scalar.activation(be[:, idx % 2, 0:n], ps[:, 4 + idx % 2, 0:n], ACT.Sigmoid).then_inc(sig_done, 1)
                elif kind == "V":
                    act.wait_ge(v_mm, r + 1)
                    act.wait_ge(pv_mm, r * 2)
                    bank = ps[:, 6, :].rearrange("p (b d) -> p b d", d=P)
                    for e in range(2):
                        last = nc.scalar.activation(vph[:, e, :, HALF[e]], bank[:, :, HALF[e]], ACT.Copy)
                    last.then_inc(vhi_done, 1)
                elif kind == "sum":
                    act.wait_ge(pv_mm, r * 2 + (h + 1))
                    nc.scalar.activation(pvl[HALF[h], :], ps[HALF[1 - h], 7, :], ACT.Copy).then_inc(pv_low, 1)
                elif kind == "T":
                    i = step[2]
                    idx = 4 * h + i
                    act.wait_ge(t_mm, r * 8 + (idx + 1))
                    act.wait_ge(pv_mm, r * 2 + h)
                    nc.scalar.activation(wTh[:, 0:i + 1, i * P:(i + 1) * P],
                                         ps[:, 6, 0:(i + 1) * P].rearrange("p (b t) -> p b t", t=P), ACT.Copy).then_inc(thi_done, 1)

            def att_out(r):
                act.wait_ge(ga_done, r + 1)
                nc.scalar.activation(gah[:, bass.ds(r, 1), :] if not isinstance(r, int) else gah[:, r:r + 1, :],
                                     ga[:].unsqueeze(1), ACT.Copy).then_inc(gah_done, 1)

            def att_read(i, j):
                act.wait_ge(slot_used, i * 2 + (S_ATT + j + 1))
                if j == 0:
                    act.wait_ge(q_mm, i * 8)
                    for e in range(2):
                        last = nc.scalar.activation(k2[HALF[e], e, :], ps[HALF[e], 1, :], ACT.Copy)
                    last.then_inc(qe_done, 1)
                    for e in range(2):
                        last = nc.scalar.activation(q2[HALF[e], e, :], ps[HALF[e], 0, :], ACT.Copy, scale=ZSCALE)
                    last.then_inc(qe_done, 1)
                    act.wait_ge(qe_done, i * 3 + 1)
                    for e in range(2):
                        last = nc.scalar.activation(k2[HALF[1 - e], e, :], k2[HALF[e], e, :].bitcast(fp32), ACT.Copy)
                    last.then_inc(qe_done, 1)
                else:
                    nc.scalar.activation(v2[:], ps[:, 2, :], ACT.Copy).then_inc(ve_done, 1)
                    act.wait_ge(zs_done, i)
                    nc.scalar.activation(sz[:], ps[:, 3, :], ACT.Sigmoid).then_inc(sz_done, 1)

            def att_round(r):
                for j in range(2):
                    for s in range(8):
                        if s == ATT_SPLIT[j]:
                            hi(S_ATT + j + 3, r)
                        if j == 1 and s == 0:
                            att_read(r + 1, 0)
                        for step in ATT_STEPS.get(8 * j + s, []):
                            att_step(step, r)
                att_step(("sum", 1), r)
                att_read(r + 1, 1)
                att_out(r)

            att_read(0, 0)
            hi(S_ATT + 2)
            att_read(0, 1)
            att_round(0)
            with act.Fori(1, PAIRS - 1) as r:
                att_round(r)

            def pool_slot(j):
                kind, g = POOL_ORDER[j]
                b = 2 * (j % 2)
                act.wait_ge(slot_used, S_POOL + j + 1)
                if kind == "u":
                    if g == 0:
                        act.wait_ge(w_done, 8 * PAIRS)
                    else:
                        act.wait_ge(d_done, g)
                    nc.scalar.activation(uS[:], ps[:, b:b + 2, :], ACT.Copy).then_inc(u_in, 1)
                else:
                    act.wait_ge(zb_done, g)
                    nc.scalar.activation(sb2[:], ps[:, b:b + 2, :], ACT.Sigmoid).then_inc(zsig, 1)

            def pool_hi(g):
                act.wait_ge(d_done, g + 1)
                source = p1 if g in (1, 3) else p2
                nc.scalar.activation(dh[:, 2 * g:2 * g + 2, :], source[:], ACT.Copy).then_inc(dhi_done, 1)

            for j in range(2):
                for s in range(8):
                    if s == ATT_SPLIT[j]:
                        hi(S_POOL + j + 1)
                    for step in ATT_STEPS.get(8 * j + s, []):
                        att_step(step, PAIRS - 1)
                if j == 1:
                    att_step(("sum", 1), PAIRS - 1)
                    att_out(PAIRS - 1)
                    pool_hi(0)
                pool_slot(j)
            for j in range(2, 8):
                hi(S_POOL + j + 1)
                kind, g = POOL_ORDER[j - 1]
                if kind == "u":
                    pool_hi(g)
                pool_slot(j)
            hi(S_FIN)
            for g in range(4):
                act.wait_ge(yb_t, g + 1)
                nc.scalar.activation(dh[:, 2 * g:2 * g + 2, :], (p1 if g % 2 == 0 else p2)[:], ACT.Copy).then_inc(ybh_done, 1)
            hi(S_FIN + 1)

            def out_hi(j):
                act.wait_ge(mg_done, j + 1)
                nc.scalar.activation(ah[:, 2 * j:2 * j + 2, :], mg[:, 2 * j:2 * j + 2, :], ACT.Copy).then_inc(rhi_done, 1)

            def branches(c):
                first, last = (isinstance(c, int) and c == x for x in (0, 3))
                for j in range(4):
                    n = S_FIN + j
                    act.wait_ge(raw_full[n % 2], c * 32 + landed[n + 2])
                    act.wait_ge(slot_used, c * 4 + (n + 1))
                    nc.scalar.activation(wh[n % 2][:], raw[n % 2][:], ACT.Copy).then_inc(hi_done, 1)
                    if j == 0:
                        act.wait_ge(m_done, c * 2)
                        gate = ps[:, 4:6, :] if first else ps[:, 0:2, :]
                        nc.scalar.activation(sm[:], gate, ACT.Sigmoid).then_inc(sm_done, 1)
                    elif j == 2:
                        act.wait_ge(ybl_done, 4)
                        act.wait_ge(m_done, c * 2)
                        nc.scalar.activation(sn[:], ps[:, 0:2, :], ACT.Sigmoid).then_inc(sm_done, 1)
                        if last:
                            for unit in range(3):
                                out_hi(unit)

            branches(0)
            with act.Fori(1, 3) as c:
                branches(c)
            branches(3)
            out_hi(3)
            for j in range(2):
                hi(S_OUT + j + 2)
            load_root(3)
            squares(7, lambda j, k: act.wait_ge(x_ready, XB[4] + j + 1))
            root(7)
            act.wait_ge(rstd_done, 8)
            for n in OUT_ACT:
                act.wait_ge(ot_mm, n + 1)
                k = OUT_ORDER[n]
                for b in range(TB):
                    last = nc.scalar.activation(outS[:, b, k * P:(k + 1) * P], ps[:, k, b * P:(b + 1) * P], ACT.Copy, scale=r4[:, b:b + 1])
                last.then_inc(ota_done, 1)

        @block.vector
        def _(dve):
            chain = Chain(dve, dve_self)

            def lo(n, i=0):
                dve.wait_ge(hi_done, i * 2 + (n + 1))
                nc.vector.tensor_tensor(wl[n % 2][:], raw[n % 2][:], wh[n % 2][:].bitcast(fp32), ALU.subtract).then_inc(lo_done, 1)

            def variance(stage, bank, spread=True):
                dve.wait_ge(sum_done, stage + 1)
                chain.link(nc.vector.tensor_scalar(r4[:], ps[:, bank, 0:TB], 1.0 / D, EPS, ALU.mult, ALU.add))
                nc.vector.reciprocal(r4[:], r4[:]).then_inc(var_done, 1)
                dve.wait_ge(*((rb_done if spread else rstd_done), stage + 1))

            def pre_norm(stage, pre, gain, shift=False):
                variance(stage, 4)

                def scaled(j):
                    if j >= 2:
                        dve.wait_ge(a_ready, 8 * pre + j - 1)
                    k = ORDER[j]
                    nc.vector.scalar_tensor_tensor(tt[:, j % 2, :], xT[:, k, :], gain(k), ps[:, 4, :], ALU.mult, ALU.mult).then_inc(t_done, 1)

                scaled(0)
                for j, k in enumerate(ORDER):
                    if j + 1 < KD:
                        scaled(j + 1)
                    dve.wait_ge(ah_done, 8 * pre + j + 1)
                    if shift:
                        nc.vector.scalar_tensor_tensor(al[:, k, :], tt[:, j % 2, :], mod[:, k:k + 1], ah[:, k, :].bitcast(fp32),
                                                       ALU.add, ALU.subtract).then_inc(a_ready, 1)
                    else:
                        nc.vector.tensor_tensor(al[:, k, :], tt[:, j % 2, :], ah[:, k, :].bitcast(fp32), ALU.subtract).then_inc(a_ready, 1)

            def scaled_lo(j, pre, gain):
                k = ORDER[j]
                dve.wait_ge(ah_done, 8 * pre + j + 1)
                nc.vector.scalar_tensor_tensor(al[:, k, :], xT[:, k, :], pcol(gain, k), ah[:, k, :].bitcast(fp32),
                                               ALU.mult, ALU.subtract).then_inc(a_ready, 1)

            def add_squares(stage):
                for j in range(1, 7):
                    dve.wait_ge(sq_done, 8 * stage + j + 1)
                    dve.wait_ge(*((sum_done, stage) if j == 1 else (acc_step, ACC[stage] + j - 1)))
                    nc.vector.tensor_tensor(acc[:], sq[:, 0, :] if j == 1 else acc[:], sq[:, j % 2, :], ALU.add).then_inc(acc_step, 1)

            def post_norm(stage, o, last, gain, x_stage, after=None):
                dve.wait_ge(*whole(o, last, 0))
                nc.vector.tensor_copy(h7[:], ps[:, 7, :]).then_inc(h7_done, 1)
                add_squares(stage)
                variance(stage, 7)

                def scaled(j):
                    if j >= 2:
                        if after:
                            dve.wait_ge(x_ready, XB[x_stage] + j - 1)
                        else:
                            dve.wait_ge(*((x_ready, XB[x_stage] + j // 2) if j % 2 == 0 else (x_odd, j // 2)))
                    k = ORDER[j]
                    dve.wait_ge(*whole(o, last, j))
                    nc.vector.scalar_tensor_tensor(tt[:, j % 2, :], ps[:, k, :] if j else h7[:], pcol(gain, k), rstd[:] if j else ps[:, 7, :],
                                                   ALU.mult, ALU.mult).then_inc(t_done, 1)

                def added(j):
                    k = ORDER[j]
                    dve.wait_ge(t_done, 8 * T_OF[stage] + j + 1)
                    nc.vector.tensor_tensor(xT[:, k, :], tt[:, j % 2, :], xT[:, k, :], ALU.add).then_inc(x_ready, 1)

                scaled(0)
                if after:
                    added(0)
                chain.link(nc.vector.tensor_copy(rstd[:], ps[:, 7, :]))
                for j in range(KD):
                    if j + 1 < KD:
                        scaled(j + 1)
                    if after and j:
                        after(j - 1)
                    elif not after and j % 2 == 0:
                        added(j)
                if after:
                    after(KD - 1)
                else:
                    for j in range(5, 8):
                        dve.wait_ge(sq_done, 8 * 6 + j + 1)
                        dve.wait_ge(*((sum_done, 6) if j == 5 else (acc_step, ACC[6] + j - 5)))
                        nc.vector.tensor_tensor(acc[:], sq6(4) if j == 5 else acc[:], sq6(j), ALU.add).then_inc(acc_step, 1)

            def ffn(f, stage, base_in, base_out):
                r2 = rstd[:].unsqueeze(1).to_broadcast([P, 2, T])

                def unit(j, i=0):
                    dve.wait_ge(rhi_done, i * 2 + ((R_F1, R_F2)[f] + j + 1))
                    nc.vector.tensor_tensor(rl[:, j % 2, :, :], hid[:, bass.ds(i * 4 + 2 * j, 2), :],
                                            rh[:, j % 2, :, :].bitcast(fp32), ALU.subtract).then_inc(rlo_done, 1)

                def pair(i, units=()):
                    lo(base_in + 2, i)
                    if isinstance(i, int) and i == 0:
                        variance(stage, 4)
                        chain.link(nc.vector.tensor_copy(rstd[:], ps[:, 4, :]))
                    else:
                        dve.wait_ge(hid_ready, i + f * NFO)
                    dve.wait_ge(slot_used, i * 2 + (base_in + 1))
                    gate = ps[:, 6:8, :] if isinstance(i, int) and i == 0 else ps[:, 0:2, :]
                    nc.vector.tensor_tensor(gt[:], gate, r2, ALU.mult).then_inc(gt_done, 1)
                    for j in units:
                        unit(j)
                    dve.wait_ge(silu_done, i + (f * NFO + 1))
                    dve.wait_ge(slot_used, i * 2 + (base_in + 2))
                    nc.vector.tensor_tensor(gt[:], sg[:], ps[:, 2:4, :], ALU.mult).then_inc(ut_done, 1)
                    dve.wait_ge(ut_done, i + (f * NFO + 1))
                    nc.vector.tensor_tensor(hid[:, bass.ds(i * 2, 2), :], gt[:], r2, ALU.mult).then_inc(hid_ready, 1)
                    lo(base_in + 3, i)

                pair(0)
                with dve.Fori(1, NFO - 1) as i:
                    pair(i)
                pair(NFO - 1, (0, 1))
                with dve.Fori(0, 4) as i:
                    for j in range(2):
                        lo(base_out + j + 2, i)
                        unit(j + 2, i)
                lo(base_out + 10)
                unit(10)
                lo(base_out + 11)

            nc.vector.memset(gbias[:], 0.0).then_inc(par_cols, 1)
            for j, k in enumerate(ORDER[:X_DVE]):
                dve.wait_ge(xt_mm, j + 1)
                nc.vector.tensor_copy(xT[:, k, :], ps[:, k, :]).then_inc(x_ready, 1)
                if j == 1:
                    dve.wait_ge(xt_mm, KD + 1)
                    chain.link(nc.vector.tensor_copy(par[:, 0:n_par], ps[:, 7, 0:n_par]))
                    for name in ("norm_ffn1_post", "norm_ffn2_post"):
                        cols = par[:, col[name]:col[name] + KD]
                        last = nc.vector.tensor_scalar(cols, cols, 0.5, None, ALU.mult)
                    last.then_inc(par_ready, 1)
            dve.wait_ge(par_ready, 1)
            for half, ready, done, chunks in ((FIRST, hi_first, lo_first, range(3)), (OTHER, hi_done, lo_done, range(3, KD))):
                dve.wait_ge(ready, 1)
                nc.vector.tensor_tensor(wl[0][:, half], raw[0][:, half], wh[0][:, half].bitcast(fp32), ALU.subtract).then_inc(done, 1)
                for j in chunks:
                    scaled_lo(j, 0, "norm_ffn1_pre")
            lo(1)
            ffn(0, 0, S_F1I, S_F1O)
            dve.wait_ge(gw_hi, 1)
            for q in range(4):
                cols = slice(32 * q, 32 * q + HEADS)
                last = nc.vector.tensor_tensor(gl[:, :, cols], gw[:, :, HEADS * q:HEADS * q + HEADS],
                                               gh[:, :, cols].bitcast(fp32), ALU.subtract)
            last.then_inc(gw_lo, 1)
            post_norm(1, 0, S_MIX - 1, "norm_ffn1_post", 1, after=lambda j: scaled_lo(j, 1, "norm_mix_pre"))

            lo(S_MIX + 1)

            def mixer_step(kind, *step):
                if kind == "ada" and step[0] == 7:
                    dve.wait_ge(ada_mm, 1)
                    chain.link(nc.vector.tensor_tensor(mod[:], ps[:, 7, 0:24], par[:, col["b_ada_2"]:col["b_ada_2"] + 24], ALU.add))
                    chain.link(nc.vector.tensor_scalar(gmod[:], mod[:, 8:16], 1.0, None, ALU.add))
                    nc.vector.tensor_tensor(gmod[:], gmod[:], par[:, col["norm_gain_2"]:col["norm_gain_2"] + 8], ALU.mult).then_inc(mod_done, 1)
                elif kind == "spread":
                    variance(2, 4)
                    chain.link(nc.vector.tensor_copy(rstd[:], ps[:, 4, :]))
                    chain.link(nc.vector.tensor_tensor(rsq, rstd[:], rstd[:], ALU.mult))
                elif kind == "rows" and step[0] == 0:
                    dve.wait_ge(gate_mm, 1)
                    nc.vector.tensor_tensor(zrow, ps[:, 6, :], rstd[:], ALU.mult).then_inc(zr_done, 1)
                    dve.wait_ge(z_done, 1)
                    nc.vector.scalar_tensor_tensor(lrow, zrow, -1.0, zrow, ALU.mult, ALU.min).then_inc(abs_done, 1)
                elif kind == "rows" and step[0] == 1:
                    dve.wait_ge(ln_done, 1)
                    chain.link(nc.vector.scalar_tensor_tensor(frow, zrow[64:128, :], 0.0, lrow[64:128, :], ALU.min, ALU.subtract))
                    f, r = slice(0, 32), slice(32, 64)
                    zeros = zero1[0:32, :].to_broadcast([32, T])
                    zeros_r = zero1[32:64, :].to_broadcast([32, T])
                    nc.vector.tensor_tensor_scan(brow[f, :], frow[f, :], zeros, 0.0, ALU.add, ALU.add)
                    chain.link(nc.vector.tensor_tensor_scan(brow[r, ::-1], frow[r, ::-1], zeros_r, 0.0, ALU.add, ALU.add))
                    chain.link(nc.vector.tensor_tensor(crow, zrow[0:64, :], brow, ALU.subtract))
                    nc.vector.tensor_tensor_scan(mrow[f, :], crow[f, :], crow[f, :], NEG, ALU.max, ALU.max)
                    chain.link(nc.vector.tensor_tensor_scan(mrow[r, ::-1], crow[r, ::-1], crow[r, ::-1], NEG, ALU.max, ALU.max))
                    chain.link(nc.vector.scalar_tensor_tensor(erow[:], brow, -1.0, mrow[:], ALU.mult, ALU.subtract))
                    nc.vector.tensor_scalar(erow[:], erow[:], 88.0, None, ALU.min).then_inc(rows_done, 1)
                elif kind == "prep":
                    p, h, d = step
                    u = 4 * p + 2 * h + d
                    dve.wait_ge(wk_free, WORK["bc", p, 2 * h + d])
                    dve.wait_ge(E_done, u)
                    mask = (maskF, maskB)[d]
                    nc.vector.scalar_tensor_tensor(dg, Mb[:, 2 * h + d, :].rearrange("p (b t) -> p b t", t=P), -1.0,
                                                   mask[:].unsqueeze(1).to_broadcast([P, TB, P]), ALU.mult, ALU.add).then_inc(dg_done, 1)
                elif kind == "weigh":
                    p, h, d = step
                    u = 4 * p + 2 * h + d
                    dve.wait_ge(E_done, u + 1)
                    dve.wait_ge(wk_free, WORK["S", p, h, TB - 1])
                    for b in range(TB):
                        t0, t1 = span(d, b)
                        last = nc.vector.tensor_tensor(E[:, u % 2, b, t0:t1], E[:, u % 2, b, t0:t1], Sx[:, b, t0:t1], ALU.mult)
                    last.then_inc(p_ready, 1)
                elif kind == "div":
                    p, h, d = step
                    u, row = 4 * p + 2 * h + d, 32 * d + 2 * p + h
                    dve.wait_ge(u_mm, u + 1)
                    blocks = ps[:, 6:8, 0:2 * (DV + 1)].rearrange("p w (b d) -> p w b d", d=DV + 1)
                    den, numer = blocks[:, :, :, DV], blocks[:, :, :, 0:DV]
                    each = d4[:].unsqueeze(3).to_broadcast([P, 2, 2, DV])
                    chain.link(nc.vector.tensor_tensor(d4[:], den, cT[:, 1, :, row].rearrange("p (w b) -> p w b", w=2), ALU.max))
                    chain.link(nc.vector.scalar_tensor_tensor(d4[:], den, -1.0, d4[:], ALU.mult, ALU.max))
                    chain.link(nc.vector.reciprocal(d4[:], d4[:]))
                    target = hs[:, h, :].rearrange("p (w b d) -> p w b d", w=2, d=DV)
                    if d == 0:
                        nc.vector.tensor_tensor(target, numer, each, ALU.mult).then_inc(h_done, 1)
                    else:
                        chain.link(nc.vector.tensor_tensor(dt_[:].rearrange("p (w b d) -> p w b d", w=2, d=DV), numer, each, ALU.mult))
                        nc.vector.tensor_tensor(hs[:, h, :], hs[:, h, :], dt_[:], ALU.add).then_inc(h_done, 1)
                    dve.wait_ge(h_done, u + 1)
                elif kind == "hn":
                    p, h = step
                    mean = h4[:, 2 * p + h, :]
                    chain.link(nc.vector.tensor_tensor(dt_[:], hs[:, h, :], hs[:, h, :], ALU.mult))
                    chain.link(nc.vector.tensor_reduce(mean, dt_[:].rearrange("p (b d) -> p b d", d=DV), AX.X, ALU.add))
                    chain.link(nc.vector.tensor_scalar(mean, mean, 1.0 / DV, EPS, ALU.mult, ALU.add))
                    nc.vector.reciprocal(mean, mean).then_inc(hr_done, 1)
                elif kind == "hx":
                    p, h = step
                    head = 2 * p + h
                    dve.wait_ge(hsr_done, head + 1)
                    target = hs[:, h, :].rearrange("p (b d) -> p b d", d=DV)
                    nc.vector.tensor_tensor(target, target, h4[:, head, :].unsqueeze(2).to_broadcast([P, TB, DV]), ALU.mult).then_inc(hn_done, 1)
                elif kind == "hz":
                    p, h = step
                    head = 2 * p + h
                    dve.wait_ge(wk_free, WORK["hy", p, h])
                    dve.wait_ge(so_done, p + 1)
                    nc.vector.scalar_tensor_tensor((yA, yB)[p][:, 2 + h, :], tt[:, h, :], pcol("mlstm_norm", head), sgo[:, head, :],
                                                   ALU.mult, ALU.mult).then_inc(y_done, 1)
                elif kind == "conv":
                    p = step[0]
                    dve.wait_ge(*evacuated[p, "hc"])
                    for tap in (1, 0, 2):
                        for c in range(2):
                            w = pcol("conv_w", 4 * tap + 2 * p + c)
                            if tap == 1:
                                last = nc.vector.tensor_scalar(ct[:, c, :], ux[:, c, 1:T + 1], w, pcol("conv_b", 2 * p + c), ALU.mult, ALU.add)
                            else:
                                last = nc.vector.scalar_tensor_tensor(ct[:, c, :], ux[:, c, tap:tap + T], w, ct[:, c, :], ALU.mult, ALU.add)
                        chain.link(last)
                    chain.link(nc.vector.tensor_tensor(ct[:], ct[:], rstd[:].unsqueeze(1).to_broadcast([P, 2, T]), ALU.mult))
                elif kind == "split":
                    unit = MIX_OUT[step[0]]
                    dve.wait_ge(rhi_done, R_MO + step[0] + 1)
                    nc.vector.tensor_tensor(yl[:, step[0], :, :], y_unit[unit], yh[:, step[0], :, :].bitcast(fp32),
                                            ALU.subtract).then_inc(rlo_done, 1)

            for n, (p, what, during) in enumerate(MIXER):
                b = 2 * (n % 2)
                for k in range(KD):
                    if k == 3 and n and MIXER[n - 1][1] != "qk":
                        lo(S_MIX + n + 1)
                    for step in during.get(k, ()):
                        mixer_step(*step)
                dve.wait_ge(slot_used, S_MIX + n + 1)
                sums, r2 = ps[:, b:b + 2, :], rstd[:].unsqueeze(1).to_broadcast([P, 2, T])
                if what == "qk":
                    if p:
                        dve.wait_ge(wk_free, WORK["S", 0, 1, TB - 1])
                    nc.vector.tensor_tensor(kS[:], ps[:, b + 1, :], rstd[:], ALU.mult)
                    nc.vector.scalar_tensor_tensor(qS[:], ps[:, b, :], ZSCALE, rstd[:], ALU.mult, ALU.mult).then_inc(pf_done, 1)
                    lo(S_MIX + n + 2)
                    dve.wait_ge(qk_hi, p + 1)
                    for h in range(2):
                        own, other = HALF[h], HALF[1 - h]
                        nc.vector.tensor_tensor(k2m[other, h, :], kS[own, :], k2m[own, h, :].bitcast(fp32), ALU.subtract)
                        last = nc.vector.tensor_tensor(ql[own, :], qS[own, :], q2m[own, h, :].bitcast(fp32), ALU.subtract)
                    last.then_inc(qk_lo, 1)
                elif what == "v":
                    if p:
                        dve.wait_ge(wk_free, WORK["vt", 0, 1])
                    nc.vector.tensor_tensor(vT[:], sums, r2, ALU.mult).then_inc(pf_done, 1)
                elif what == "o":
                    nc.vector.tensor_tensor(sgo[:, 2 * p:2 * p + 2, :], sums, r2, ALU.mult).then_inc(pf_done, 1)
                elif what == "cg":
                    if p:
                        dve.wait_ge(*evacuated[0, "hc"])
                    nc.vector.tensor_tensor(cgS[:], sums, rsq.unsqueeze(1).to_broadcast([P, 2, T]), ALU.mult).then_inc(pf_done, 1)
                elif what == "hc":
                    dve.wait_ge(*evacuated[p, "cg"])
                    dve.wait_ge(edges, 1)
                    nc.vector.tensor_tensor(ux[:, :, 1:T + 1], cgS[:], sums, ALU.mult).then_inc(pf_done, 1)
                elif what == "bg":
                    nc.vector.tensor_tensor((yA, yB)[p][:, 0:2, :], ct[:], sums, ALU.mult).then_inc(pf_done, 1)
            for j in range(2):
                unit = MIX_OUT[2 + j]
                dve.wait_ge(rhi_done, R_MO + j + 3)
                nc.vector.tensor_tensor(al[:, 2 * j:2 * j + 2, :], y_unit[unit], ah[:, 2 * j:2 * j + 2, :].bitcast(fp32),
                                        ALU.subtract).then_inc(rlo_done, 1)
                lo(S_MO + j + 1)
            lo(S_MO + 3)
            lo(S_MO + 4)

            post_norm(3, 1, S_F2I - 1, "norm_mix_post", 2, after=lambda j: scaled_lo(j, 2, "norm_ffn2_pre"))
            lo(S_F2I + 1)
            add_squares(4)
            ffn(1, 4, S_F2I, S_F2O)
            post_norm(5, 2, S_ATT - 1, "norm_ffn2_post", 3)

            pre_norm(6, 3, lambda k: gmod[:, k:k + 1], shift=True)
            lo(S_ATT + 1)
            dve.wait_ge(att_init, 1)

            def att_step(step, r):
                kind, h = step[0], step[1] if len(step) > 1 else 0
                if kind == "Q":
                    i = step[2]
                    idx, n = 4 * h + i, (i + 1) * P
                    dve.wait_ge(sig_done, r * 8 + (idx + 1))
                    at = gc_at(i)
                    chain.link(nc.vector.tensor_tensor_scan(Gc[:, at:at + n][:, ::-1], g1[:, idx % 2, 0:n][:, ::-1],
                                                            zero1[:].to_broadcast([P, n]), 1.0, ALU.mult, ALU.add))
                    dve.wait_ge(t_mm, r * 8 + max(idx - 3, 0))
                    nc.vector.tensor_tensor(wt_of(i), be[:, idx % 2, 0:n], Gc[:, at + 1:at + n + 1], ALU.mult).then_inc(w_done, 1)
                elif kind == "V":
                    dve.wait_ge(vhi_done, r + 1)
                    bank = ps[:, 6, :].rearrange("p (b d) -> p b d", d=P)
                    for e in range(2):
                        last = nc.vector.tensor_tensor(vp[:, e, :, HALF[1 - e]], bank[:, :, HALF[e]], vph[:, e, :, HALF[e]].bitcast(fp32), ALU.subtract)
                    last.then_inc(vlo_done, 1)
                elif kind == "sum":
                    dve.wait_ge(pv_low, r * 2 + (h + 1))
                    if h == 0:
                        dve.wait_ge(gah_done, r)
                        dve.wait_ge(gal_done, r)
                    nc.vector.tensor_tensor(ga[HALF[h], :], ps[HALF[h], 7, :], pvl[HALF[h], :], ALU.add).then_inc(pv_sum, 1)
                elif kind == "T":
                    i = step[2]
                    idx = 4 * h + i
                    dve.wait_ge(thi_done, r * 8 + (idx + 1))
                    place = (slice(None), slice(0, i + 1), slice(i * P, (i + 1) * P))
                    nc.vector.tensor_tensor(wTl[place], ps[:, 6, 0:(i + 1) * P].rearrange("p (b t) -> p b t", t=P),
                                            wTh[place].bitcast(fp32), ALU.subtract).then_inc(tlo_done, 1)

            def att_gate(r):
                att_step(("sum", 1), r)
                dve.wait_ge(pv_sum, r * 2 + 2)
                nc.vector.tensor_tensor(ga[:], ga[:], zs[:], ALU.mult).then_inc(ga_done, 1)

            def att_out(r):
                one = slice(r, r + 1) if isinstance(r, int) else bass.ds(r, 1)
                dve.wait_ge(gah_done, r + 1)
                nc.vector.tensor_tensor(gal[:, one, :], ga[:].unsqueeze(1), gah[:, one, :].bitcast(fp32), ALU.subtract).then_inc(gal_done, 1)

            def att_read(i, j):
                if j == 0:
                    dve.wait_ge(qe_done, i * 3 + 1)
                    dve.wait_ge(q_mm, i * 8)
                    for e in range(2):
                        nc.vector.tensor_tensor(kl[HALF[e], :], ps[HALF[e], 1, :], k2[HALF[e], e, :].bitcast(fp32), ALU.subtract)
                    dve.wait_ge(qe_done, i * 3 + 2)
                    for e in range(2):
                        last = nc.vector.scalar_tensor_tensor(q2[HALF[1 - e], e, :], ps[HALF[e], 0, :], ZSCALE, q2[HALF[e], e, :].bitcast(fp32),
                                                              ALU.mult, ALU.subtract)
                    last.then_inc(ke_done, 1)
                else:
                    dve.wait_ge(sz_done, i + 1)
                    dve.wait_ge(ga_done, i)
                    nc.vector.tensor_tensor(zs[:], sz[:], ps[:, 3, :], ALU.mult).then_inc(zs_done, 1)

            def att_round(r):
                for j in range(2):
                    for s in range(8):
                        for step in ATT_STEPS.get(8 * j + s, []):
                            att_step(step, r)
                    if j == 0:
                        att_read(r + 1, 0)
                att_gate(r)
                att_read(r + 1, 1)
                att_out(r)

            att_read(0, 0)
            att_read(0, 1)
            att_round(0)
            with dve.Fori(1, PAIRS - 1) as r:
                chain.enter(r, 8, 1)
                att_round(r)
            chain.leave(PAIRS - 1)

            def pooled(g):
                dve.wait_ge(u_in, g + 1)
                if g:
                    dve.wait_ge(dlo_done, g)
                w = WINDOWS[g]
                source, target, reach = uS, p1, 1
                while reach < w:
                    nc.vector.tensor_copy(target[:, :, 0:reach], source[:, :, 0:reach])
                    chain.link(nc.vector.tensor_tensor(target[:, :, reach:T], source[:, :, reach:T], source[:, :, 0:T - reach], ALU.add))
                    source, target, reach = target, (p2 if target is p1 else p1), 2 * reach
                chain.link(nc.vector.tensor_tensor(target[:, :, 0:w], source[:, :, 0:w],
                                                   invc[:, g, 0:w].unsqueeze(1).to_broadcast([P, 2, w]), ALU.mult))
                nc.vector.tensor_tensor(target[:, :, 0:w], target[:, :, 0:w], uS[:, :, 0:w], ALU.subtract)
                nc.vector.scalar_tensor_tensor(target[:, :, w:T], source[:, :, w:T], 1.0 / w, uS[:, :, w:T],
                                               ALU.mult, ALU.subtract).then_inc(d_done, 1)
                dve.wait_ge(dhi_done, g + 1)
                nc.vector.tensor_tensor(dl[:, 2 * g:2 * g + 2, :], target[:], dh[:, 2 * g:2 * g + 2, :].bitcast(fp32),
                                        ALU.subtract).then_inc(dlo_done, 1)

            def pool_slot(j):
                kind, g = POOL_ORDER[j]
                if kind == "z":
                    dve.wait_ge(zsig, g + 1)
                    nc.vector.tensor_tensor(zb[:, 2 * g:2 * g + 2, :], sb2[:], ps[:, 2 * (j % 2):2 * (j % 2) + 2, :], ALU.mult).then_inc(zb_done, 1)

            for j in range(2):
                for s in range(8):
                    for step in ATT_STEPS.get(8 * j + s, []):
                        att_step(step, PAIRS - 1)
                if j == 1:
                    att_gate(PAIRS - 1)
                    att_out(PAIRS - 1)
                    pooled(0)
                pool_slot(j)
            dve.wait_ge(lo_done, S_POOL + 3)
            for j in range(2, 8):
                lo(S_POOL + j + 1)
                kind, g = POOL_ORDER[j - 1]
                if kind == "u":
                    pooled(g)
                pool_slot(j)
            lo(S_FIN)
            for g in range(4):
                if g < 3:
                    dve.wait_ge(pw_mm, g + 1)
                else:
                    dve.wait_ge(slot_used, S_FIN)
                part = p1 if g % 2 == 0 else p2
                dve.wait_ge(dlo_done, 4)
                if g >= 2:
                    dve.wait_ge(ybl_done, g - 1)
                for c in range(2):
                    last = nc.vector.scalar_tensor_tensor(part[:, c, :], ps[:, 2 * (g % 2) + c, :], pcol("pool_scale_2", 2 * g + c),
                                                          zb[:, 2 * g + c, :], ALU.mult, ALU.mult)
                last.then_inc(yb_t, 1)
                dve.wait_ge(ybh_done, g + 1)
                nc.vector.tensor_tensor(dl[:, 2 * g:2 * g + 2, :], part[:], dh[:, 2 * g:2 * g + 2, :].bitcast(fp32),
                                        ALU.subtract).then_inc(ybl_done, 1)
            lo(S_FIN + 1)

            def out_lo(j):
                dve.wait_ge(rhi_done, R_OUT + j + 1)
                nc.vector.tensor_tensor(al[:, 2 * j:2 * j + 2, :], mg[:, 2 * j:2 * j + 2, :], ah[:, 2 * j:2 * j + 2, :].bitcast(fp32),
                                        ALU.subtract).then_inc(rlo_done, 1)

            def branches(c):
                last = isinstance(c, int) and c == 3
                for j in range(4):
                    n = S_FIN + j
                    dve.wait_ge(hi_done, c * 4 + (n + 3))
                    nc.vector.tensor_tensor(wl[n % 2][:], raw[n % 2][:], wh[n % 2][:].bitcast(fp32), ALU.subtract).then_inc(lo_done, 1)
                    if j == 1:
                        dve.wait_ge(sm_done, c * 2 + 1)
                        dve.wait_ge(mg_done, c)
                        dve.wait_ge(slot_used, c * 4 + (n + 1))
                        nc.vector.tensor_tensor(m1[:], sm[:], ps[:, 2:4, :], ALU.mult).then_inc(m_done, 1)
                    elif j == 2 and last:
                        for unit in range(3):
                            out_lo(unit)
                    elif j == 3:
                        dve.wait_ge(sm_done, c * 2 + 2)
                        dve.wait_ge(slot_used, c * 4 + (n + 1))
                        nc.vector.tensor_tensor(m2[:], sn[:], ps[:, 2:4, :], ALU.mult).then_inc(m_done, 1)
                        dve.wait_ge(m_done, c * 2 + 2)
                        nc.vector.tensor_tensor(mg[:, bass.ds(c * 2, 2), :], m1[:], m2[:], ALU.add).then_inc(mg_done, 1)

            branches(0)
            with dve.Fori(1, 3) as c:
                branches(c)
            branches(3)
            out_lo(3)
            for j in range(2):
                lo(S_OUT + j + 2)
            def gained(j):
                k = ORDER[j]
                dve.wait_ge(x_ready, XB[4] + j + 1)
                if j >= 3:
                    dve.wait_ge(ot_mm, j - 2)
                target = h7[:] if k == 7 else tt[:, j % 2, :]
                nc.vector.tensor_scalar(target, xT[:, k, :], pcol("final_gain_2", k), None, ALU.mult).then_inc(t_done, 1)

            for j, k in enumerate(ORDER):
                dve.wait_ge(*whole(3, S_END - 1, j))
                nc.vector.scalar_tensor_tensor(xT[:, k, :], ps[:, k, :], mod[:, 16 + k:17 + k], xT[:, k, :], ALU.mult, ALU.add).then_inc(x_ready, 1)
                if j:
                    gained(j - 1)
            gained(KD - 1)
            variance(7, 7, spread=False)
            for n in OUT_DVE:
                dve.wait_ge(ot_mm, n + 1)
                k = OUT_ORDER[n]
                nc.vector.tensor_tensor(outS[:, :, k * P:(k + 1) * P], ps[:, k, :].rearrange("p (b d) -> p b d", d=P),
                                        r4[:].unsqueeze(2).to_broadcast([P, TB, P]), ALU.mult).then_inc(otv_done, 1)

        @block.tensor
        def _(pe):
            def three(bank, w, m, start, stop):
                nc.tensor.matmul(bank, w[0], m[0], start=start, stop=False)
                nc.tensor.matmul(bank, w[0], m[1], start=False, stop=False)
                return nc.tensor.matmul(bank, w[1], m[0], start=False, stop=stop)

            def in_slot(n, i, banks, moving, steps=None, ready=None, each=2, halves=False):
                if not halves:
                    pe.wait_ge(lo_done, i * each + (n + 1))
                for j, k in enumerate(ORDER):
                    if halves and j in (0, 3):
                        pe.wait_ge((lo_first, lo_done)[j // 3], 1)
                    if steps:
                        steps(j)
                    if ready is not None:
                        pe.wait_ge(a_ready, 8 * ready + j + 1)
                    for c in range(2):
                        at = slice(k * CB + c * P, k * CB + (c + 1) * P)
                        last = three(ps[:, banks + c, :], (wh[n % 2][:, at], wl[n % 2][:, at]),
                                     (moving[0][:, k, :], moving[1][:, k, :]), j == 0, j == KD - 1)
                last.then_inc(slot_used, 1)

            def out_slot(n, i, moving, ready, first=False, blocks=range(KD), before=None):
                pe.wait_ge(lo_done, i * 2 + (n + 1))
                pe.wait_ge(rlo_done, ready)
                for kk in range(2):
                    for c in blocks:
                        if kk == 0 and before:
                            before(c)
                        at = slice(kk * D + c * P, kk * D + (c + 1) * P)
                        end = three(ps[:, c, :], (wh[n % 2][:, at], wl[n % 2][:, at]), (moving[0][:, kk, :], moving[1][:, kk, :]),
                                    first and kk == 0, False)
                end.then_inc(slot_used, 1)

            def last_slot(n, moving, ready, o, stage, before=None, whole_bank=None):
                pe.wait_ge(lo_done, n + 1)
                pe.wait_ge(rlo_done, ready)
                for j, c in enumerate(ORDER):
                    for kk in range(2):
                        at = slice(kk * D + c * P, kk * D + (c + 1) * P)
                        end = three(ps[:, c, :], (wh[n % 2][:, at], wl[n % 2][:, at]), (moving[0][:, kk, :], moving[1][:, kk, :]),
                                    False, kk == 1)
                    end.then_inc(bank_done if j < 7 else slot_used, 1)
                    if j >= 2 and whole_bank:
                        whole_bank(j - 2)
                before()
                sums(stage, 7)
                for j in (6, 7):
                    if whole_bank:
                        whole_bank(j)

            def sums(stage, bank):
                for step in range(2):
                    if step == 0:
                        pe.wait_ge(acc_step, ACC[stage] + 6)
                    else:
                        pe.wait_ge(sq_done, 8 * stage + 8)
                    source = acc[:] if step == 0 else sq[:, 1, :]
                    for b in range(TB):
                        last = nc.tensor.matmul(ps[:, bank, b:b + 1], source[:, b * P:(b + 1) * P], ones[:, 0:1],
                                                start=step == 0 and b == 0, stop=step == 1 and b == TB - 1)
                last.then_inc(sum_done, 1)

            def spread(stage, bank):
                pe.wait_ge(rstd_done, stage + 1)
                for b in range(TB):
                    last = nc.tensor.transpose(ps[:, bank, b * P:(b + 1) * P], r4[:, b:b + 1].to_broadcast([P, P]), ident[:])
                last.then_inc(rb_done, 1)

            def ffn(f, pre, stage, base_in, base_out, o):
                def pair(i):
                    first = isinstance(i, int) and i == 0
                    if not first:
                        pe.wait_ge(gt_done, i + f * NFO)
                        in_slot(base_in, i, 0, (ah, al))
                    else:
                        if f:
                            pe.wait_ge(t_done, 8 * T_OF[3] + 2)
                        in_slot(base_in, 0, 6, (ah, al), ready=pre, halves=base_in == 0)
                    if f or not first:
                        pe.wait_ge(ut_done, i + f * NFO)
                    in_slot(base_in + 1, i, 2, (ah, al), steps=norm if first else None)

                def norm(k):
                    if k == 4:
                        sums(stage, 4)
                    elif k == 6:
                        spread(stage, 4)

                pair(0)
                with pe.Fori(1, NFO) as i:
                    pair(i)

                def unit(j, i=0, **more):
                    out_slot(base_out + j, i, (rh[:, j % 2, :, :], rl[:, j % 2, :, :]), i * 2 + ((R_F1, R_F2)[f] + j + 1), **more)

                def free(c):
                    if c == 0:
                        pe.wait_ge(gt_done, (f + 1) * NFO)
                    if c == 2:
                        pe.wait_ge(ut_done, (f + 1) * NFO)

                unit(0, first=True, blocks=[4, 5, 6, 7, 0, 1, 2, 3], before=free)
                with pe.Fori(0, 4) as i:
                    unit(1, i)
                    unit(2, i)
                unit(9)
                last_slot(base_out + 10, (rh[:, 0, :, :], rl[:, 0, :, :]), (R_F1, R_F2)[f] + 11, o, stage + 1,
                          lambda: pe.wait_ge(h7_done, o + 1))
                spread(stage + 1, 7)

            pe.wait_ge(const_done, 1)
            for b in range(TB):
                pe.wait_ge(x_in[b], 16)
                for k in ORDER:
                    last = nc.tensor.transpose(ps[:, k, b * P:(b + 1) * P], xtok[:, b, k * P:(k + 1) * P], ident[:])
                    if b == TB - 1:
                        last.then_inc(xt_mm, 1)
            pe.wait_ge(par_in, 16 * len(vectors))
            pe.wait_ge(x_ready, 1)
            nc.tensor.transpose(ps[:, 7, 0:n_par], par_rows[0:n_par, :], ident[0:n_par, 0:n_par]).then_inc(xt_mm, 1)
            ffn(0, 0, 0, S_F1I, S_F1O, 0)


            def use_work(*step):
                if WORK[step] > 2:
                    pe.wait_ge(wk_free, WORK[step] - 2)
                return ps[:, 4 + WORK[step] % 2, :]

            def mixer_step(kind, *step):
                if kind == "gates":
                    pe.wait_ge(gw_lo, 1)
                    pe.wait_ge(t_done, 8 * T_OF[1] + 2)
                    for j, k in enumerate(ORDER):
                        pe.wait_ge(a_ready, 8 * 1 + j + 1)
                        last = three(ps[:, 6, :], (gh[:, k, :], gl[:, k, :]), (ah[:, k, :], al[:, k, :]), j == 0, j == KD - 1)
                    last.then_inc(gate_mm, 1)
                elif kind == "ada":
                    pe.wait_ge(ada_step, 3 * KD)
                    for j in range(3 * step[0], 3 * step[0] + 3):
                        last = nc.tensor.matmul(ps[:, 7, j:j + 1], ada[:, j * P:(j + 1) * P], ones[:, 0:1], start=True, stop=True)
                    if step[0] == 7:
                        last.then_inc(ada_mm, 1)
                elif kind == "sums":
                    sums(2, 4)
                elif kind == "spread":
                    spread(2, 4)
                elif kind == "cols":
                    pe.wait_ge(erow_done, 1)
                    bank = use_work(kind)
                    for w, source in enumerate((crow, erow)):
                        for b in range(TB):
                            at = (w * TB + b) * 64
                            last = nc.tensor.transpose(bank[:, at:at + 64], source[:, b * P:(b + 1) * P], ident[0:64, 0:64])
                    last.then_inc(wk_mm, 1)
                elif kind == "bc":
                    p, u = step
                    pe.wait_ge(rows_done, 1)
                    row = 32 * (u % 2) + 2 * p + u // 2
                    nc.tensor.matmul(use_work(kind, *step), ident[0:64, row:row + 1].to_broadcast([64, P]), mrow[:],
                                     start=True, stop=True).then_inc(wk_mm, 1)
                elif kind == "S":
                    p, h, b = step
                    pe.wait_ge(qk_lo, p + 1)
                    bank, at = use_work(kind, *step), slice(b * P, (b + 1) * P)
                    nc.tensor.matmul(bank, k2m[:, h, at], q2m[:, h, :], start=True, stop=False)
                    nc.tensor.matmul(bank, k2m[HALF[h], h, at], ql[HALF[h], :], start=False, stop=True).then_inc(wk_mm, 1)
                elif kind == "vt":
                    p, h = step
                    pe.wait_ge(*evacuated[p, "v"])
                    bank = use_work(kind, *step)
                    for b in range(TB):
                        last = nc.tensor.transpose(bank[:, b * P:(b + 1) * P], vT[:, h, b * P:(b + 1) * P], ident[:])
                    last.then_inc(wk_mm, 1)
                elif kind == "mm":
                    p, h, d = step
                    u = 4 * p + 2 * h + d
                    pe.wait_ge(p_ready, u + 1)
                    pe.wait_ge(wk_free, WORK["vt", p, h])
                    pe.wait_ge(mod_done, 1)
                    pe.wait_ge(h_done, u)
                    pe.wait_ge(edges, 1)
                    for w in range(2):
                        seen = [(t, b) for t in (2 * w, 2 * w + 1) for b in (range(t + 1) if d == 0 else range(t, TB))]
                        for j, (t, b) in enumerate(seen):
                            at = (t - 2 * w) * (DV + 1)
                            last = nc.tensor.matmul(ps[:, 6 + w, at:at + DV + 1], E[:, u % 2, b, t * P:(t + 1) * P], vS[:, h, b, :],
                                                    start=j == 0, stop=j == len(seen) - 1)
                    last.then_inc(u_mm, 1)
                elif kind == "hy":
                    p, h = step
                    pe.wait_ge(hn_done, 2 * p + h + 1)
                    bank = use_work(kind, *step)
                    for b in range(TB):
                        last = nc.tensor.transpose(bank[:, b * P:(b + 1) * P], hs[:, h, b * P:(b + 1) * P], ident[:])
                    last.then_inc(wk_mm, 1)

            for n, (p, what, during) in enumerate(MIXER):
                if n >= 2:
                    pe.wait_ge(*evacuated[MIXER[n - 2][:2]])

                def steps(k):
                    for step in during.get(k, ()):
                        mixer_step(*step)
                in_slot(S_MIX + n, 0, 2 * (n % 2), (ah, al), steps=steps)

            def free(c):
                if c == 4:
                    pe.wait_ge(wk_free, len(WORK))
                    pe.wait_ge(h_done, 8)
                if c == 0:
                    pe.wait_ge(*evacuated[1, "hc"])
                if c == 2:
                    pe.wait_ge(*evacuated[1, "bg"])

            for j in range(3):
                moving = (yh[:, j, :, :], yl[:, j, :, :]) if j < 2 else (ah[:, 0:2, :], al[:, 0:2, :])
                out_slot(S_MO + j, 0, moving, R_MO + j + 1, first=j == 0, blocks=[4, 5, 6, 7, 0, 1, 2, 3], before=free if j == 0 else None)
            last_slot(S_F2I - 1, (ah[:, 2:4, :], al[:, 2:4, :]), R_MO + 4, 1, 3, lambda: pe.wait_ge(h7_done, 2))
            spread(3, 7)

            ffn(1, 2, 4, S_F2I, S_F2O, 2)

            pe.wait_ge(t_done, 8 * T_OF[5] + 3)
            for j in range(5):
                if j < 4:
                    pe.wait_ge(sq_done, 8 * 6 + j + 1)
                else:
                    pe.wait_ge(acc_step, ACC[6] + 3)
                source = sq6(j) if j < 4 else acc[:]
                for b in range(TB):
                    last = nc.tensor.matmul(ps[:, 4, b:b + 1], source[:, b * P:(b + 1) * P], ones[:, 0:1],
                                            start=j == 0 and b == 0, stop=j == 4 and b == TB - 1)
            last.then_inc(sum_done, 1)
            spread(6, 4)

            def att_step(step, r):
                kind, h = step[0], step[1] if len(step) > 1 else 0
                if kind == "Q":
                    i = step[2]
                    idx, n = 4 * h + i, (i + 1) * P
                    if idx == 0:
                        pe.wait_ge(qe_done, r * 3 + 3)
                        pe.wait_ge(ke_done, r + 1)
                    pe.wait_ge(sig_done, r * 8 + max(idx - 1, 0))
                    bank, d = ps[:, 4 + idx % 2, :], slice(DK * h, DK * h + DK)
                    nc.tensor.matmul(bank[:, 0:n], q2[:, h, i * P:n], k2[:, h, 0:n], start=True, stop=False)
                    nc.tensor.matmul(bank[:, 0:n], q2[d, h, i * P:n], kl[d, 0:n], start=False, stop=False)
                    nc.tensor.matmul(bank[:, i * P:n], identb[:], maskS[:], start=False, stop=True).then_inc(q_mm, 1)
                elif kind == "V":
                    pe.wait_ge(ve_done, r + 1)
                    pe.wait_ge(tlo_done, r * 8)
                    for b in range(TB):
                        last = nc.tensor.transpose(ps[:, 6, b * P:(b + 1) * P], v2[:, b * P:(b + 1) * P], ident[:])
                    last.then_inc(v_mm, 1)
                elif kind == "T":
                    i = step[2]
                    idx = 4 * h + i
                    pe.wait_ge(w_done, r * 8 + (idx + 1))
                    if idx == 0:
                        pe.wait_ge(vlo_done, r + 1)
                    else:
                        pe.wait_ge(tlo_done, r * 8 + idx)
                    for b in range(i + 1):
                        last = nc.tensor.transpose(ps[:, 6, b * P:(b + 1) * P], wt_of(i)[:, b * P:(b + 1) * P], ident[:])
                    last.then_inc(t_mm, 1)
                elif kind == "PV":
                    pe.wait_ge(tlo_done, r * 8 + (4 * h + 4))
                    pe.wait_ge(vp_done, r + 1)
                    pe.wait_ge(pv_sum, r * 2 + h)
                    for b in range(TB):
                        nc.tensor.matmul(ps[:, 7, b * P:T], vp[:, h, b, :], wTh[:, b, b * P:T], start=b == 0, stop=False)
                        last = nc.tensor.matmul(ps[:, 7, b * P:T], vph[:, h, b, :], wTl[:, b, b * P:T], start=False, stop=b == TB - 1)
                    last.then_inc(pv_mm, 1)

            def steps_of(j, r):
                def steps(k):
                    for step in ATT_STEPS.get(8 * j + k, []):
                        att_step(step, r)
                return steps

            in_slot(S_ATT, 0, 0, (ah, al), ready=3)
            in_slot(S_ATT + 1, 0, 2, (ah, al))

            def att_round(r):
                pe.wait_ge(qe_done, r * 3 + 3)
                pe.wait_ge(ke_done, r + 1)
                in_slot(S_ATT + 2, r, 0, (ah, al), steps=steps_of(0, r))
                pe.wait_ge(ve_done, r + 1)
                pe.wait_ge(zs_done, r + 1)
                in_slot(S_ATT + 3, r, 2, (ah, al), steps=steps_of(1, r))

            att_round(0)
            with pe.Fori(1, PAIRS - 1) as r:
                att_round(r)
            pool_read = {"u": u_in, "z": zb_done}
            for j in range(8):
                if j < 2:
                    pe.wait_ge(*((qe_done, 3 * PAIRS) if j == 0 else (ve_done, PAIRS)))
                    pe.wait_ge((ke_done, zs_done)[j], PAIRS)
                else:
                    kind, g = POOL_ORDER[j - 2]
                    pe.wait_ge(pool_read[kind], g + 1)
                in_slot(S_POOL + j, 0, 2 * (j % 2), (ah, al), steps=steps_of(j, PAIRS - 1) if j < 2 else None)
            n = S_POOL + 8
            pe.wait_ge(lo_done, n + 1)
            for g in range(4):
                pe.wait_ge(dlo_done, g + 1)
                if g < 2:
                    pe.wait_ge(pool_read[POOL_ORDER[6 + g][0]], POOL_ORDER[6 + g][1] + 1)
                else:
                    pe.wait_ge(yb_t, g - 1)
                for c in range(2):
                    for k in range(2):
                        at = slice((2 * g + k) * CB + c * P, (2 * g + k) * CB + (c + 1) * P)
                        last = three(ps[:, 2 * (g % 2) + c, :], (wh[n % 2][:, at], wl[n % 2][:, at]),
                                     (dh[:, 2 * g + k, :], dl[:, 2 * g + k, :]), k == 0, k == 1)
                last.then_inc(pw_mm if g < 3 else slot_used, 1)

            def branches(c):
                first = isinstance(c, int) and c == 0
                for j, moving in enumerate(((ah, al), (gah, gal), (ah, al), (dh, dl))):
                    if j % 2 == 0:
                        if not first or j:
                            pe.wait_ge(yb_t, 3)
                            pe.wait_ge(sm_done, c * 2 + j // 2)
                    else:
                        pe.wait_ge(yb_t, 4)
                        pe.wait_ge(m_done, c * 2 + j // 2)
                        pe.wait_ge(gal_done, PAIRS)
                    if j == 3:
                        pe.wait_ge(ybl_done, 4)
                    in_slot(S_FIN + j, c, 4 if first and j == 0 else 2 * (j % 2), moving, each=4)

            branches(0)
            with pe.Fori(1, 4) as c:
                branches(c)

            def free(c):
                if c == 0:
                    pe.wait_ge(sm_done, 8)
                if c == 2:
                    pe.wait_ge(m_done, 8)

            for j in range(3):
                out_slot(S_OUT + j, 0, (ah[:, 2 * j:2 * j + 2, :], al[:, 2 * j:2 * j + 2, :]), R_OUT + j + 1, first=j == 0,
                         blocks=[4, 5, 6, 7, 0, 1, 2, 3], before=free if j == 0 else None)

            def turn(j):
                k = ORDER[j]
                pe.wait_ge(t_done, 8 * T_OF[7] + j + 1)
                for b in range(TB):
                    source = h7[:, b * P:(b + 1) * P] if k == 7 else tt[:, j % 2, b * P:(b + 1) * P]
                    last = nc.tensor.transpose(ps[:, k, b * P:(b + 1) * P], source, ident[:])
                last.then_inc(ot_mm, 1)

            last_slot(S_END - 1, (ah[:, 6:8, :], al[:, 6:8, :]), R_OUT + 4, 3, 7, lambda: None, lambda j: turn(j) if j else None)
            pe.wait_ge(var_done, 8)
            turn(0)


def kernel(**inputs):
    import numpy as np
    import concourse.bacc as bacc
    from concourse import mybir as m
    from concourse.bass_utils import run_bass_kernel_spmd as run

    nc = bacc.Bacc("TRN2", target_bir_lowering=False, num_devices=1)
    arrays, aps = {}, {}
    for name, value in inputs.items():
        value = np.ascontiguousarray(value)
        arrays["in_" + name] = value
        aps[name] = nc.dram_tensor("in_" + name, value.shape, m.dt.from_np(value.dtype), kind="ExternalInput").ap()
    out = nc.dram_tensor("out_0", (1, T, D), m.dt.float32, kind="ExternalOutput").ap()
    program(nc, aps, out)
    return run(nc, [arrays], core_ids=[0]).results[0]["out_0"]
```
